# Optimizing a Trainium2 kernel written in Bass

```python
import math
import jax, jax.numpy as jnp
from jax import lax
import numpy as np

D_MODEL = 2048
BATCH = 1
SEQ = 1024
DEPTH = 1

MIX_WIDTH = D_MODEL
LRU_WIDTH = MIX_WIDTH // 2
LRU_BLOCKS = 8
LRU_BLOCK_DIM = LRU_WIDTH // LRU_BLOCKS
CONV_WIDTH = 4
LRU_C = 8.0
ATT_WIDTH = MIX_WIDTH - LRU_WIDTH
ATT_HEADS = 8
HEAD_DIM = ATT_WIDTH // ATT_HEADS
KV_LATENT = 256
IDX_HEADS = 16
IDX_DIM = 64
INDEX_TOPK = 256
Q_BLOCK = 128
REL_BUCKETS = 32
REL_MAX_DIST = 128
EPS = 1e-6

IN_SIZES = (
    LRU_WIDTH,
    LRU_WIDTH,
    ATT_HEADS * HEAD_DIM,
    KV_LATENT,
    ATT_WIDTH,
    IDX_HEADS * IDX_DIM,
    IDX_DIM,
    IDX_HEADS,
)
IN_COLS = sum(IN_SIZES)
IN_SPLITS = tuple(int(v) for v in np.cumsum(IN_SIZES)[:-1])

kernel_name = "hymba_rglru_dsa_hybrid"

def _rmsnorm(x, g):
    x32 = x.astype(jnp.float32)
    y = x32 * lax.rsqrt(jnp.mean(x32 * x32, axis=-1, keepdims=True) + EPS)
    return (y * g.astype(jnp.float32)).astype(x.dtype)

def _layernorm(x, g, b):
    x32 = x.astype(jnp.float32)
    mu = jnp.mean(x32, axis=-1, keepdims=True)
    var = jnp.mean(jnp.square(x32 - mu), axis=-1, keepdims=True)
    y = (x32 - mu) * lax.rsqrt(var + EPS)
    return (y * g.astype(jnp.float32) + b.astype(jnp.float32)).astype(x.dtype)

def _t5_bucket(dist):
    n = jnp.maximum(dist, 0)
    max_exact = REL_BUCKETS // 2
    nf = jnp.maximum(n, 1).astype(jnp.float32)
    large = max_exact + (jnp.log(nf / max_exact) / math.log(REL_MAX_DIST / max_exact)
                         * (REL_BUCKETS - max_exact)).astype(jnp.int32)
    large = jnp.minimum(large, REL_BUCKETS - 1)
    return jnp.where(n < max_exact, n, large)

def _lru_combine(left, right):
    a1, b1 = left
    a2, b2 = right
    return a1 * a2, a2 * b1 + b2

def _rglru_branch(xa, conv_w, conv_b, wa, ba, wx, bx, lam):
    B, S, W = xa.shape
    xp = jnp.pad(xa, ((0, 0), (CONV_WIDTH - 1, 0), (0, 0)))
    xc = conv_b + sum(xp[:, j:j + S] * conv_w[j] for j in range(CONV_WIDTH))
    xb = xc.reshape(B, S, LRU_BLOCKS, LRU_BLOCK_DIM)
    r = jax.nn.sigmoid(jnp.einsum('bsgi,gij->bsgj', xb, wa).reshape(B, S, W) + ba)
    i = jax.nn.sigmoid(jnp.einsum('bsgi,gij->bsgj', xb, wx).reshape(B, S, W) + bx)
    log_a = -LRU_C * r.astype(jnp.float32) * jax.nn.softplus(-lam.astype(jnp.float32))
    a = jnp.exp(log_a)
    mult = jnp.sqrt(-jnp.expm1(2.0 * log_a))
    mult = jnp.where((jnp.arange(S) == 0)[None, :, None], 1.0, mult)
    bvals = mult * (i * xc).astype(jnp.float32)
    _, h = lax.associative_scan(_lru_combine, (a, bvals), axis=1)
    return h.astype(xa.dtype)

def _dsa_branch(q, ckv, qi, ki, wi, ckv_norm_g, ik_g, ik_b, w_uk, w_uv, rel_bias):
    B, S, _ = q.shape
    topk = min(INDEX_TOPK, S // 4)
    nblk = S // Q_BLOCK
    neg = jnp.finfo(jnp.float32).min
    q = q.reshape(B, S, ATT_HEADS, HEAD_DIM)
    q_abs = jnp.einsum('bshd,hdc->bshc', q, w_uk)
    c = _rmsnorm(ckv, ckv_norm_g)
    qi = qi.reshape(B, S, IDX_HEADS, IDX_DIM)
    ki = _layernorm(ki, ik_g, ik_b)
    wi = wi * (IDX_HEADS ** -0.5 * IDX_DIM ** -0.5)
    pos = jnp.arange(S, dtype=jnp.int32)

    def to_blocks(t):
        return jnp.moveaxis(t.reshape((B, nblk, Q_BLOCK) + t.shape[2:]), 1, 0)

    def block_fn(args):
        qa_b, qi_b, wi_b, pos_b = args
        s_idx = jnp.einsum('bqhd,bsd->bqhs', qi_b, ki).astype(jnp.float32)
        score = jnp.einsum('bqhs,bqh->bqs', jax.nn.relu(s_idx), wi_b.astype(jnp.float32))
        causal = pos[None, None, :] <= pos_b[None, :, None]
        score = jnp.where(causal, score, neg)
        _, sel = lax.top_k(score, topk)
        c_sel = jax.vmap(lambda cb, ib: cb[ib])(c, sel)
        logits = jnp.einsum('bqhc,bqkc->bqhk', qa_b, c_sel).astype(jnp.float32) * (HEAD_DIM ** -0.5)
        dist = pos_b[None, :, None] - sel
        bias = rel_bias[_t5_bucket(dist)].astype(jnp.float32)
        logits = logits + jnp.moveaxis(bias, -1, 2)
        logits = jnp.where((dist >= 0)[:, :, None, :], logits, neg)
        p = jax.nn.softmax(logits, axis=-1).astype(c.dtype)
        return jnp.einsum('bqhk,bqkc->bqhc', p, c_sel)

    o = lax.map(block_fn, (to_blocks(q_abs), to_blocks(qi), to_blocks(wi), pos.reshape(nblk, Q_BLOCK)))
    o = jnp.moveaxis(o, 0, 1).reshape(B, S, ATT_HEADS, KV_LATENT)
    out = jnp.einsum('bshc,hcd->bshd', o, w_uv)
    return out.reshape(B, S, ATT_WIDTH)

def setup_inputs(seed: int = 0) -> dict:
    key = jax.random.key(seed)
    ks = jax.random.split(key, 20)
    f32 = jnp.float32
    nrm = lambda k, shape, scale: jax.random.normal(k, shape, f32) * scale
    a0 = jax.random.uniform(ks[9], (DEPTH, LRU_WIDTH), f32, 0.9, 0.999)
    s0 = a0 ** (1.0 / LRU_C)
    lam = jnp.log(s0) - jnp.log1p(-s0)
    return {
        "x": nrm(ks[0], (BATCH, SEQ, D_MODEL), 1.0),
        "norm_g": 1.0 + nrm(ks[1], (DEPTH, D_MODEL), 0.02),
        "w_in": nrm(ks[2], (DEPTH, D_MODEL, IN_COLS), D_MODEL ** -0.5),
        "conv_w": nrm(ks[3], (DEPTH, CONV_WIDTH, LRU_WIDTH), CONV_WIDTH ** -0.5),
        "conv_b": nrm(ks[4], (DEPTH, LRU_WIDTH), 0.01),
        "lru_wa": nrm(ks[5], (DEPTH, LRU_BLOCKS, LRU_BLOCK_DIM, LRU_BLOCK_DIM), LRU_BLOCK_DIM ** -0.5),
        "lru_ba": nrm(ks[6], (DEPTH, LRU_WIDTH), 0.01),
        "lru_wx": nrm(ks[7], (DEPTH, LRU_BLOCKS, LRU_BLOCK_DIM, LRU_BLOCK_DIM), LRU_BLOCK_DIM ** -0.5),
        "lru_bx": nrm(ks[8], (DEPTH, LRU_WIDTH), 0.01),
        "lru_lambda": lam,
        "ckv_norm_g": 1.0 + nrm(ks[10], (DEPTH, KV_LATENT), 0.02),
        "idx_k_norm_g": 1.0 + nrm(ks[11], (DEPTH, IDX_DIM), 0.02),
        "idx_k_norm_b": nrm(ks[12], (DEPTH, IDX_DIM), 0.01),
        "w_uk": nrm(ks[13], (DEPTH, ATT_HEADS, HEAD_DIM, KV_LATENT), HEAD_DIM ** -0.5),
        "w_uv": nrm(ks[14], (DEPTH, ATT_HEADS, KV_LATENT, HEAD_DIM), KV_LATENT ** -0.5),
        "w_out": nrm(ks[15], (DEPTH, MIX_WIDTH, D_MODEL), MIX_WIDTH ** -0.5),
        "rel_bias": nrm(ks[16], (REL_BUCKETS, ATT_HEADS), 0.5),
        "final_norm_g": 1.0 + nrm(ks[17], (D_MODEL,), 0.02),
    }

def reference(x, norm_g, w_in, conv_w, conv_b, lru_wa, lru_ba, lru_wx, lru_bx, lru_lambda,
              ckv_norm_g, idx_k_norm_g, idx_k_norm_b, w_uk, w_uv, w_out, rel_bias, final_norm_g):
    for l in range(DEPTH):
        h = _rmsnorm(x, norm_g[l])
        proj = jnp.einsum('bsd,de->bse', h, w_in[l])
        xa, ga, q, ckv, gb, qi, ki, wi = jnp.split(proj, IN_SPLITS, axis=-1)
        ya = _rglru_branch(xa, conv_w[l], conv_b[l], lru_wa[l], lru_ba[l],
                           lru_wx[l], lru_bx[l], lru_lambda[l]) * jax.nn.silu(ga)
        yb = _dsa_branch(q, ckv, qi, ki, wi, ckv_norm_g[l], idx_k_norm_g[l], idx_k_norm_b[l],
                         w_uk[l], w_uv[l], rel_bias) * jax.nn.silu(gb)
        y = jnp.concatenate([ya, yb], axis=-1)
        x = x + jnp.einsum('bse,ed->bsd', y, w_out[l])
    return _rmsnorm(x, final_norm_g)


_drawn_inputs = setup_inputs


def setup_inputs(seed=0):
    import zlib

    import numpy as np

    out = dict(_drawn_inputs(seed))
    spreads = {}
    factors = {'norm_g': 4.841,
     'conv_b': 10.77,
     'lru_ba': 64.0,
     'lru_bx': 64.0,
     'ckv_norm_g': 8.0,
     'idx_k_norm_g': 8.0,
     'idx_k_norm_b': 8.0,
     'final_norm_g': 8.002}
    for name, (base, spread) in spreads.items():
        noise = np.random.default_rng([zlib.crc32(name.encode()), seed]).standard_normal(out[name].shape)
        drawn = base * np.exp(spread * noise) if base else spread * noise
        out[name] = __import__('jax').numpy.asarray(drawn.astype(out[name].dtype))
    for name, factor in factors.items():
        out[name] = (out[name] * factor).astype(out[name].dtype)
    return out
```

```python
import math
from contextlib import ExitStack

import concourse.bass as bass
from concourse import mybir

F32 = mybir.dt.float32
F32R = mybir.dt.float32r
BF16 = mybir.dt.bfloat16
ALU = mybir.AluOpType
ACT = mybir.ActivationFunctionType
AX = mybir.AxisListType
ds = bass.ds

P = 128
D = 2048
S = 1024
KT = D // P
QB = S // P
LRU = 1024
G = LRU // P
CONV = 4
NH = 8
HD = 128
C = 256
CT = C // P
IH = 16
ID = 64
TOPK = 256
BUCKETS = 32
MAX_DIST = 128
EPS = 1e-6
NT = 512

COL_XA, COL_GA, COL_Q, COL_CKV, COL_GB, COL_QI, COL_KI = 0, 1024, 2048, 3072, 3328, 4352, 5376
KW = ID + IH
PIECES = 4
PK = KT // PIECES

T_KW, T_C, T_QI, T_LRU, T_ATT = 0, 1, 3, 11, 27
TILES = 43

PARS = (CONV + 4) * G + CT + 2

AHEAD = 3

FIRST_SCORED = TOPK // P
UNITS = 2 * (QB - FIRST_SCORED)
FULL = sum((q + 1) * P for q in range(QB))
OFF = [P * q * (q + 1) // 2 for q in range(QB)]
SCORED = FULL - OFF[FIRST_SCORED]
NEG = -3.0e38
TAKEN = -3.38e38
BIG = 1.0e30
ROUNDS = TOPK // 8
BR = 3 * P

OC = 512
OCH = D // OC
OPK = 2
OP = KT // OPK
HALF_T = 4


def off(q):
    return OFF[q] - OFF[FIRST_SCORED]


class Tally:

    def __init__(self, sem):
        self.sem, self.base, self.n = sem, 0, 0

    def did(self, ins):
        ins.then_inc(self.sem, 1)
        self.n += 1
        return self.base + self.n

    def now(self):
        return self.base + self.n

    def enter(self, i, per):
        self.start, self.per = self.base + self.n, per
        self.base, self.n = self.start + i * per, 0

    def leave(self, count):
        assert self.n == self.per, (self.n, self.per)
        self.base, self.n = self.start + count * self.per, 0


def layer(nc, a, out):
    x, w_in, w_out = a["x"][0], a["w_in"][0], a["w_out"][0]

    yl_d = nc.dram_tensor("y_lru_dram", [G, P, S], F32).ap()
    q_d = nc.dram_tensor("q_dram", [NH, P, S], F32).ap()
    gate_d = nc.dram_tensor("gate_dram", [NH, P, S], F32).ap()
    c_d = nc.dram_tensor("c_dram", [CT, P, S], F32).ap()
    wk_d = nc.dram_tensor("wuk_dram", [NH, P, CT, HD], F32).ap()
    bias_h = nc.dram_tensor("bias_rows", [NH, P * BR], F32)
    bias_d = bias_h.ap()

    ctx = ExitStack()
    with ctx:
        def sem(name):
            return ctx.enter_context(nc.semaphore(name))

        def alloc(stack):
            return lambda name, shape, dt=F32: stack.enter_context(nc.sbuf_tensor(name, shape, dt))

        sb = alloc(ctx)
        hT_hi = sb("hT_hi", [P, KT, S], F32R)
        hT_lo = sb("hT_lo", [P, KT, S], F32R)
        ident = sb("ident", [P, P])
        causal = sb("causal", [P, P])
        par_t = sb("par_t", [P, PARS])
        conv_w = par_t[:, 0:CONV * G].rearrange("p (j g) -> p j g", g=G)
        lru_p = par_t[:, CONV * G:(CONV + 4) * G].rearrange("p (k g) -> p k g", g=G)
        c_g = par_t[:, PARS - 4:PARS - 2]
        k_gb = par_t[0:ID, PARS - 2:PARS]
        decay = sb("decay", [P, 2, G])
        sp_t = sb("sp_t", [P, 5, G])
        eps = sb("eps", [P, 1])
        pause = sb("pause", [P, 1])
        stat = sb("stat", [P, 8])
        w_nat = sb("w_nat", [P, QB, IH])
        top8 = sb("top8", [P, QB, 8])
        sums = sb("sums", [P, QB, 3])

        ph = ExitStack()
        sbp = alloc(ph)
        w_raw = sbp("w_raw", [P, PIECES, PK, P])
        w_hi = sbp("w_hi", [P, PIECES, PK, P], F32R)
        w_lo = sbp("w_lo", [P, PIECES, PK, P], F32R)
        p0 = ExitStack()
        s0 = alloc(p0)
        xin = s0("xin", [P, 2, D])
        g_bc = s0("g_bc", [P, D])
        junk = s0("junk", [P, 2, D], BF16)
        par_rows = s0("par_rows", [PARS, P])
        wuk = s0("wuk", [P, NH, C])
        wuk_t = s0("wuk_tr", [P, NH * CT, HD])
        onehot = s0("onehot", [BUCKETS, BR])
        rel = s0("rel", [BUCKETS, NH])
        bias_sb = s0("bias_sb", [NH, BR])
        p0.close()
        scores = sbp("scores", [P, SCORED])
        pb = ExitStack()
        sB = alloc(pb)
        ki_hi = sB("ki_hi", [P, S], F32R)
        ki_lo = sB("ki_lo", [P, S], F32R)
        pa = ExitStack()
        sA = alloc(pa)
        kw_sb = sA("kw_sb", [KW, S])
        k_t = sA("k_t", [ID, S])
        c_sb = sA("c_sb", [P, CT, S])
        c_sq = sA("c_sq", [P, CT, S])
        c_rs = sA("c_rs", [P, S])
        ones_k = sA("ones_k", [ID, ID])
        ones_c = sA("ones_c", [P, P])
        pa.close()
        stack_a = [sB(f"stack_a{i}", [P, S], F32R) for i in range(2)]
        stack_b = [sB(f"stack_b{i}", [P, S], F32R) for i in range(2)]
        relu = [sB(f"relu{i}", [P, S]) for i in range(2)]
        pb.close()
        pc = ExitStack()
        sC = alloc(pc)
        xc = sC("xc", [P, S])
        rg = sC("rg", [P, S])
        th = sC("th", [P, S])
        av = sC("av", [P, S])
        ig = sC("ig", [P, S])
        sg = sC("sg", [P, S])
        w_gates = sC("w_gates", [P, 2, P])
        mask_at = 4 * (3 * PIECES * PK * P + SCORED + 6 * S + 2 * P)
        mask = sC("mask", [P, FULL], BF16)
        pc.close()
        ph.close()

        ph = ExitStack()
        s3 = alloc(ph)
        c_t = s3("c_t", [P, CT, S])
        kT = [s3(f"kT{i}", [P, S]) for i in range(2)]
        vN = [s3(f"vN{i}", [P, QB, HD]) for i in range(2)]
        qT = [s3(f"qT{i}", [P, S]) for i in range(2)]
        prob_sb = s3("prob_sb", [P, (8 + 7 + 6) * P])
        pT0 = s3("pT0", [P, 6, 2 * P])
        pT1 = s3("pT1", [P, 8, 2 * P])
        gate = s3("gate", [P, 2, 2 * P])
        wk = [s3(f"wk{i}", [P, CT, HD]) for i in range(2)]
        wv = [s3(f"wv{i}", [P, CT, HD]) for i in range(2)]
        tb = [s3(f"tb{i}", [P, 2 * P]) for i in range(2)]
        yf = s3("yf", [P, 2 * P])
        before = 4 * (CT * S + 6 * S + 21 * P + 14 * 2 * P + 4 * P + 4 * CT * HD + 4 * P + 2 * P)
        assert before == mask_at
        s3("mask_kept", [P, FULL], BF16)
        yl_raw = s3("yl_raw", [P, NT])
        pT = [pT0, pT1]
        ph.close()

        ph = ExitStack()
        s4 = alloc(ph)
        wo_raw = s4("wo_raw", [P, 4, OPK, OC])
        gf_bc = s4("gf_bc", [P, D])
        wo_hi = s4("wo_hi", [P, 2, OPK, OC], F32R)
        wo_lo = s4("wo_lo", [P, 2, OPK, OC], F32R)
        res = s4("res", [P, HALF_T, D])
        junk4 = s4("junk4", [P, OC], BF16)
        ssq = s4("ssq", [P, HALF_T, OCH])
        fstat = s4("fstat", [P, 3, HALF_T])
        ph.close()

        PS = [ctx.enter_context(nc.psum_tensor(f"ps{i}", [P, S], F32)) for i in range(4)]
        PJ, X = PS[0:2], PS[2:4]

        PROB_AT = [15 * P, 16 * P, 18 * P, 8 * P, 0, 15 * P, 8 * P, 0]
        prob = [prob_sb[:, PROB_AT[q]:PROB_AT[q] + (q + 1) * P] for q in range(QB)]
        LG = [PS[0][:, 0:NT], PS[0][:, NT:S], PS[1][:, 0:NT], PS[1][:, NT:S], PS[2], PS[0], PS[1], PS[2]]
        LAST = [3, 4, 4, 5, 5, 4, 3, 3]

        id_made = sem("id_made")
        consts = sem("consts")
        eps_made = sem("eps_made")
        ones_made = sem("ones_made")
        rows_clear = sem("rows_clear")
        small_in = sem("small_in")
        small_tp = sem("small_tp")
        small_cp = sem("small_cp")
        bias_in = sem("bias_in")
        bias_mm = sem("bias_mm")
        bias_cp = sem("bias_cp")
        bias_st = sem("bias_st")
        wuk_in = sem("wuk_in")
        wuk_tp = sem("wuk_tp")
        wuk_cp = sem("wuk_cp")
        wuk_st = sem("wuk_st")
        g_in = sem("g_in")
        x_in = [sem(f"x_in{i}") for i in range(2)]
        x_sd = sem("x_sd")
        x_norm = sem("x_norm")
        x_tp = sem("x_tp")
        h_hi = sem("h_hi")
        h_lo = sem("h_lo")
        w_in_s = [sem(f"w_in{j}") for j in range(PIECES)]
        w_hi_s = sem("w_hi_s")
        w_lo_s = sem("w_lo_s")
        w_used = sem("w_used")
        pj_free = [sem("pj_free0"), sem("pj_free1")]
        kw_cp = sem("kw_cp")
        k_mean = sem("k_mean")
        k_dev = sem("k_dev")
        k_sq = sem("k_sq")
        k_var = sem("k_var")
        k_sd = sem("k_sd")
        k_nrm = sem("k_nrm")
        k_ln = sem("k_ln")
        ki_done = sem("ki_done")
        w_tp = sem("w_tp")
        w_nat_s = sem("w_nat_s")
        c_sq_s = sem("c_sq_s")
        c_var = sem("c_var")
        c_sd = sem("c_sd")
        c_done = sem("c_done")
        c_st = sem("c_st")
        st_hi = sem("st_hi")
        ix_mm = sem("ix_mm")
        ix_relu = sem("ix_relu")
        ix_acc = sem("ix_acc")
        sp_exp = sem("sp_exp")
        sp_in = sem("sp_in")
        dec_s = sem("dec_s")
        gw_in = sem("gw_in")
        xc0 = sem("xc0")
        gates_mm = sem("gates_mm")
        r_sig = sem("r_sig")
        i_sig = sem("i_sig")
        g_sig = sem("g_sig")
        a_sq = sem("a_sq")
        one_m = sem("one_m")
        root = sem("root")
        y_lru = sem("y_lru_s")
        y_st = sem("y_st")
        d_sig = sem("d_sig")
        q_st = sem("q_st")
        gate_st = sem("gate_st")
        mask_s = sem("mask_s")
        c_ld = sem("c_ld")
        kv_ld = [sem("kv_ld0"), sem("kv_ld1")]
        qb_ld = [sem("qb_ld0"), sem("qb_ld1")]
        gate_ld = [sem("gate_ld0"), sem("gate_ld1")]
        yl_ld = sem("yl_ld")
        yl_hi = sem("yl_hi")
        yl_lo = sem("yl_lo")
        kv_mm_s = sem("kv_mm")
        ro_mm = sem("ro_mm")
        kv_cp = sem("kv_cp")
        o_used = sem("o_used")
        lg_mm = sem("lg_mm")
        lg_used = sem("lg_used")
        p_exp = sem("p_exp")
        p_norm = sem("p_norm")
        p_tp = sem("p_tp")
        p_cp = sem("p_cp")
        y_att = sem("y_att")
        wo_in = [sem(f"wo_in{i}") for i in range(4)]
        wo_hi_s = sem("wo_hi_s")
        wo_lo_s = sem("wo_lo_s")
        wo_used = sem("wo_used")
        gf_in = sem("gf_in")
        res_in = sem("res_in")
        o_mm = sem("o_mm")
        o_add = sem("o_add")
        o_sq = sem("o_sq")
        f_tot = sem("f_tot")
        f_sd = sem("f_sd")
        f_out = sem("f_out")
        out_st = sem("out_st")
        act_step = sem("act_step")
        dve_step = sem("dve_step")
        pool_step = sem("pool_step")

        def cols(t0, step=0, i=0):
            return ds(t0 + step * i, P)

        def w_rows(c0, n):
            v = w_in.rearrange("(j k p) e -> j p k e", j=PIECES, p=P)
            return [v[j, :, :, ds(c0, n)] for j in range(PIECES)]

        block = ctx.enter_context(nc.Block())

        @block.sync
        def _(sp):
            def weights(t, c0, n=P):
                for j, src in enumerate(w_rows(c0, n)):
                    sp.wait_ge(w_lo_s, 4 * t + j + 1)
                    sp.dma_start(w_raw[:, j, :, 0:n], src).then_inc(w_in_s[j], 16)

            sp.dma_start(rel[:, :], a["rel_bias"]).then_inc(bias_in, 16)
            sp.dma_start(onehot[:, :], a["onehot"]).then_inc(bias_in, 16)
            sp.dma_start(wuk[:, :, :], a["w_uk"][0].rearrange("h d c -> d h c")).then_inc(wuk_in, 16)
            sp.dma_start(g_bc[:, :], a["norm_g"].broadcast_to([P, D])).then_inc(g_in, 16)
            weights(T_KW, COL_KI, KW)
            sp.wait_ge(rows_clear, 1)
            rows = 0
            for name, n, m in [("conv_w", CONV * G, P), ("conv_b", G, P), ("lru_ba", G, P), ("lru_bx", G, P),
                               ("lru_lambda", G, P), ("ckv_norm_g", CT, P), ("idx_k_norm_g", 1, ID),
                               ("idx_k_norm_b", 1, ID)]:
                v = a[name][0]
                src = v.rearrange("j (g p) -> (j g) p", p=P) if len(v.shape) == 2 else v.rearrange("(g p) -> g p", p=m)
                sp.dma_start(par_rows[rows:rows + n, 0:m], src).then_inc(small_in, 16)
                rows += n
            sp.wait_ge(bias_cp, 1)
            sp.dma_start(bias_d.rearrange("h (p m) -> h p m", p=P),
                         bias_sb[:, :].rearrange("h (o m) -> h o m", o=1).broadcast_to([NH, P, BR])).then_inc(bias_st, 16)
            sp.wait_ge(wuk_cp, 2)
            sp.dma_start(wk_d.rearrange("h c t d -> c h t d"),
                         wuk_t[:, :, :].rearrange("c (h t) d -> c h t d", t=CT)).then_inc(wuk_st, 16)
            weights(T_C, COL_CKV)
            weights(T_C + 1, COL_CKV + P)
            weights(T_QI, COL_QI)
            weights(T_QI + 1, COL_QI + P)
            for t in range(CT):
                sp.wait_ge(c_done, t + 1)
                sp.dma_start(c_d[t], c_sb[:, t, :]).then_inc(c_st, 16)
            with sp.Fori(0, 6) as i:
                weights(T_QI + 2 + i, COL_QI + 2 * P + i * P)
            def lru_loads(g):
                weights(T_LRU + 2 * g, COL_XA + g * P)
                weights(T_LRU + 1 + 2 * g, COL_GA + g * P)

            def gate_loads(g):
                sp.wait_ge(gates_mm, g + 1)
                sp.dma_start(w_gates[:, 0, :], a["lru_wa"][0, ds(g, 1)].rearrange("o i j -> (o i) j")
                             ).then_inc(gw_in, 16)
                sp.dma_start(w_gates[:, 1, :], a["lru_wx"][0, ds(g, 1)].rearrange("o i j -> (o i) j")
                             ).then_inc(gw_in, 16)

            lru_loads(0)
            sp.wait_ge(ix_acc, 8 + 8 * UNITS)
            gate_loads(0)
            with sp.Fori(1, G) as g:
                lru_loads(g)
                sp.wait_ge(y_lru, g + 1)
                sp.dma_start(yl_d[ds(g - 1, 1)].rearrange("o p s -> (o p) s"), sg[:, :]).then_inc(y_st, 16)
                gate_loads(g)
            def att_loads(h):
                weights(T_ATT + 2 * h, COL_Q + h * P)
                weights(T_ATT + 1 + 2 * h, COL_GB + h * P)

            def att_stores(h):
                sp.wait_ge(pj_free[1], h + T_ATT // 2 + 2)
                sp.dma_start(q_d[ds(h, 1)].rearrange("o p s -> (o p) s"), av[:, :]).then_inc(q_st, 16)
                sp.wait_ge(pj_free[0], h + (T_ATT + 1) // 2 + 2)
                sp.dma_start(gate_d[ds(h, 1)].rearrange("o p s -> (o p) s"), rg[:, :]).then_inc(gate_st, 16)

            att_loads(0)
            sp.wait_ge(y_lru, G + 1)
            sp.dma_start(yl_d[G - 1], sg[:, :]).then_inc(y_st, 16)
            with sp.Fori(1, NH) as h:
                att_loads(h)
                att_stores(h - 1)
            att_stores(NH - 1)
            sp.wait_ge(mask_s, 1)
            sp.wait_ge(y_st, 16 * (G + 1))
            sp.wait_ge(q_st, 16 * (NH + 1))
            sp.wait_ge(gate_st, 16 * (NH + 1))
            sp.wait_ge(c_st, 16 * CT)
            sp.wait_ge(wuk_st, 16)
            sp.wait_ge(bias_st, 16)
            sp.dma_start(c_t[:, :, :], c_d.rearrange("t p s -> p t s")).then_inc(c_ld, 16)

            def kv_loads(h, p):
                sp.dma_start(wk[p][:, :, :], wk_d[ds(h, 1)].rearrange("o p t d -> (o p) t d")).then_inc(kv_ld[p], 16)
                sp.dma_start(wv[p][:, :, :], a["w_uv"][0, ds(h, 1)].rearrange("o (t p) d -> (o p) t d", p=P)
                             ).then_inc(kv_ld[p], 16)

            def qb_loads(h, p):
                sp.dma_start(qT[p][:, :], q_d[ds(h, 1)].rearrange("o p s -> (o p) s")).then_inc(qb_ld[p], 16)
                src = bias_d[ds(h, 1), P - 1:P - 1 + P * (BR - 1)].rearrange("o (p m) -> (o p) m", p=P)[:, 0:2 * P]
                sp.dma_start(tb[p][:, :], src).then_inc(qb_ld[p], 16)

            def tail_loads(h):
                for k in range(2):
                    sp.wait_ge(yl_lo, 2 * h + k + 1)
                    sp.dma_start(yl_raw[:, :], yl_d[ds(h, 1), :, k * NT:(k + 1) * NT].rearrange(
                        "o p s -> (o p) s")).then_inc(yl_ld, 16)

            def head_loads(h, p):
                sp.wait_ge(kv_mm_s, 4 * h - 4)
                kv_loads(h, p)
                sp.wait_ge(lg_used, 8 * h - 8)
                qb_loads(h, p)
                tail_loads(h - 1)

            for h in range(2):
                kv_loads(h, h)
                qb_loads(h, h)
            tail_loads(0)
            with sp.Fori(1, NH // 2) as i:
                head_loads(i * 2, 0)
                head_loads(i * 2 + 1, 1)
            v_out = w_out.rearrange("(j k p) e -> j p k e", j=OP, p=P)

            def out_weights(cg, chunk, js=range(OP)):
                for j in js:
                    sp.wait_ge(wo_lo_s, 8 * cg + j + 1)
                    sp.dma_start(wo_raw[:, j % 4, :, :], v_out[j, :, :, ds(chunk * OC, OC)]
                                 ).then_inc(wo_in[j % 4], 16)

            sp.wait_ge(kv_mm_s, 4 * NH)
            out_weights(0, 0, range(2))
            sp.wait_ge(lg_used, 8 * (NH - 1))
            out_weights(0, 0, [2])
            tail_loads(NH - 1)
            sp.wait_ge(lg_used, 8 * NH)
            out_weights(0, 0, [3])
            sp.wait_ge(y_att, 4 * NH + 1)

            def residual(th):
                for q in range(HALF_T):
                    r0 = (th * HALF_T + q) * P
                    sp.dma_start(res[:, q, :], x[r0:r0 + P, :]).then_inc(res_in, 16)

            def stores(th):
                for q in range(HALF_T):
                    r0 = (th * HALF_T + q) * P
                    sp.wait_ge(f_out, HALF_T * th + q + 1)
                    sp.dma_start(out[0, r0:r0 + P, :], res[:, q, :]).then_inc(out_st, 16)

            residual(0)
            sp.dma_start(gf_bc[:, :], a["final_norm_g"].rearrange("(o d) -> o d", o=1).broadcast_to([P, D])
                         ).then_inc(gf_in, 16)
            out_weights(0, 0, range(4, OP))
            with sp.Fori(1, OCH) as c:
                out_weights(c, c)
            out_weights(OCH, 0)
            stores(0)
            sp.wait_ge(out_st, 16 * HALF_T)
            residual(1)
            with sp.Fori(1, OCH) as c:
                out_weights(c + OCH, c)
            stores(1)
            sp.wait_ge(out_st, 16 * 2 * HALF_T)

        @block.gpsimd
        def _(pool):
            nc.gpsimd.sem_inc(w_lo_s, PIECES)
            nc.gpsimd.sem_inc(wo_lo_s, 4)
            step = Tally(pool_step)
            nc.gpsimd.memset(ident[:, :], 0.0).then_inc(pool_step, 1)
            nc.gpsimd.memset(causal[:, :], 0.0).then_inc(pool_step, 1)
            pool.wait_ge(pool_step, 2)
            nc.gpsimd.affine_select(out=ident[:, :], in_=ident[:, :], compare_op=ALU.not_equal, fill=1.0,
                                    base=0, pattern=[[-1, P]], channel_multiplier=1).then_inc(id_made, 1)
            nc.gpsimd.affine_select(out=causal[:, :], in_=causal[:, :], compare_op=ALU.is_ge, fill=NEG,
                                    base=0, pattern=[[-1, P]], channel_multiplier=1).then_inc(consts, 1)
            for u in range(2):
                pool.dma_start(xin[:, u, :], x[u * P:(u + 1) * P, :]).then_inc(x_in[u], 16)
            with pool.Fori(0, QB // 2 - 1) as k:
                for u in range(2):
                    pool.wait_ge(x_tp, 4 * k + 2 * u + 2)
                    pool.dma_start(xin[:, u, :], x[ds(k * 2 * P + (2 + u) * P, P), :]).then_inc(x_in[u], 16)

            def low(t, n=P):
                for j in range(PIECES):
                    pool.wait_ge(w_hi_s, 4 * t + j + 1)
                    nc.gpsimd.tensor_tensor(w_lo[:, j, :, 0:n], w_raw[:, j, :, 0:n],
                                            w_hi[:, j, :, 0:n].bitcast(F32), ALU.subtract).then_inc(w_lo_s, 1)

            low(T_KW, KW)
            with pool.Fori(1, TILES) as t:
                low(t)
            pool.wait_ge(gate_st, 16 * (NH + 1))
            pool.wait_ge(mask_s, 1)
            with pool.Fori(0, NH) as h:
                for r in range(4):
                    pool.wait_ge(o_used, 4 * h + r + 3)
                    pool.dma_start(gate[:, r % 2, :], gate_d[ds(h, 1), :, 2 * r * P:2 * (r + 1) * P].rearrange(
                        "o p s -> (o p) s")).then_inc(gate_ld[r % 2], 16)
            pool.wait_ge(p_tp, 8 * NH + 3)
            with pool.Fori(0, 2 * OCH) as c:
                for j in range(OP):
                    pool.wait_ge(wo_hi_s, 8 * c + j + 1)
                    nc.gpsimd.tensor_tensor(wo_lo[:, j % 2, :, :], wo_raw[:, j % 4, :, :],
                                            wo_hi[:, j % 2, :, :].bitcast(F32), ALU.subtract).then_inc(wo_lo_s, 1)

        @block.scalar
        def _(act):
            nc.scalar.sem_inc(ix_relu, 2)
            nc.scalar.sem_inc(pj_free[0], 1)
            nc.scalar.sem_inc(pj_free[1], 1)
            nc.scalar.sem_inc(p_cp, 4)
            nc.scalar.sem_inc(o_sq, 1)
            nc.scalar.sem_inc(i_sig, 1)
            nc.scalar.sem_inc(y_st, 16)
            nc.scalar.sem_inc(q_st, 16)
            nc.scalar.sem_inc(gate_st, 16)
            step = Tally(act_step)
            done = lambda t: 4 * t + 8

            def square(k, u):
                act.wait_ge(x_in[u], 16 * k + 16)
                step.did(nc.scalar.activation(junk[:, u, :], xin[:, u, :], ACT.Square, accum_out=stat[:, u:u + 1]))

            def root_x(k, u):
                act.wait_ge(act_step, step.now())
                nc.scalar.activation(stat[:, 2 + u:3 + u], stat[:, u:u + 1], ACT.Sqrt, scale=1.0 / D,
                                     bias=eps[:, :]).then_inc(x_sd, 1)

            def high_x(k, u):
                for j in range(2):
                    act.wait_ge(x_tp, 4 * k + 2 * u + j + 1)
                    nc.scalar.activation(
                        hT_hi[:, 8 * j:8 * j + 8, ds(k * 2 * P + u * P, P)],
                        PS[2 * u + j][:, :].rearrange("p (t s) -> p t s", s=P), ACT.Copy).then_inc(h_hi, 1)

            act.wait_ge(eps_made, 1)
            square(0, 0)
            act.wait_ge(bias_mm, 1)
            nc.scalar.activation(bias_sb[:, :], X[0][0:NH, 0:BR], ACT.Copy).then_inc(bias_cp, 1)
            for k in range(2):
                act.wait_ge(wuk_tp, k + 1)
                nc.scalar.activation(wuk_t[:, 8 * k:8 * k + 8, :],
                                     PJ[k][:, :].rearrange("p (t d) -> p t d", d=HD), ACT.Copy).then_inc(wuk_cp, 1)
            act.wait_ge(small_tp, 1)
            nc.scalar.activation(par_t[:, :], X[1][:, 0:PARS], ACT.Copy).then_inc(small_cp, 1)
            with act.Fori(0, QB // 2 - 1) as k:
                step.enter(k, 2)
                root_x(k, 0)
                square(k, 1)
                high_x(k, 0)
                root_x(k, 1)
                square(k + 1, 0)
                high_x(k, 1)
                step.leave(QB // 2 - 1)
            root_x(QB // 2 - 1, 0)
            square(QB // 2 - 1, 1)
            high_x(QB // 2 - 1, 0)
            root_x(QB // 2 - 1, 1)
            high_x(QB // 2 - 1, 1)

            def high(t, js=range(PIECES), n=P):
                for j in js:
                    act.wait_ge(w_in_s[j], 16 * t + 16)
                    act.wait_ge(w_used, 4 * t + j + 1)
                    nc.scalar.activation(w_hi[:, j, :, 0:n], w_raw[:, j, :, 0:n], ACT.Copy).then_inc(w_hi_s, 1)

            high(0, n=KW)
            high(1)
            act.wait_ge(bias_st, 16)
            act.wait_ge(wuk_st, 16)
            act.wait_ge(w_used, done(0))
            nc.scalar.activation(kw_sb[:, :], PJ[0][0:KW, :], ACT.Copy).then_inc(pj_free[0], 1)
            high(2)
            act.wait_ge(w_used, done(1))
            nc.scalar.activation(c_sb[:, 0, :], PJ[1][:, :], ACT.Copy).then_inc(pj_free[1], 1)
            act.wait_ge(pj_free[1], 2)
            nc.scalar.activation(c_sq[:, 0, :], c_sb[:, 0, :], ACT.Square).then_inc(c_sq_s, 1)
            act.wait_ge(k_dev, 1)
            nc.scalar.activation(k_t[:, :], kw_sb[0:ID, :], ACT.Square).then_inc(k_sq, 1)
            high(3)
            act.wait_ge(w_used, done(2))
            nc.scalar.activation(c_sb[:, 1, :], PJ[0][:, :], ACT.Copy).then_inc(pj_free[0], 1)
            act.wait_ge(pj_free[0], 3)
            nc.scalar.activation(c_sq[:, 1, :], c_sb[:, 1, :], ACT.Square).then_inc(c_sq_s, 1)
            act.wait_ge(k_var, 1)
            nc.scalar.activation(k_t[:, :], X[1][0:ID, :], ACT.Sqrt, bias=eps[0:ID, :]).then_inc(k_sd, 1)
            act.wait_ge(k_nrm, 1)
            nc.scalar.activation(k_t[:, :], kw_sb[0:ID, :], ACT.Identity, scale=k_gb[:, 0:1],
                                 bias=k_gb[:, 1:2]).then_inc(k_ln, 1)
            act.wait_ge(k_ln, 1)
            nc.scalar.activation(ki_hi[0:ID, :], k_t[:, :], ACT.Copy).then_inc(k_ln, 1)
            nc.scalar.activation(ki_hi[ID:P, :], k_t[:, :], ACT.Copy).then_inc(k_ln, 1)
            high(4)
            act.wait_ge(c_var, 1)
            nc.scalar.activation(c_rs[:, :], X[1][:, :], ACT.Sqrt, bias=eps[:, :]).then_inc(c_sd, 1)
            act.wait_ge(sp_in, 1)
            nc.scalar.activation(sp_t[:, 1, :], sp_t[:, 0, :], ACT.Exp).then_inc(sp_exp, 1)
            act.wait_ge(c_st, 16 * CT)

            def stacks(t, par):
                act.wait_ge(w_used, done(t))
                act.wait_ge(ix_mm, t * UNITS - UNITS * (T_QI - 1))
                nc.scalar.activation(stack_a[par][0:ID, :], PJ[par][0:ID, :], ACT.Copy).then_inc(st_hi, 1)
                nc.scalar.activation(stack_b[par][ID:P, :], PJ[par][ID:P, :], ACT.Copy).then_inc(st_hi, 1)

            def relus(t, ms):
                for m in ms:
                    q = FIRST_SCORED + m % (UNITS // 2)
                    w = (q + 1) * P
                    k = t * UNITS + (m - UNITS * T_QI)
                    act.wait_ge(ix_mm, k + 1 + 2 * UNITS)
                    act.wait_ge(ix_acc, k + 7)
                    nc.scalar.activation(relu[m % 2][:, 0:w], X[m % 2][:, 0:w], ACT.Relu).then_inc(ix_relu, 1)

            def act_b(t, par):
                stacks(t - 1, 1 - par)
                for j in range(PIECES):
                    high(t + 1, [j])
                    relus(t - 1, range(3 * j, 3 * j + 3))

            with act.Fori(0, 3) as i:
                act_b(i * 2 + (T_QI + 1), 0)
                act_b(i * 2 + (T_QI + 2), 1)
            act_b(T_QI + 7, 0)
            stacks(T_QI + 7, 0)
            relus(T_QI + 7, range(UNITS))

            act.wait_ge(ix_acc, 8 + 8 * UNITS)
            act.wait_ge(dec_s, 1)
            with act.Fori(0, G) as g:
                step.enter(g, 1)
                par = lambda k: lru_p[:, k, ds(g, 1)]
                high(g * 2 + (T_LRU + 1))
                act.wait_ge(w_used, g * 8 + done(T_LRU))
                act.wait_ge(y_lru, g + 1)
                nc.scalar.activation(xc[:, :], PJ[1][:, :], ACT.Identity, scale=conv_w[:, CONV - 1, ds(g, 1)],
                                     bias=par(0)).then_inc(xc0, 1)
                high(g * 2 + (T_LRU + 2))
                act.wait_ge(gates_mm, g + 2)
                nc.scalar.activation(rg[:, :], X[0][:, :], ACT.Sigmoid, bias=par(1)).then_inc(r_sig, 1)
                nc.scalar.activation(ig[:, :], X[1][:, :], ACT.Sigmoid, bias=par(2)).then_inc(i_sig, 1)
                act.wait_ge(y_st, 16 * g + 16)
                nc.scalar.activation(sg[:, :], PJ[0][:, :], ACT.Sigmoid).then_inc(g_sig, 1)
                act.wait_ge(r_sig, g + 1)
                nc.scalar.activation(th[:, :], rg[:, :], ACT.Tanh, scale=decay[:, 0, ds(g, 1)])
                s = step.did(nc.scalar.activation(av[:, :], rg[:, :], ACT.Exp, scale=decay[:, 1, ds(g, 1)]))
                act.wait_ge(act_step, s)
                nc.scalar.activation(rg[:, :], av[:, :], ACT.Square).then_inc(a_sq, 1)
                act.wait_ge(one_m, g + 1)
                nc.scalar.activation(th[:, :], th[:, :], ACT.Sqrt).then_inc(root, 1)
                step.leave(G)

            act.wait_ge(y_lru, G + 1)

            def att(h, last):
                high(h * 2 + (T_ATT + 1))
                act.wait_ge(w_used, h * 8 + done(T_ATT))
                act.wait_ge(q_st, h * 16 + 16)
                nc.scalar.activation(av[:, :], PJ[1][:, :], ACT.Copy, scale=-HD ** -0.5).then_inc(pj_free[1], 1)
                if not last:
                    high(h * 2 + (T_ATT + 2))
                act.wait_ge(w_used, h * 8 + done(T_ATT + 1))
                act.wait_ge(pj_free[0], h + (T_ATT + 1) // 2 + 1)
                nc.scalar.activation(ig[:, :], PJ[0][:, :], ACT.Sigmoid).then_inc(d_sig, 1)

            with act.Fori(0, NH - 1) as h:
                att(h, False)
            att(NH - 1, True)

            def kv(h, p, part):
                for k in range(2):
                    act.wait_ge(kv_mm_s, 4 * h + 2 * part + k + 1)
                    src = X[1][:, k * NT:(k + 1) * NT]
                    if part == 0:
                        dst = kT[p][:, k * NT:(k + 1) * NT]
                    else:
                        dst, src = vN[p][:, 4 * k:4 * k + 4, :], src.rearrange("p (t d) -> p t d", d=HD)
                    nc.scalar.activation(dst, src, ACT.Copy).then_inc(kv_cp, 1)

            def softexp(h, q):
                act.wait_ge(lg_used, 8 * h + q + 1)
                nc.scalar.activation(prob[q], prob[q], ACT.Exp, scale=-1.0,
                                     bias=sums[:, q, 0:1], accum_out=sums[:, q, 1:2]).then_inc(p_exp, 1)

            def p_copy(h, q):
                act.wait_ge(p_tp, 8 * h + q + 4)
                if q % 2 == 0:
                    act.wait_ge(ro_mm, 4 * h + q // 2 + 3)
                nc.scalar.activation(pT[(q // 2) % 2][:, 0:q + 1, (q % 2) * P:(q % 2) * P + P],
                                     LG[q][:, 0:(q + 1) * P].rearrange("p (t s) -> p t s", s=P),
                                     ACT.Copy).then_inc(p_cp, 1)

            def act_head(h, p, last=False):
                for q in range(QB):
                    p_copy(h, q)
                    if q + 2 < QB:
                        softexp(h, q + 2)
                    elif not last:
                        softexp(h + 1, q + 2 - QB)
                    if q == 0 and not last:
                        kv(h + 1, 1 - p, 0)
                    if q == 1 and not last:
                        kv(h + 1, 1 - p, 1)
                    if q in (4, 6):
                        k = q // 2 - 2
                        act.wait_ge(yl_ld, 32 * h + 16 * k + 16)
                        nc.scalar.activation(hT_hi[:, ds(h, 1), k * NT:(k + 1) * NT],
                                             yl_raw[:, :].rearrange("p (o s) -> p o s", o=1), ACT.Copy
                                             ).then_inc(yl_hi, 1)

            kv(0, 0, 0)
            kv(0, 0, 1)
            softexp(0, 0)
            softexp(0, 1)
            with act.Fori(0, 3) as i:
                act_head(i * 2, 0)
                act_head(i * 2 + 1, 1)
            act_head(6, 0)
            act_head(7, 1, last=True)

            def out_high(cg, js):
                for j in js:
                    act.wait_ge(wo_in[j % 4], 32 * cg + 16 * (j // 4) + 16)
                    act.wait_ge(wo_used, 8 * cg + j + 1)
                    nc.scalar.activation(wo_hi[:, j % 2, :, :], wo_raw[:, j % 4, :, :], ACT.Copy
                                         ).then_inc(wo_hi_s, 1)

            def squares(cg, c):
                for q in range(HALF_T):
                    act.wait_ge(o_add, 4 * cg + q + 9)
                    act.wait_ge(o_sq, 4 * cg + q + 1)
                    nc.scalar.activation(junk4[:, :], res[:, q, ds(c * OC, OC)], ACT.Square,
                                         accum_out=ssq[:, q, ds(c, 1)]).then_inc(o_sq, 1)

            def root_mean(th):
                act.wait_ge(f_tot, th + 1)
                nc.scalar.activation(fstat[:, 1, :], fstat[:, 0, :], ACT.Sqrt, scale=1.0 / D, bias=eps[:, :]
                                     ).then_inc(f_sd, 1)

            out_high(0, range(2))
            with act.Fori(0, OCH) as c:
                out_high(c, range(2, OP))
                out_high(c + 1, range(2))
                squares(c, c)
            root_mean(0)
            with act.Fori(0, OCH - 1) as c:
                out_high(c + OCH, range(2, OP))
                out_high(c + OCH + 1, range(2))
                squares(c + OCH, c)
            out_high(2 * OCH - 1, range(2, OP))
            squares(2 * OCH - 1, OCH - 1)
            root_mean(1)

        @block.tensor
        def _(pe):
            nc.tensor.sem_inc(w_used, PIECES)
            nc.tensor.sem_inc(wo_used, 2)
            nc.tensor.sem_inc(ix_mm, 2 * UNITS)
            nc.tensor.sem_inc(gates_mm, 1)
            nc.tensor.sem_inc(p_tp, 3)
            nc.tensor.sem_inc(ro_mm, 4)
            pe.wait_ge(bias_in, 32)
            nc.tensor.matmul(X[0][0:NH, 0:BR], rel[:, :], onehot[:, :], start=True, stop=True).then_inc(bias_mm, 1)
            pe.wait_ge(wuk_in, 16)
            pe.wait_ge(id_made, 1)
            for k in range(2):
                for n in range(8):
                    h, t = (8 * k + n) // CT, n % CT
                    last = nc.tensor.transpose(PJ[k][:, n * P:(n + 1) * P], wuk[:, h, t * P:(t + 1) * P], ident[:, :])
                last.then_inc(wuk_tp, 1)
            pe.wait_ge(wuk_cp, 2)
            pe.wait_ge(bias_cp, 1)
            pe.wait_ge(small_in, 16 * 8)
            nc.tensor.transpose(X[1][:, 0:PARS], par_rows[:, :], ident[0:PARS, 0:PARS]).then_inc(small_tp, 1)
            pe.wait_ge(small_cp, 1)
            with pe.Fori(0, QB // 2) as k:
                for u in range(2):
                    pe.wait_ge(x_norm, k * 2 + u + 1)
                    for j in range(2):
                        pe.wait_ge(h_lo, k * 4 + 2 * u + j + 1)
                        for n in range(8):
                            last = nc.tensor.transpose(PS[2 * u + j][:, n * P:(n + 1) * P],
                                                       xin[:, u, (8 * j + n) * P:(8 * j + n + 1) * P], ident[:, :])
                        last.then_inc(x_tp, 1)
            pe.wait_ge(h_lo, 4 + 2 * QB)

            def project_tile(t, par, turn, m=P, between=None):
                pe.wait_ge(pj_free[par], turn + 1)
                for j in range(PIECES):
                    pe.wait_ge(w_lo_s, 4 * t + j + 1 + PIECES)
                    for k in range(PK):
                        kt = j * PK + k
                        for n in range(2):
                            o = PJ[par][0:m, n * NT:(n + 1) * NT]
                            hi, lo = hT_hi[:, kt, n * NT:(n + 1) * NT], hT_lo[:, kt, n * NT:(n + 1) * NT]
                            whi, wlo = w_hi[:, j, k, 0:m], w_lo[:, j, k, 0:m]
                            end = kt == KT - 1
                            nc.tensor.matmul(o, wlo, hi, start=(kt == 0), stop=False)
                            nc.tensor.matmul(o, whi, lo, start=False, stop=False)
                            last = nc.tensor.matmul(o, whi, hi, start=False, stop=end)
                    last.then_inc(w_used, 1)
                    if between:
                        between(j)

            project_tile(0, 0, 0, m=KW)
            project_tile(1, 1, 0)
            pe.wait_ge(pj_free[0], 2)
            pe.wait_ge(ones_made, 1)
            for n in range(2):
                last = nc.tensor.matmul(X[0][0:ID, n * NT:(n + 1) * NT], ones_k[:, :],
                                        kw_sb[0:ID, n * NT:(n + 1) * NT], start=True, stop=True)
            last.then_inc(k_mean, 1)
            project_tile(2, 0, 1)
            pe.wait_ge(k_sq, 1)
            for n in range(2):
                last = nc.tensor.matmul(X[1][0:ID, n * NT:(n + 1) * NT], ones_k[:, :],
                                        k_t[:, n * NT:(n + 1) * NT], start=True, stop=True)
            last.then_inc(k_var, 1)
            for q in range(QB):
                last = nc.tensor.transpose(X[0][:, q * IH:(q + 1) * IH], kw_sb[ID:KW, q * P:(q + 1) * P],
                                           ident[ID:KW, ID:KW])
            last.then_inc(w_tp, 1)
            project_tile(3, 1, 1)
            pe.wait_ge(c_sq_s, 2)
            pe.wait_ge(k_sd, 1)
            for n in range(2):
                for t in range(CT):
                    last = nc.tensor.matmul(X[1][:, n * NT:(n + 1) * NT], ones_c[:, :],
                                            c_sq[:, t, n * NT:(n + 1) * NT], start=(t == 0), stop=(t == CT - 1))
            last.then_inc(c_var, 1)

            pe.wait_ge(ki_done, 2)
            pe.wait_ge(c_sd, 1)
            pe.wait_ge(w_nat_s, 1)

            def score(t, par, turn, ms):
                for m in ms:
                    q = FIRST_SCORED + m % (UNITS // 2)
                    w = (q + 1) * P
                    k = t * UNITS + (m - UNITS * T_QI)
                    if m == 0:
                        pe.wait_ge(pj_free[par], turn + 2)
                    pe.wait_ge(ix_relu, k + 1)
                    st = (stack_a, stack_b)[m // (UNITS // 2)][par]
                    for n in range(0, w, NT):
                        e = min(n + NT, w)
                        nc.tensor.matmul(X[m % 2][:, n:e], st[:, q * P:(q + 1) * P], ki_lo[:, n:e],
                                         start=True, stop=False)
                        last = nc.tensor.matmul(X[m % 2][:, n:e], st[:, q * P:(q + 1) * P], ki_hi[:, n:e],
                                                start=False, stop=True)
                    last.then_inc(ix_mm, 1)

            def step_b(t, par, turn):
                before = turn - 1 + par
                project_tile(t, par, turn, between=lambda j: score(t - 1, 1 - par, before, range(3 * j, 3 * j + 3)))

            with pe.Fori(0, 3) as i:
                step_b(i * 2 + (T_QI + 1), 0, i + 2)
                step_b(i * 2 + (T_QI + 2), 1, i + 2)
            step_b(T_QI + 7, 0, 5)
            score(T_QI + 7, 0, 5, range(UNITS))

            with pe.Fori(0, G) as g:
                project_tile(g * 2 + T_LRU, 1, g + T_LRU // 2)
                project_tile(g * 2 + (T_LRU + 1), 0, g + (T_LRU + 1) // 2)
                pe.wait_ge(pj_free[1], g + T_LRU // 2 + 2)
                pe.wait_ge(gw_in, g * 32 + 32)
                pe.wait_ge(i_sig, g + 1)
                for k in range(2):
                    for n in range(2):
                        last = nc.tensor.matmul(X[k][:, n * NT:(n + 1) * NT], w_gates[:, k, :],
                                                xc[:, n * NT:(n + 1) * NT], start=True, stop=True)
                last.then_inc(gates_mm, 1)

            with pe.Fori(0, NH) as h:
                project_tile(h * 2 + T_ATT, 1, h + T_ATT // 2)
                project_tile(h * 2 + (T_ATT + 1), 0, h + (T_ATT + 1) // 2)

            def kv_mm(h, p, part, turn):
                if part == 0:
                    pe.wait_ge(kv_ld[p], turn * 32 + 32)
                for k in range(2):
                    if part == 0:
                        pe.wait_ge(o_used, 4 * h - 1 + k)
                    else:
                        pe.wait_ge(kv_cp, 4 * h + k + 1)
                    o = X[1][:, k * NT:(k + 1) * NT]
                    if part == 0:
                        for t in range(CT):
                            last = nc.tensor.matmul(o, wk[p][:, t, :], c_t[:, t, k * NT:(k + 1) * NT],
                                                    start=(t == 0), stop=(t == CT - 1))
                    else:
                        for s in range(4):
                            for t in range(CT):
                                last = nc.tensor.matmul(o[:, s * HD:(s + 1) * HD],
                                                        c_t[:, t, (4 * k + s) * P:(4 * k + s + 1) * P], wv[p][:, t, :],
                                                        start=(t == 0), stop=(t == CT - 1))
                    last.then_inc(kv_mm_s, 1)

            def logits(h, q, p, turn):
                w = (q + 1) * P
                if q == 0:
                    pe.wait_ge(qb_ld[p], turn * 32 + 32)
                    pe.wait_ge(kv_cp, 4 * h + 2)
                pe.wait_ge(p_cp, 8 * h + q + 5 - LAST[q])
                for n in range(0, w, NT):
                    e = min(n + NT, w)
                    last = nc.tensor.matmul(LG[q][:, n:e], qT[p][:, q * P:(q + 1) * P], kT[p][:, n:e],
                                            start=True, stop=True)
                last.then_inc(lg_mm, 1)

            def turn_p(h, q):
                pe.wait_ge(p_norm, 8 * h + q + 1)
                for t in range(q + 1):
                    last = nc.tensor.transpose(LG[q][:, t * P:(t + 1) * P], prob[q][:, t * P:(t + 1) * P],
                                               ident[:, :])
                last.then_inc(p_tp, 1)

            def read_out(h, pr, p, last_head):
                pe.wait_ge(p_cp, 8 * h + 2 * pr + 6)
                if pr == 0:
                    pe.wait_ge(kv_cp, 4 * h + 4)
                if pr < 2 and not last_head:
                    pe.wait_ge(kv_cp, 4 * h + pr + 7)
                else:
                    pe.wait_ge(o_used, 4 * h + pr + 3)
                k = pr % 2
                for t in range(2 * pr + 2):
                    c0 = P if t == 2 * pr + 1 else 0
                    last = nc.tensor.matmul(X[1][:, k * NT + c0:k * NT + 2 * P], vN[p][:, t, :],
                                            pT[k][:, t, c0:2 * P], start=(t == 0), stop=(t == 2 * pr + 1))
                last.then_inc(ro_mm, 1)

            def pe_head(h, p, turn_next, last=False):
                for q in range(QB):
                    turn_p(h, q)
                    if q < 2 and not last:
                        kv_mm(h + 1, 1 - p, q, turn_next)
                    if q in (3, 4, 6):
                        read_out(h, {3: 0, 4: 1, 6: 2}[q], p, last)
                    if q + AHEAD < QB:
                        logits(h, q + AHEAD, p, None)
                    elif not last:
                        logits(h + 1, q + AHEAD - QB, 1 - p, turn_next)
                read_out(h, 3, p, last)

            pe.wait_ge(pj_free[0], (TILES - 1) // 2 + 2)
            pe.wait_ge(c_ld, 16)
            pe.wait_ge(mask_s, 1)
            pe.wait_ge(kv_ld[0], 32)
            for k in range(2):
                for t in range(CT):
                    last = nc.tensor.matmul(X[1][:, k * NT:(k + 1) * NT], wk[0][:, t, :],
                                            c_t[:, t, k * NT:(k + 1) * NT], start=(t == 0), stop=(t == CT - 1))
                last.then_inc(kv_mm_s, 1)
            kv_mm(0, 0, 1, 0)
            logits(0, 0, 0, 0)
            logits(0, 1, 0, 0)
            logits(0, 2, 0, 0)
            with pe.Fori(0, 3) as i:
                pe_head(i * 2, 0, i)
                pe_head(i * 2 + 1, 1, i + 1)
            pe_head(6, 0, 3)
            pe_head(7, 1, None, last=True)

            def banks(u, q):
                return PS[2 * u + q // 2][:, (q % 2) * NT:(q % 2) * NT + OC]

            def out_chunk(cg, th, u):
                for j in range(OP):
                    pe.wait_ge(wo_lo_s, 8 * cg + j + 5)
                    for q in range(HALF_T):
                        if j == 0:
                            pe.wait_ge(o_add, 4 * cg + q + 1)
                        tok = slice((th * HALF_T + q) * P, (th * HALF_T + q + 1) * P)
                        for k in range(OPK):
                            kt = j * OPK + k
                            o = banks(u, q)
                            nc.tensor.matmul(o, hT_lo[:, kt, tok], wo_hi[:, j % 2, k, :], start=(kt == 0), stop=False)
                            nc.tensor.matmul(o, hT_hi[:, kt, tok], wo_lo[:, j % 2, k, :], start=False, stop=False)
                            last = nc.tensor.matmul(o, hT_hi[:, kt, tok], wo_hi[:, j % 2, k, :],
                                                    start=False, stop=(kt == KT - 1))
                        if j == OP - 1 and q < HALF_T - 1:
                            last.then_inc(o_mm, 1)
                    last.then_inc(wo_used, 1)

            pe.wait_ge(y_att, 4 * NH + 1)
            pe.wait_ge(yl_lo, 1 + 2 * G)
            for th in range(2):
                with pe.Fori(0, 2) as i:
                    out_chunk(i * 2 + OCH * th, th, 0)
                    out_chunk(i * 2 + (OCH * th + 1), th, 1)

        @block.vector
        def _(dve):
            nc.vector.sem_inc(h_lo, 4)
            nc.vector.sem_inc(ix_acc, 8)
            nc.vector.sem_inc(y_lru, 1)
            nc.vector.sem_inc(o_used, 4)
            nc.vector.sem_inc(yl_lo, 1)
            nc.vector.sem_inc(y_att, 1)
            nc.vector.sem_inc(o_add, 8)
            step = Tally(dve_step)
            tt, stt = nc.vector.tensor_tensor, nc.vector.scalar_tensor_tensor

            def chain(ins):
                dve.wait_ge(dve_step, step.did(ins))

            def hold():
                nc.vector.memset(pause[:, :], 0.0)

            nc.vector.memset(eps[:, :], EPS).then_inc(eps_made, 1)
            nc.vector.memset(par_rows[:, :], 0.0).then_inc(rows_clear, 1)
            dve.wait_ge(g_in, 16)

            def norm_x(k, u):
                dve.wait_ge(x_sd, k * 2 + u + 1)
                chain(nc.vector.reciprocal(stat[:, 4 + u:5 + u], stat[:, 2 + u:3 + u]))
                stt(xin[:, u, :], xin[:, u, :], stat[:, 4 + u:5 + u], g_bc[:, :], ALU.mult, ALU.mult
                    ).then_inc(x_norm, 1)

            def low_x(k, u):
                for j in range(2):
                    dve.wait_ge(h_hi, k * 4 + 2 * u + j + 1)
                    tok = ds(k * 2 * P + u * P, P)
                    tt(hT_lo[:, 8 * j:8 * j + 8, tok], PS[2 * u + j][:, :].rearrange("p (t s) -> p t s", s=P),
                       hT_hi[:, 8 * j:8 * j + 8, tok].bitcast(F32), ALU.subtract).then_inc(h_lo, 1)

            norm_x(0, 0)
            with dve.Fori(0, QB // 2 - 1) as k:
                step.enter(k, 2)
                norm_x(k, 1)
                low_x(k, 0)
                norm_x(k + 1, 0)
                low_x(k, 1)
                step.leave(QB // 2 - 1)
            norm_x(QB // 2 - 1, 1)
            low_x(QB // 2 - 1, 0)
            low_x(QB // 2 - 1, 1)

            dve.wait_ge(x_tp, 2 * QB)
            dve.wait_ge(bias_st, 16)
            dve.wait_ge(wuk_st, 16)
            chain(nc.vector.memset(ones_k[:, :], 1.0 / ID))
            nc.vector.memset(ones_c[:, :], 1.0 / C).then_inc(ones_made, 1)
            chain(nc.vector.memset(scores[:, :], 0.0))
            dve.wait_ge(consts, 1)
            for q in range(FIRST_SCORED, QB):
                s = step.did(nc.vector.tensor_copy(scores[:, off(q) + q * P:off(q) + (q + 1) * P], causal[:, :]))
            dve.wait_ge(dve_step, s)
            dve.wait_ge(small_cp, 1)
            lam = lru_p[:, 3, :]
            chain(nc.vector.tensor_scalar(sp_t[:, 4, :], lam, -1.0, None, ALU.mult))
            chain(nc.vector.tensor_scalar(sp_t[:, 2, :], sp_t[:, 4, :], 0.0, None, ALU.max))
            tt(sp_t[:, 0, :], sp_t[:, 4, :], lam, ALU.min).then_inc(sp_in, 1)
            dve.wait_ge(k_mean, 1)
            tt(kw_sb[0:ID, :], kw_sb[0:ID, :], X[0][0:ID, :], ALU.subtract).then_inc(k_dev, 1)
            dve.wait_ge(k_sd, 1)
            chain(nc.vector.reciprocal(k_t[:, :], k_t[:, :]))
            tt(kw_sb[0:ID, :], kw_sb[0:ID, :], k_t[:, :], ALU.mult).then_inc(k_nrm, 1)
            dve.wait_ge(w_tp, 1)
            nc.vector.tensor_scalar(w_nat[:, :, :], X[0][:, 0:QB * IH].rearrange("p (q h) -> p q h", h=IH),
                                    IH ** -0.5 * ID ** -0.5, None, ALU.mult).then_inc(w_nat_s, 1)
            dve.wait_ge(k_ln, 3)
            tt(ki_lo[0:ID, :], k_t[:, :], ki_hi[0:ID, :].bitcast(F32), ALU.subtract).then_inc(ki_done, 1)
            tt(ki_lo[ID:P, :], k_t[:, :], ki_hi[0:ID, :].bitcast(F32), ALU.subtract).then_inc(ki_done, 1)
            dve.wait_ge(c_sd, 1)
            chain(nc.vector.reciprocal(c_rs[:, :], c_rs[:, :]))
            for t in range(CT):
                stt(c_sb[:, t, :], c_sb[:, t, :], c_g[:, t:t + 1], c_rs[:, :], ALU.mult, ALU.mult
                    ).then_inc(c_done, 1)
            dve.wait_ge(sp_exp, 1)
            z, s_, q_, p_ = (sp_t[:, k, :] for k in (1, 3, 4, 0))
            chain(nc.vector.tensor_scalar(s_, z, 2.0, None, ALU.add))
            chain(nc.vector.reciprocal(s_, s_))
            chain(tt(s_, s_, z, ALU.mult))
            chain(tt(q_, s_, s_, ALU.mult))
            chain(nc.vector.tensor_scalar(p_, q_, 1.0 / 13, None, ALU.mult))
            for n in (11, 9, 7, 5, 3):
                chain(stt(p_, p_, 1.0 / n, q_, ALU.add, ALU.mult))
            chain(stt(p_, p_, 1.0, s_, ALU.add, ALU.mult))
            chain(stt(p_, p_, 2.0, sp_t[:, 2, :], ALU.mult, ALU.add))
            chain(nc.vector.tensor_scalar(decay[:, 0, :], p_, 8.0, None, ALU.mult))
            nc.vector.tensor_scalar(decay[:, 1, :], p_, -8.0, None, ALU.mult).then_inc(dec_s, 1)
            dve.wait_ge(c_st, 16 * CT)

            def stacks(t, par):
                dve.wait_ge(st_hi, t * 2 - 2 * (T_QI - 1))
                tt(stack_a[par][ID:P, :], PJ[par][0:ID, :], stack_a[par][0:ID, :].bitcast(F32), ALU.subtract)
                tt(stack_b[par][0:ID, :], PJ[par][ID:P, :], stack_b[par][ID:P, :].bitcast(F32), ALU.subtract
                   ).then_inc(pj_free[par], 1)

            def add_scores(t):
                for m in range(UNITS):
                    q = FIRST_SCORED + m % (UNITS // 2)
                    w = (q + 1) * P
                    k = t * UNITS + (m - UNITS * T_QI)
                    dve.wait_ge(ix_relu, k + 3)
                    dve.wait_ge(ix_acc, k + 3)
                    acc = scores[:, off(q):off(q) + w]
                    head = t * 2 + (m // (UNITS // 2) - 2 * T_QI)
                    stt(acc, relu[m % 2][:, 0:w], w_nat[:, q, ds(head, 1)], acc, ALU.mult, ALU.add
                        ).then_inc(ix_acc, 1)

            def dve_b(t, par):
                stacks(t - 1, 1 - par)
                add_scores(t - 1)

            with dve.Fori(0, 3) as i:
                dve_b(i * 2 + (T_QI + 1), 0)
                dve_b(i * 2 + (T_QI + 2), 1)
            dve_b(T_QI + 7, 0)
            stacks(T_QI + 7, 0)
            add_scores(T_QI + 7)
            dve.wait_ge(ix_acc, 8 + 8 * UNITS)

            def top_rounds(n):
                for _ in range(n):
                    for q in range(FIRST_SCORED, QB):
                        found = step.did(nc.vector.max(top8[:, q, :], scores[:, off(q):off(q) + (q + 1) * P]))
                    dve.wait_ge(dve_step, found)
                    hold()
                    for q in range(FIRST_SCORED, QB):
                        left = scores[:, off(q):off(q) + (q + 1) * P]
                        marked = step.did(nc.vector.match_replace(left, top8[:, q, :], left, TAKEN))
                    dve.wait_ge(dve_step, marked)
                    hold()

            per = ROUNDS // (G + NH)
            with dve.Fori(0, G) as g:
                step.enter(g, 2 + 12 * per + 4)
                dve.wait_ge(xc0, g + 1)
                xa = PJ[1]
                for n in (1, 2, 3):
                    tap = stt(xc[:, n:], xa[:, 0:S - n], conv_w[:, CONV - 1 - n, ds(g, 1)], xc[:, n:],
                              ALU.mult, ALU.add)
                    if n < 3:
                        chain(tap)
                    else:
                        tap.then_inc(pj_free[1], 1)
                top_rounds(per)
                dve.wait_ge(a_sq, g + 1)
                stt(th[:, :], rg[:, :], 1.0, th[:, :], ALU.add, ALU.mult).then_inc(one_m, 1)
                dve.wait_ge(i_sig, g + 2)
                chain(tt(ig[:, :], ig[:, :], xc[:, :], ALU.mult))
                dve.wait_ge(g_sig, g + 1)
                tt(sg[:, :], PJ[0][:, :], sg[:, :], ALU.mult).then_inc(pj_free[0], 1)
                dve.wait_ge(root, g + 1)
                chain(nc.vector.memset(th[:, 0:1], 1.0))
                chain(tt(ig[:, :], ig[:, :], th[:, :], ALU.mult))
                chain(nc.vector.tensor_tensor_scan(rg[:, :], av[:, :], ig[:, :], 0.0, ALU.mult, ALU.add))
                tt(sg[:, :], sg[:, :], rg[:, :], ALU.mult).then_inc(y_lru, 1)
                step.leave(G)
            dve.wait_ge(y_lru, G + 1)

            with dve.Fori(0, NH) as h:
                step.enter(h, 12 * per)
                top_rounds(per)
                dve.wait_ge(d_sig, h + 1)
                dve.wait_ge(gate_st, h * 16 + 16)
                tt(rg[:, :], PJ[0][:, :], ig[:, :], ALU.mult).then_inc(pj_free[0], 1)
                step.leave(NH)
            for q in range(FIRST_SCORED, QB):
                nc.vector.tensor_scalar(mask[:, OFF[q]:OFF[q] + (q + 1) * P], scores[:, off(q):off(q) + (q + 1) * P],
                                        (NEG + TAKEN) / 2, BIG, ALU.is_gt, ALU.mult)
            nc.vector.memset(mask[:, P:2 * P], 0.0)
            nc.vector.tensor_scalar(mask[:, 0:P], causal[:, :], NEG / 2, BIG, ALU.is_lt, ALU.mult)
            nc.vector.tensor_scalar(mask[:, 2 * P:3 * P], causal[:, :], NEG / 2, BIG, ALU.is_lt, ALU.mult
                                    ).then_inc(mask_s, 1)
            dve.wait_ge(mask_s, 1)

            def softmin(h, q, p, turn):
                w = (q + 1) * P
                n = min(w, 2 * P)
                if q == 0:
                    dve.wait_ge(qb_ld[p], turn * 32 + 32)
                dve.wait_ge(lg_mm, 8 * h + q + 1)
                lg = LG[q]
                chain(tt(lg[:, w - n:w], lg[:, w - n:w], tb[p][:, 2 * P - n:2 * P], ALU.add))
                dve.wait_ge(p_tp, 8 * h + q + 1)
                hold()
                nc.vector.tensor_tensor_reduce(prob[q], lg[:, 0:w], mask[:, OFF[q]:OFF[q] + w],
                                               1.0, 3.0e38, ALU.add, ALU.min, sums[:, q, 0:1]
                                               ).then_inc(lg_used, 1)

            def normalise(h, q):
                dve.wait_ge(p_exp, 8 * h + q + 1)
                chain(nc.vector.reciprocal(sums[:, q, 2:3], sums[:, q, 1:2]))
                nc.vector.tensor_scalar(prob[q], prob[q], sums[:, q, 2:3], None, ALU.mult).then_inc(p_norm, 1)

            def gated(h, r):
                dve.wait_ge(ro_mm, 4 * h + r + 5)
                dve.wait_ge(gate_ld[r % 2], h * 32 + 16 * (r // 2) + 16)
                dve.wait_ge(y_att, 4 * h + r + 1)
                tok = slice(2 * r * P, 2 * (r + 1) * P)
                tt(yf[:, :], X[1][:, (r % 2) * NT:(r % 2) * NT + 2 * P], gate[:, r % 2, :], ALU.mult).then_inc(o_used, 1)
                dve.wait_ge(o_used, 4 * h + r + 5)
                y3 = yf[:, :].rearrange("p (o s) -> p o s", o=1)
                chain(nc.vector.tensor_copy(hT_hi[:, ds(h + G, 1), tok], y3))
                tt(hT_lo[:, ds(h + G, 1), tok], y3, hT_hi[:, ds(h + G, 1), tok].bitcast(F32), ALU.subtract
                   ).then_inc(y_att, 1)

            def dve_head(h, p, turn, last=False):
                for q in range(QB):
                    if q + 1 < QB:
                        normalise(h, q + 1)
                    elif not last:
                        normalise(h + 1, 0)
                    if q + AHEAD < QB:
                        softmin(h, q + AHEAD, p, None)
                    elif not last:
                        softmin(h + 1, q + AHEAD - QB, 1 - p, turn)
                    if q in (4, 5, 7):
                        gated(h, {4: 0, 5: 1, 7: 2}[q])
                    if q in (4, 6):
                        k = q // 2 - 2
                        dve.wait_ge(yl_hi, 2 * h + k + 1)
                        piece = (slice(None), ds(h, 1), slice(k * NT, (k + 1) * NT))
                        tt(hT_lo[piece], yl_raw[:, :].rearrange("p (o s) -> p o s", o=1),
                           hT_hi[piece].bitcast(F32), ALU.subtract).then_inc(yl_lo, 1)
                gated(h, 3)

            softmin(0, 0, 0, 0)
            softmin(0, 1, 0, 0)
            softmin(0, 2, 0, 0)
            normalise(0, 0)
            links = 8 + 8 + 4
            with dve.Fori(0, 3) as i:
                step.enter(i, 2 * links)
                dve_head(i * 2, 0, i)
                dve_head(i * 2 + 1, 1, i + 1)
                step.leave(3)
            dve_head(6, 0, 3)
            dve_head(7, 1, None, last=True)
            dve.wait_ge(y_att, 4 * NH + 1)

            def add_residual(cg, c, u):
                for q in range(HALF_T):
                    if q < HALF_T - 1:
                        dve.wait_ge(o_mm, cg * (HALF_T - 1) + q + 1)
                    else:
                        dve.wait_ge(wo_used, cg * OP + OP + 2)
                    r = res[:, q, ds(c * OC, OC)]
                    tt(r, PS[2 * u + q // 2][:, (q % 2) * NT:(q % 2) * NT + OC], r, ALU.add).then_inc(o_add, 1)

            dve.wait_ge(gf_in, 16)
            for th_ in range(2):
                dve.wait_ge(res_in, 64 * (th_ + 1))
                with dve.Fori(0, OCH // 2) as i:
                    for u in range(2):
                        add_residual(i * 2 + (OCH * th_ + u), i * 2 + u, u)
                dve.wait_ge(o_sq, HALF_T * OCH * (th_ + 1) + 1)
                nc.vector.reduce_sum(fstat[:, 0, :], ssq[:, :, :], AX.X).then_inc(f_tot, 1)
                dve.wait_ge(f_sd, th_ + 1)
                chain(nc.vector.reciprocal(fstat[:, 2, :], fstat[:, 1, :]))
                for q in range(HALF_T):
                    stt(res[:, q, :], res[:, q, :], fstat[:, 2, q:q + 1], gf_bc[:, :], ALU.mult, ALU.mult
                        ).then_inc(f_out, 1)


def distance_buckets():
    import numpy as np
    dist = np.maximum(2 * P - 1 - np.arange(BR), 0)
    exact = BUCKETS // 2
    far = exact + (np.log(np.maximum(dist, 1) / exact) / math.log(MAX_DIST / exact)
                   * (BUCKETS - exact)).astype(np.int64)
    bucket = np.where(dist < exact, dist, np.minimum(far, BUCKETS - 1))
    hot = (np.arange(BUCKETS)[:, None] == bucket[None, :]).astype(np.float32)
    hot[BUCKETS - 1] -= 1.0
    return np.ascontiguousarray(-hot)


_INS = ["x", "norm_g", "w_in", "conv_w", "conv_b", "lru_wa", "lru_ba", "lru_wx", "lru_bx", "lru_lambda",
        "ckv_norm_g", "idx_k_norm_g", "idx_k_norm_b", "w_uk", "w_uv", "w_out", "rel_bias", "final_norm_g"]


def kernel(**inputs):
    import numpy as np
    import concourse.bacc as bacc
    from concourse.bass_utils import run_bass_kernel_spmd

    nc = bacc.Bacc("TRN2", target_bir_lowering=False, num_devices=1)
    arrays, aps = {}, {}
    values = {name: np.ascontiguousarray(inputs[name]) for name in _INS}
    values["onehot"] = distance_buckets()
    for name, v in values.items():
        arrays[f"in_{name}"] = v
        aps[name] = nc.dram_tensor(f"in_{name}", v.shape, mybir.dt.from_np(v.dtype), kind="ExternalInput").ap()
    out = nc.dram_tensor("out_0", (1, S, D), F32, kind="ExternalOutput").ap()
    layer(nc, aps, out)
    r = run_bass_kernel_spmd(nc, [arrays], core_ids=[0])
    return r.results[0]["out_0"]
```

```python
import math
from contextlib import ExitStack

import concourse.bass as bass
from concourse import mybir

F32 = mybir.dt.float32
F32R = mybir.dt.float32r
BF16 = mybir.dt.bfloat16
ALU = mybir.AluOpType
ACT = mybir.ActivationFunctionType
AX = mybir.AxisListType
ds = bass.ds

P = 128
D = 2048
S = 1024
KT = D // P
QB = S // P
LRU = 1024
G = LRU // P
CONV = 4
NH = 8
HD = 128
C = 256
CT = C // P
IH = 16
ID = 64
TOPK = 256
BUCKETS = 32
MAX_DIST = 128
EPS = 1e-6
NT = 512

COL_XA, COL_GA, COL_Q, COL_CKV, COL_GB, COL_QI, COL_KI = 0, 1024, 2048, 3072, 3328, 4352, 5376
KW = ID + IH
PIECES = 4
PK = KT // PIECES

T_KW, T_C, T_QI, T_LRU, T_ATT = 0, 1, 3, 11, 27
TILES = 43

PARS = (CONV + 4) * G + CT + 2

XB = 4
AHEAD = 3

FIRST_SCORED = TOPK // P
UNITS = 2 * (QB - FIRST_SCORED)
FULL = sum((q + 1) * P for q in range(QB))
OFF = [P * q * (q + 1) // 2 for q in range(QB)]
SCORED = FULL - OFF[FIRST_SCORED]
NEG = -3.0e38
TAKEN = -3.38e38
BIG = 1.0e30
ROUNDS = TOPK // 8
BR = 3 * P

OC = 512
OCH = D // OC
OPK = 2
OP = KT // OPK
HALF_T = 4


def off(q):
    return OFF[q] - OFF[FIRST_SCORED]


class Tally:

    def __init__(self, sem):
        self.sem, self.base, self.n = sem, 0, 0

    def did(self, ins):
        ins.then_inc(self.sem, 1)
        self.n += 1
        return self.base + self.n

    def now(self):
        return self.base + self.n

    def enter(self, i, per):
        self.start, self.per = self.base + self.n, per
        self.base, self.n = self.start + i * per, 0

    def leave(self, count):
        assert self.n == self.per, (self.n, self.per)
        self.base, self.n = self.start + count * self.per, 0


def layer(nc, a, out):
    x, w_in, w_out = a["x"][0], a["w_in"][0], a["w_out"][0]

    yl_d = nc.dram_tensor("y_lru_dram", [G, P, S], F32).ap()
    q_d = nc.dram_tensor("q_dram", [NH, P, S], F32).ap()
    gate_d = nc.dram_tensor("gate_dram", [NH, P, S], F32).ap()
    c_d = nc.dram_tensor("c_dram", [CT, P, S], F32).ap()
    wk_d = nc.dram_tensor("wuk_dram", [NH, P, CT, HD], F32).ap()
    bias_h = nc.dram_tensor("bias_rows", [NH, P * BR], F32)
    bias_d = bias_h.ap()

    ctx = ExitStack()
    with ctx:
        def sem(name):
            return ctx.enter_context(nc.semaphore(name))

        def alloc(stack):
            return lambda name, shape, dt=F32: stack.enter_context(nc.sbuf_tensor(name, shape, dt))

        sb = alloc(ctx)
        hT_hi = sb("hT_hi", [P, KT, S], F32R)
        hT_lo = sb("hT_lo", [P, KT, S], F32R)
        ident = sb("ident", [P, P])
        causal = sb("causal", [P, P])
        par_t = sb("par_t", [P, PARS])
        conv_w = par_t[:, 0:CONV * G].rearrange("p (j g) -> p j g", g=G)
        lru_p = par_t[:, CONV * G:(CONV + 4) * G].rearrange("p (k g) -> p k g", g=G)
        c_g = par_t[:, PARS - 4:PARS - 2]
        k_gb = par_t[0:ID, PARS - 2:PARS]
        decay = sb("decay", [P, 2, G])
        sp_t = sb("sp_t", [P, 5, G])
        eps = sb("eps", [P, 1])
        pause = sb("pause", [P, 1])
        stat = sb("stat", [P, 12])
        w_nat = sb("w_nat", [P, QB, IH])
        top8 = sb("top8", [P, QB, 8])
        sums = sb("sums", [P, QB, 3])

        ph = ExitStack()
        sbp = alloc(ph)
        w_raw = sbp("w_raw", [P, PIECES, PK, P])
        w_hi = sbp("w_hi", [P, PIECES, PK, P], F32R)
        w_lo = sbp("w_lo", [P, PIECES, PK, P], F32R)
        p0 = ExitStack()
        s0 = alloc(p0)
        xin = s0("xin", [P, XB, D])
        g_bc = s0("g_bc", [P, D])
        junk = s0("junk", [P, D], BF16)
        par_rows = s0("par_rows", [PARS, P])
        onehot = s0("onehot", [BUCKETS, BR])
        rel = s0("rel", [BUCKETS, NH])
        bias_sb = s0("bias_sb", [NH, BR])
        p0.close()
        scores = sbp("scores", [P, SCORED])
        pb = ExitStack()
        sB = alloc(pb)
        ki_hi = sB("ki_hi", [P, S], F32R)
        ki_lo = sB("ki_lo", [P, S], F32R)
        pa = ExitStack()
        sA = alloc(pa)
        kw_sb = sA("kw_sb", [KW, S])
        k_t = sA("k_t", [ID, S])
        c_sb = sA("c_sb", [P, CT, S])
        c_sq = sA("c_sq", [P, CT, S])
        c_rs = sA("c_rs", [P, S])
        ones_k = sA("ones_k", [ID, ID])
        ones_c = sA("ones_c", [P, P])
        pa.close()
        stack_a1 = sB("stack_a1", [P, S], F32R)
        stack_b1 = sB("stack_b1", [P, S], F32R)
        stack_a0 = sB("stack_a0", [P, S], F32R)
        stack_b0 = sB("stack_b0", [P, S], F32R)
        relu = [sB(f"relu{i}", [P, S]) for i in range(2)]
        stack_a, stack_b = [stack_a0, stack_a1], [stack_b0, stack_b1]
        pb.close()
        pc = ExitStack()
        sC = alloc(pc)
        rg = sC("rg", [P, S])
        av = sC("av", [P, S])
        ig = sC("ig", [P, S])
        pu = ExitStack()
        sU = alloc(pu)
        wuk = sU("wuk", [P, NH, C])
        wuk_t0 = sU("wuk_t0", [P, NH * CT // 2, HD])
        pu.close()
        pu = ExitStack()
        wuk_t1 = alloc(pu)("wuk_t1", [P, NH * CT // 2, HD])
        pu.close()
        wuk_t = [wuk_t0, wuk_t1]
        xc = sC("xc", [P, S])
        th = sC("th", [P, S])
        sg = sC("sg", [P, S])
        w_gates = sC("w_gates", [P, 2, P])
        mask_at = 4 * (3 * PIECES * PK * P + SCORED + 6 * S + 2 * P)
        mask = sC("mask", [P, FULL], BF16)
        pc.close()
        ph.close()

        ph = ExitStack()
        s3 = alloc(ph)
        c_t = s3("c_t", [P, CT, S])
        kT = [s3(f"kT{i}", [P, S]) for i in range(2)]
        vN = [s3(f"vN{i}", [P, QB, HD]) for i in range(2)]
        prob_sb = s3("prob_sb", [P, (8 + 7 + 6) * P])
        pT0 = s3("pT0", [P, 6, 2 * P])
        pT1 = s3("pT1", [P, 8, 2 * P])
        qT1 = s3("qT1", [P, S])
        qT0 = s3("qT0", [P, S])
        qT = [qT0, qT1]
        gate = s3("gate", [P, 2, 2 * P])
        wk = [s3(f"wk{i}", [P, CT, HD]) for i in range(2)]
        wv = [s3(f"wv{i}", [P, CT, HD]) for i in range(2)]
        tb = [s3(f"tb{i}", [P, 2 * P]) for i in range(2)]
        yf = s3("yf", [P, 2 * P])
        before = 4 * (CT * S + 6 * S + 21 * P + 14 * 2 * P + 4 * P + 4 * CT * HD + 4 * P + 2 * P)
        assert before == mask_at
        s3("mask_kept", [P, FULL], BF16)
        yl_raw = s3("yl_raw", [P, NT])
        pT = [pT0, pT1]
        ph.close()

        ph = ExitStack()
        s4 = alloc(ph)
        wo_raw = s4("wo_raw", [P, 4, OPK, OC])
        gf_bc = s4("gf_bc", [P, D])
        wo_lo = s4("wo_lo", [P, 2, OPK, OC], F32R)
        res01 = s4("res01", [P, 2, D])
        s4("wo_pad", [P, P])
        wo_hi = s4("wo_hi", [P, 2, OPK, OC], F32R)
        res23 = s4("res23", [P, 2, D])
        res = [res01[:, 0, :], res01[:, 1, :], res23[:, 0, :], res23[:, 1, :]]
        junk4 = s4("junk4", [P, OC], BF16)
        ssq = s4("ssq", [P, HALF_T, OCH])
        fstat = s4("fstat", [P, 3, HALF_T])
        ph.close()

        PS = [ctx.enter_context(nc.psum_tensor(f"ps{i}", [P, S], F32)) for i in range(4)]
        PJ, X = PS[0:2], PS[2:4]

        PROB_AT = [15 * P, 16 * P, 18 * P, 8 * P, 0, 15 * P, 8 * P, 0]
        prob = [prob_sb[:, PROB_AT[q]:PROB_AT[q] + (q + 1) * P] for q in range(QB)]
        LG = [PS[0][:, 0:NT], PS[0][:, NT:S], PS[1][:, 0:NT], PS[1][:, NT:S], PS[2], PS[0], PS[1], PS[2]]
        LAST = [3, 4, 4, 5, 5, 4, 3, 3]

        id_made = sem("id_made")
        consts = sem("consts")
        eps_made = sem("eps_made")
        ones_made = sem("ones_made")
        rows_clear = sem("rows_clear")
        small_in = sem("small_in")
        small_tp = sem("small_tp")
        small_cp = sem("small_cp")
        bias_in = sem("bias_in")
        bias_mm = sem("bias_mm")
        bias_cp = sem("bias_cp")
        bias_st = sem("bias_st")
        wuk_in = sem("wuk_in")
        wuk_tp = sem("wuk_tp")
        wuk_cp = sem("wuk_cp")
        wuk_st = sem("wuk_st")
        g_in = sem("g_in")
        x_in = [sem(f"x_in{i}") for i in range(XB)]
        x_rest = [sem(f"x_rest{i}") for i in range(QB - XB)]
        x_sd = sem("x_sd")
        x_norm = sem("x_norm")
        x_tp = sem("x_tp")
        h_hi = sem("h_hi")
        h_lo = sem("h_lo")
        w_in_s = [sem(f"w_in{j}") for j in range(PIECES)]
        w_hi_s = sem("w_hi_s")
        w_lo_s = sem("w_lo_s")
        w_used = sem("w_used")
        pj_free = [sem("pj_free0"), sem("pj_free1")]
        kw_cp = sem("kw_cp")
        k_mean = sem("k_mean")
        k_dev = sem("k_dev")
        k_sq = sem("k_sq")
        k_var = sem("k_var")
        k_sd = sem("k_sd")
        k_nrm = sem("k_nrm")
        k_ln = sem("k_ln")
        ki_done = sem("ki_done")
        w_tp = sem("w_tp")
        w_nat_s = sem("w_nat_s")
        c_sq_s = sem("c_sq_s")
        c_var = sem("c_var")
        c_sd = sem("c_sd")
        c_done = sem("c_done")
        c_st = sem("c_st")
        st_hi = sem("st_hi")
        ix_mm = sem("ix_mm")
        ix_relu = sem("ix_relu")
        ix_acc = sem("ix_acc")
        sp_exp = sem("sp_exp")
        sp_in = sem("sp_in")
        dec_s = sem("dec_s")
        gw_in = sem("gw_in")
        xc0 = sem("xc0")
        gates_mm = sem("gates_mm")
        r_sig = sem("r_sig")
        i_sig = sem("i_sig")
        g_sig = sem("g_sig")
        a_sq = sem("a_sq")
        one_m = sem("one_m")
        root = sem("root")
        y_lru = sem("y_lru_s")
        y_st = sem("y_st")
        d_sig = sem("d_sig")
        q_st = sem("q_st")
        gate_st = sem("gate_st")
        mask_s = sem("mask_s")
        c_ld = sem("c_ld")
        kv_ld = [sem("kv_ld0"), sem("kv_ld1")]
        qb_ld = [sem("qb_ld0"), sem("qb_ld1")]
        gate_ld = [sem("gate_ld0"), sem("gate_ld1")]
        yl_ld = sem("yl_ld")
        yl_hi = sem("yl_hi")
        yl_lo = sem("yl_lo")
        kv_mm_s = sem("kv_mm")
        ro_mm = sem("ro_mm")
        kv_cp = sem("kv_cp")
        o_used = sem("o_used")
        lg_mm = sem("lg_mm")
        lg_used = sem("lg_used")
        p_exp = sem("p_exp")
        p_norm = sem("p_norm")
        p_tp = sem("p_tp")
        p_cp = sem("p_cp")
        y_att = sem("y_att")
        wo_in = [sem(f"wo_in{i}") for i in range(4)]
        wo_hi_s = sem("wo_hi_s")
        wo_lo_s = sem("wo_lo_s")
        wo_used = sem("wo_used")
        gf_in = sem("gf_in")
        res_in = sem("res_in")
        o_mm = sem("o_mm")
        o_add = sem("o_add")
        o_sq = sem("o_sq")
        f_tot = sem("f_tot")
        f_sd = sem("f_sd")
        f_out = sem("f_out")
        out_st = [sem(f"out_st{q}") for q in range(HALF_T)]
        act_step = sem("act_step")
        dve_step = sem("dve_step")
        pool_step = sem("pool_step")

        def cols(t0, step=0, i=0):
            return ds(t0 + step * i, P)

        def w_rows(c0, n):
            v = w_in.rearrange("(j k p) e -> j p k e", j=PIECES, p=P)
            return [v[j, :, :, ds(c0, n)] for j in range(PIECES)]

        block = ctx.enter_context(nc.Block())

        @block.sync
        def _(sp):
            def weights(t, c0, n=P):
                for j, src in enumerate(w_rows(c0, n)):
                    sp.wait_ge(w_lo_s, 4 * t + j + 1)
                    sp.dma_start(w_raw[:, j, :, 0:n], src).then_inc(w_in_s[j], 16)

            def x_load(i):
                sp.dma_start(xin[:, i, :], x[i * P:(i + 1) * P, :]).then_inc(x_in[i], 16)

            x_load(0)
            sp.dma_start(g_bc[:, :], a["norm_g"].broadcast_to([P, D])).then_inc(g_in, 16)
            x_load(1)
            sp.dma_start(rel[:, :], a["rel_bias"]).then_inc(bias_in, 16)
            sp.dma_start(onehot[:, :], a["onehot"]).then_inc(bias_in, 16)
            for i in range(2, XB):
                x_load(i)
            sp.wait_ge(rows_clear, 1)
            rows = 0
            for name, n, m in [("conv_w", CONV * G, P), ("conv_b", G, P), ("lru_ba", G, P), ("lru_bx", G, P),
                               ("lru_lambda", G, P), ("ckv_norm_g", CT, P), ("idx_k_norm_g", 1, ID),
                               ("idx_k_norm_b", 1, ID)]:
                v = a[name][0]
                src = v.rearrange("j (g p) -> (j g) p", p=P) if len(v.shape) == 2 else v.rearrange("(g p) -> g p", p=m)
                sp.dma_start(par_rows[rows:rows + n, 0:m], src).then_inc(small_in, 16)
                rows += n
            weights(T_KW, COL_KI, KW)
            sp.wait_ge(bias_cp, 1)
            sp.wait_ge(x_norm, QB - 1)
            sp.dma_start(bias_d.rearrange("h (p m) -> h p m", p=P),
                         bias_sb[:, :].rearrange("h (o m) -> h o m", o=1).broadcast_to([NH, P, BR])).then_inc(bias_st, 16)
            weights(T_C, COL_CKV)
            weights(T_C + 1, COL_CKV + P)
            weights(T_QI, COL_QI)
            weights(T_QI + 1, COL_QI + P)
            weights(T_QI + 2, COL_QI + 2 * P)
            sp.wait_ge(c_done, 4 * CT)
            for t in range(CT):
                sp.dma_start(c_d[t], c_sb[:, t, :]).then_inc(c_st, 16)
            with sp.Fori(0, 5) as i:
                weights(T_QI + 3 + i, COL_QI + 3 * P + i * P)
            def lru_loads(g):
                weights(T_LRU + 2 * g, COL_XA + g * P)
                weights(T_LRU + 1 + 2 * g, COL_GA + g * P)

            def gate_loads(g):
                sp.wait_ge(gates_mm, g + 1)
                sp.dma_start(w_gates[:, 0, :], a["lru_wa"][0, ds(g, 1)].rearrange("o i j -> (o i) j")
                             ).then_inc(gw_in, 16)
                sp.dma_start(w_gates[:, 1, :], a["lru_wx"][0, ds(g, 1)].rearrange("o i j -> (o i) j")
                             ).then_inc(gw_in, 16)

            lru_loads(0)
            sp.wait_ge(ix_acc, 8 + 8 * UNITS)
            gate_loads(0)
            with sp.Fori(1, G) as g:
                lru_loads(g)
                sp.wait_ge(y_lru, g + 1)
                sp.dma_start(yl_d[ds(g - 1, 1)].rearrange("o p s -> (o p) s"), sg[:, :]).then_inc(y_st, 16)
                gate_loads(g)
            def att_loads(h):
                weights(T_ATT + 2 * h, COL_Q + h * P)
                weights(T_ATT + 1 + 2 * h, COL_GB + h * P)

            def att_stores(h):
                sp.wait_ge(pj_free[1], h + T_ATT // 2 + 2)
                sp.dma_start(q_d[ds(h, 1)].rearrange("o p s -> (o p) s"), av[:, :]).then_inc(q_st, 16)
                sp.wait_ge(pj_free[0], h + (T_ATT + 1) // 2 + 2)
                sp.dma_start(gate_d[ds(h, 1)].rearrange("o p s -> (o p) s"), rg[:, :]).then_inc(gate_st, 16)

            att_loads(0)
            sp.wait_ge(y_lru, G + 1)
            sp.dma_start(yl_d[G - 1], sg[:, :]).then_inc(y_st, 16)
            sp.dma_start(wuk[:, :, :], a["w_uk"][0].rearrange("h d c -> d h c")).then_inc(wuk_in, 16)
            att_loads(1)
            att_stores(0)
            for k in range(2):
                sp.wait_ge(wuk_cp, k + 1)
                sp.dma_start(wk_d[k * NH // 2:(k + 1) * NH // 2].rearrange("h c t d -> c h t d"),
                             wuk_t[k][:, :, :].rearrange("c (h t) d -> c h t d", t=CT)).then_inc(wuk_st, 16)
            with sp.Fori(2, NH) as h:
                att_loads(h)
                att_stores(h - 1)

            def kv_loads(h, p):
                sp.dma_start(wk[p][:, :, :], wk_d[ds(h, 1)].rearrange("o p t d -> (o p) t d")).then_inc(kv_ld[p], 16)
                sp.dma_start(wv[p][:, :, :], a["w_uv"][0, ds(h, 1)].rearrange("o (t p) d -> (o p) t d", p=P)
                             ).then_inc(kv_ld[p], 16)

            def qb_loads(h, p):
                sp.dma_start(qT[p][:, :], q_d[ds(h, 1)].rearrange("o p s -> (o p) s")).then_inc(qb_ld[p], 16)
                src = bias_d[ds(h, 1), P - 1:P - 1 + P * (BR - 1)].rearrange("o (p m) -> (o p) m", p=P)[:, 0:2 * P]
                sp.dma_start(tb[p][:, :], src).then_inc(qb_ld[p], 16)

            def tail_loads(h):
                for k in range(2):
                    sp.wait_ge(yl_lo, 2 * h + k + 1)
                    sp.dma_start(yl_raw[:, :], yl_d[ds(h, 1), :, k * NT:(k + 1) * NT].rearrange(
                        "o p s -> (o p) s")).then_inc(yl_ld, 16)

            def head_loads(h, p):
                sp.wait_ge(kv_mm_s, 4 * h - 4)
                kv_loads(h, p)
                sp.wait_ge(lg_used, 8 * h - 8)
                qb_loads(h, p)
                tail_loads(h - 1)

            sp.wait_ge(c_st, 16 * CT)
            sp.wait_ge(w_lo_s, 4 * TILES + 4)
            sp.dma_start(c_t[:, :, :], c_d.rearrange("t p s -> p t s")).then_inc(c_ld, 16)
            sp.wait_ge(wuk_st, 32)
            kv_loads(0, 0)
            sp.wait_ge(bias_st, 16)
            sp.wait_ge(q_st, 32)
            qb_loads(0, 0)
            kv_loads(1, 1)
            att_stores(NH - 1)
            sp.wait_ge(mask_s, 1)
            sp.wait_ge(y_st, 16 * (G + 1))
            sp.wait_ge(q_st, 16 * (NH + 1))
            qb_loads(1, 1)
            tail_loads(0)
            with sp.Fori(1, NH // 2) as i:
                head_loads(i * 2, 0)
                head_loads(i * 2 + 1, 1)
            v_out = w_out.rearrange("(j k p) e -> j p k e", j=OP, p=P)

            def out_weights(cg, chunk, js=range(OP)):
                for j in js:
                    sp.wait_ge(wo_lo_s, 8 * cg + j + 1)
                    sp.dma_start(wo_raw[:, j % 4, :, :], v_out[j, :, :, ds(chunk * OC, OC)]
                                 ).then_inc(wo_in[j % 4], 16)

            sp.wait_ge(kv_mm_s, 4 * NH)
            out_weights(0, 0, range(2))
            sp.wait_ge(lg_used, 8 * (NH - 1))
            out_weights(0, 0, [2])
            tail_loads(NH - 1)
            sp.wait_ge(lg_used, 8 * NH)
            out_weights(0, 0, [3])
            sp.wait_ge(y_att, 4 * NH + 1)

            def token_rows(th, q):
                return slice((th * HALF_T + q) * P, (th * HALF_T + q + 1) * P)

            def residual(th, q):
                sp.dma_start(res[q], x[token_rows(th, q), :]).then_inc(res_in, 16)

            def stores(th):
                for q in range(HALF_T):
                    sp.wait_ge(f_out, HALF_T * th + q + 1)
                    sp.dma_start(out[0, token_rows(th, q), :], res[q]).then_inc(out_st[q], 16)

            for q in range(HALF_T):
                residual(0, q)
            sp.dma_start(gf_bc[:, :], a["final_norm_g"].rearrange("(o d) -> o d", o=1).broadcast_to([P, D])
                         ).then_inc(gf_in, 16)
            out_weights(0, 0, range(4, OP))
            with sp.Fori(1, OCH) as c:
                out_weights(c, c)
            out_weights(OCH, 0)
            stores(0)
            for q in range(HALF_T):
                sp.wait_ge(out_st[q], 16)
                residual(1, q)
                if q == 1:
                    out_weights(OCH + 1, 1, range(2))
            out_weights(OCH + 1, 1, range(2, OP))
            with sp.Fori(2, OCH) as c:
                out_weights(c + OCH, c)
            stores(1)
            for q in range(HALF_T):
                sp.wait_ge(out_st[q], 32)

        @block.gpsimd
        def _(pool):
            nc.gpsimd.sem_inc(w_lo_s, PIECES)
            nc.gpsimd.sem_inc(wo_lo_s, 4)
            step = Tally(pool_step)
            nc.gpsimd.memset(ident[:, :], 0.0).then_inc(pool_step, 1)
            nc.gpsimd.memset(causal[:, :], 0.0).then_inc(pool_step, 1)
            pool.wait_ge(pool_step, 2)
            nc.gpsimd.affine_select(out=ident[:, :], in_=ident[:, :], compare_op=ALU.not_equal, fill=1.0,
                                    base=0, pattern=[[-1, P]], channel_multiplier=1).then_inc(id_made, 1)
            nc.gpsimd.affine_select(out=causal[:, :], in_=causal[:, :], compare_op=ALU.is_ge, fill=NEG,
                                    base=0, pattern=[[-1, P]], channel_multiplier=1).then_inc(consts, 1)
            for i in range(QB - XB):
                pool.wait_ge(x_tp, 2 * i + 2)
                pool.dma_start(xin[:, i, :], x[(i + XB) * P:(i + XB + 1) * P, :]).then_inc(x_rest[i], 16)

            def low(t, n=P):
                for j in range(PIECES):
                    pool.wait_ge(w_hi_s, 4 * t + j + 1)
                    nc.gpsimd.tensor_tensor(w_lo[:, j, :, 0:n], w_raw[:, j, :, 0:n],
                                            w_hi[:, j, :, 0:n].bitcast(F32), ALU.subtract).then_inc(w_lo_s, 1)

            low(T_KW, KW)
            with pool.Fori(1, TILES) as t:
                low(t)
            pool.wait_ge(gate_st, 16 * (NH + 1))
            pool.wait_ge(wuk_st, 32)
            with pool.Fori(0, NH) as h:
                for r in range(4):
                    pool.wait_ge(o_used, 4 * h + r + 3)
                    pool.dma_start(gate[:, r % 2, :], gate_d[ds(h, 1), :, 2 * r * P:2 * (r + 1) * P].rearrange(
                        "o p s -> (o p) s")).then_inc(gate_ld[r % 2], 16)
            pool.wait_ge(p_tp, 8 * NH + 3)
            with pool.Fori(0, 2 * OCH) as c:
                for j in range(OP):
                    pool.wait_ge(wo_hi_s, 8 * c + j + 1)
                    nc.gpsimd.tensor_tensor(wo_lo[:, j % 2, :, :], wo_raw[:, j % 4, :, :],
                                            wo_hi[:, j % 2, :, :].bitcast(F32), ALU.subtract).then_inc(wo_lo_s, 1)

        @block.scalar
        def _(act):
            nc.scalar.sem_inc(ix_relu, 2)
            nc.scalar.sem_inc(pj_free[0], 1)
            nc.scalar.sem_inc(pj_free[1], 1)
            nc.scalar.sem_inc(p_cp, 4)
            nc.scalar.sem_inc(o_sq, 1)
            nc.scalar.sem_inc(i_sig, 1)
            nc.scalar.sem_inc(y_st, 16)
            nc.scalar.sem_inc(q_st, 16)
            nc.scalar.sem_inc(gate_st, 16)
            step = Tally(act_step)
            done = lambda t: 4 * t + 8

            def square(i):
                act.wait_ge(x_in[i] if i < XB else x_rest[i - XB], 16)
                step.did(nc.scalar.activation(junk[:, :], xin[:, i % XB, :], ACT.Square,
                                              accum_out=stat[:, i % XB:i % XB + 1]))

            def root_x(i):
                act.wait_ge(act_step, i + 2)
                nc.scalar.activation(stat[:, XB + i % XB:XB + i % XB + 1], stat[:, i % XB:i % XB + 1], ACT.Sqrt,
                                     scale=1.0 / D, bias=eps[:, :]).then_inc(x_sd, 1)

            def high_x(i):
                for j in range(2):
                    act.wait_ge(x_tp, 2 * i + j + 1)
                    nc.scalar.activation(
                        hT_hi[:, 8 * j:8 * j + 8, i * P:(i + 1) * P],
                        PS[2 * (i % 2) + j][:, :].rearrange("p (t s) -> p t s", s=P), ACT.Copy).then_inc(h_hi, 1)

            def high(t, js=range(PIECES), n=P):
                for j in js:
                    act.wait_ge(w_in_s[j], 16 * t + 16)
                    act.wait_ge(w_used, 4 * t + j + 1)
                    nc.scalar.activation(w_hi[:, j, :, 0:n], w_raw[:, j, :, 0:n], ACT.Copy).then_inc(w_hi_s, 1)

            act.wait_ge(eps_made, 1)
            s = step.did(nc.scalar.activation(junk[:, 0:1], eps[:, :], ACT.Sqrt))
            act.wait_ge(act_step, s)
            square(0)
            root_x(0)
            square(1)
            act.wait_ge(bias_mm, 1)
            nc.scalar.activation(bias_sb[:, :], X[0][0:NH, 0:BR], ACT.Copy).then_inc(bias_cp, 1)
            for i in range(QB):
                if i + 1 < QB:
                    root_x(i + 1)
                if i + 2 < QB:
                    square(i + 2)
                if i == QB - 1:
                    high(0, n=KW)
                high_x(i)

            high(1)
            act.wait_ge(small_tp, 1)
            nc.scalar.activation(par_t[:, :], X[1][:, 0:PARS], ACT.Copy).then_inc(small_cp, 1)
            act.wait_ge(bias_st, 16)
            act.wait_ge(w_used, done(0))
            nc.scalar.activation(kw_sb[:, :], PJ[0][0:KW, :], ACT.Copy).then_inc(pj_free[0], 1)
            high(2)
            act.wait_ge(w_used, done(1))
            nc.scalar.activation(c_sb[:, 0, :], PJ[1][:, :], ACT.Copy).then_inc(pj_free[1], 1)
            act.wait_ge(pj_free[1], 2)
            nc.scalar.activation(c_sq[:, 0, :], c_sb[:, 0, :], ACT.Square).then_inc(c_sq_s, 1)
            act.wait_ge(k_dev, 1)
            nc.scalar.activation(k_t[:, :], kw_sb[0:ID, :], ACT.Square).then_inc(k_sq, 1)
            high(3)
            act.wait_ge(w_used, done(2))
            nc.scalar.activation(c_sb[:, 1, :], PJ[0][:, :], ACT.Copy).then_inc(pj_free[0], 1)
            act.wait_ge(pj_free[0], 3)
            nc.scalar.activation(c_sq[:, 1, :], c_sb[:, 1, :], ACT.Square).then_inc(c_sq_s, 1)
            act.wait_ge(k_var, 1)
            nc.scalar.activation(k_t[:, :], X[1][0:ID, :], ACT.Sqrt, bias=eps[0:ID, :]).then_inc(k_sd, 1)
            act.wait_ge(k_nrm, 1)
            nc.scalar.activation(k_t[:, :], kw_sb[0:ID, :], ACT.Identity, scale=k_gb[:, 0:1],
                                 bias=k_gb[:, 1:2]).then_inc(k_ln, 1)
            act.wait_ge(k_ln, 1)
            nc.scalar.activation(ki_hi[0:ID, :], k_t[:, :], ACT.Copy).then_inc(k_ln, 1)
            nc.scalar.activation(ki_hi[ID:P, :], k_t[:, :], ACT.Copy).then_inc(k_ln, 1)
            high(4)
            act.wait_ge(sp_in, 1)
            nc.scalar.activation(sp_t[:, 1, :], sp_t[:, 0, :], ACT.Exp).then_inc(sp_exp, 1)
            act.wait_ge(c_var, 1)
            nc.scalar.activation(c_rs[:, :], X[1][:, :], ACT.Sqrt, bias=eps[:, :]).then_inc(c_sd, 1)
            act.wait_ge(ki_done, 2)
            act.wait_ge(w_tp, 1)

            def stacks(t, par):
                act.wait_ge(w_used, done(t))
                act.wait_ge(ix_mm, t * UNITS - UNITS * (T_QI - 1))
                nc.scalar.activation(stack_a[par][0:ID, :], PJ[par][0:ID, :], ACT.Copy).then_inc(st_hi, 1)
                nc.scalar.activation(stack_b[par][ID:P, :], PJ[par][ID:P, :], ACT.Copy).then_inc(st_hi, 1)

            def relus(t, ms):
                for m in ms:
                    q = FIRST_SCORED + m % (UNITS // 2)
                    w = (q + 1) * P
                    k = t * UNITS + (m - UNITS * T_QI)
                    act.wait_ge(ix_mm, k + 1 + 2 * UNITS)
                    act.wait_ge(ix_acc, k + 7)
                    nc.scalar.activation(relu[m % 2][:, 0:w], X[m % 2][:, 0:w], ACT.Relu).then_inc(ix_relu, 1)

            def act_b(t, par):
                stacks(t - 1, 1 - par)
                for j in range(PIECES):
                    high(t + 1, [j])
                    relus(t - 1, range(min(4 * j, UNITS), min(4 * j + 4, UNITS)))

            act_b(T_QI + 1, 0)
            act.wait_ge(c_st, 16 * CT)
            with act.Fori(0, 3) as i:
                act_b(i * 2 + (T_QI + 2), 1)
                act_b(i * 2 + (T_QI + 3), 0)
            act_b(T_LRU, 1)

            act.wait_ge(ix_acc, 8 + 8 * UNITS)
            act.wait_ge(dec_s, 1)

            def lru(g, first=False):
                par = lambda k: lru_p[:, k, ds(g, 1)]
                if not first:
                    high(g * 2 + (T_LRU + 1))
                act.wait_ge(w_used, g * 8 + done(T_LRU))
                act.wait_ge(y_lru, g + 1)
                nc.scalar.activation(xc[:, :], PJ[1][:, :], ACT.Identity, scale=conv_w[:, CONV - 1, ds(g, 1)],
                                     bias=par(0)).then_inc(xc0, 1)
                high(g * 2 + (T_LRU + 2))
                act.wait_ge(gates_mm, g + 2)
                nc.scalar.activation(rg[:, :], X[0][:, :], ACT.Sigmoid, bias=par(1)).then_inc(r_sig, 1)
                nc.scalar.activation(ig[:, :], X[1][:, :], ACT.Sigmoid, bias=par(2)).then_inc(i_sig, 1)
                act.wait_ge(y_st, 16 * g + 16)
                nc.scalar.activation(sg[:, :], PJ[0][:, :], ACT.Sigmoid).then_inc(g_sig, 1)
                act.wait_ge(r_sig, g + 1)
                nc.scalar.activation(th[:, :], rg[:, :], ACT.Tanh, scale=decay[:, 0, ds(g, 1)])
                s = step.did(nc.scalar.activation(av[:, :], rg[:, :], ACT.Exp, scale=decay[:, 1, ds(g, 1)]))
                act.wait_ge(act_step, s)
                nc.scalar.activation(rg[:, :], av[:, :], ACT.Square).then_inc(a_sq, 1)
                act.wait_ge(one_m, g + 1)
                nc.scalar.activation(th[:, :], th[:, :], ACT.Sqrt).then_inc(root, 1)

            lru(0, first=True)
            with act.Fori(1, G) as g:
                step.enter(g - 1, 1)
                lru(g)
                step.leave(G - 1)

            act.wait_ge(y_lru, G + 1)

            def att(h, last):
                high(h * 2 + (T_ATT + 1))
                act.wait_ge(w_used, h * 8 + done(T_ATT))
                act.wait_ge(q_st, h * 16 + 16)
                nc.scalar.activation(av[:, :], PJ[1][:, :], ACT.Copy, scale=-HD ** -0.5).then_inc(pj_free[1], 1)
                if not last:
                    high(h * 2 + (T_ATT + 2))
                act.wait_ge(w_used, h * 8 + done(T_ATT + 1))
                act.wait_ge(pj_free[0], h + (T_ATT + 1) // 2 + 1)
                nc.scalar.activation(ig[:, :], PJ[0][:, :], ACT.Sigmoid).then_inc(d_sig, 1)

            att(0, False)
            for k in range(2):
                if k == 0:
                    act.wait_ge(y_st, 16 * (G + 1))
                act.wait_ge(wuk_tp, k + 1)
                nc.scalar.activation(wuk_t[k][:, :, :], X[k][:, :].rearrange("p (t d) -> p t d", d=HD), ACT.Copy
                                     ).then_inc(wuk_cp, 1)
            with act.Fori(1, NH - 1) as h:
                att(h, False)
            att(NH - 1, True)

            def kv(h, p, part):
                for k in range(2):
                    act.wait_ge(kv_mm_s, 4 * h + 2 * part + k + 1)
                    src = X[1][:, k * NT:(k + 1) * NT]
                    if part == 0:
                        dst = kT[p][:, k * NT:(k + 1) * NT]
                    else:
                        dst, src = vN[p][:, 4 * k:4 * k + 4, :], src.rearrange("p (t d) -> p t d", d=HD)
                    nc.scalar.activation(dst, src, ACT.Copy).then_inc(kv_cp, 1)

            def softexp(h, q):
                act.wait_ge(lg_used, 8 * h + q + 1)
                nc.scalar.activation(prob[q], prob[q], ACT.Exp, scale=-1.0,
                                     bias=sums[:, q, 0:1], accum_out=sums[:, q, 1:2]).then_inc(p_exp, 1)

            def p_copy(h, q):
                act.wait_ge(p_tp, 8 * h + q + 4)
                if q % 2 == 0:
                    act.wait_ge(ro_mm, 4 * h + q // 2 + 3)
                nc.scalar.activation(pT[(q // 2) % 2][:, 0:q + 1, (q % 2) * P:(q % 2) * P + P],
                                     LG[q][:, 0:(q + 1) * P].rearrange("p (t s) -> p t s", s=P),
                                     ACT.Copy).then_inc(p_cp, 1)

            def act_head(h, p, last=False):
                for q in range(QB):
                    p_copy(h, q)
                    if q + 2 < QB:
                        softexp(h, q + 2)
                    elif not last:
                        softexp(h + 1, q + 2 - QB)
                    if q == 0 and not last:
                        kv(h + 1, 1 - p, 0)
                    if q == 1 and not last:
                        kv(h + 1, 1 - p, 1)
                    if q in (2, 5):
                        k = q // 5
                        act.wait_ge(yl_ld, 32 * h + 16 * k + 16)
                        nc.scalar.activation(hT_hi[:, ds(h, 1), k * NT:(k + 1) * NT],
                                             yl_raw[:, :].rearrange("p (o s) -> p o s", o=1), ACT.Copy
                                             ).then_inc(yl_hi, 1)

            kv(0, 0, 0)
            kv(0, 0, 1)
            softexp(0, 0)
            softexp(0, 1)
            act.wait_ge(q_st, 16 * (NH + 1))
            act.wait_ge(gate_st, 16 * (NH + 1))
            with act.Fori(0, 3) as i:
                act_head(i * 2, 0)
                act_head(i * 2 + 1, 1)
            act_head(6, 0)
            act_head(7, 1, last=True)

            def out_high(cg, js):
                for j in js:
                    act.wait_ge(wo_in[j % 4], 32 * cg + 16 * (j // 4) + 16)
                    act.wait_ge(wo_used, 8 * cg + j + 1)
                    nc.scalar.activation(wo_hi[:, j % 2, :, :], wo_raw[:, j % 4, :, :], ACT.Copy
                                         ).then_inc(wo_hi_s, 1)

            def squares(cg, c, half=None):
                for q in range(HALF_T):
                    act.wait_ge(o_add, 4 * cg + q + 9)
                    act.wait_ge(o_sq, 4 * cg + q + 1)
                    nc.scalar.activation(junk4[:, :], res[q][:, ds(c * OC, OC)], ACT.Square,
                                         accum_out=ssq[:, q, ds(c, 1)]).then_inc(o_sq, 1)
                    if half == 1 and q > 0:
                        root_mean(q - 1, 1)
                if half == 0:
                    root_mean(0, HALF_T)
                if half == 1:
                    root_mean(HALF_T - 1, 1)

            def root_mean(q, n):
                act.wait_ge(f_tot, 1 if n > 1 else q + 2)
                nc.scalar.activation(fstat[:, 1, q:q + n], fstat[:, 0, q:q + n], ACT.Sqrt, scale=1.0 / D,
                                     bias=eps[:, :]).then_inc(f_sd, 1)

            out_high(0, range(2))
            for half in range(2):
                with act.Fori(0, OCH - 1) as c:
                    out_high(c + OCH * half, range(2, OP))
                    out_high(c + (OCH * half + 1), range(2))
                    squares(c + OCH * half, c)
                out_high(OCH * half + OCH - 1, range(2, OP))
                if half == 0:
                    out_high(OCH, range(2))
                squares(OCH * half + OCH - 1, OCH - 1, half)

        @block.tensor
        def _(pe):
            nc.tensor.sem_inc(w_used, PIECES)
            nc.tensor.sem_inc(wo_used, 2)
            nc.tensor.sem_inc(ix_mm, 2 * UNITS)
            nc.tensor.sem_inc(gates_mm, 1)
            nc.tensor.sem_inc(p_tp, 3)
            nc.tensor.sem_inc(ro_mm, 4)
            pe.wait_ge(bias_in, 32)
            nc.tensor.matmul(X[0][0:NH, 0:BR], rel[:, :], onehot[:, :], start=True, stop=True).then_inc(bias_mm, 1)
            pe.wait_ge(id_made, 1)
            pe.wait_ge(bias_cp, 1)
            with pe.Fori(0, QB // XB) as k:
                for u in range(XB):
                    pe.wait_ge(x_norm, k * XB + u + 1)
                    for j in range(2):
                        pe.wait_ge(h_lo, k * (2 * XB) + 2 * u + j + 1)
                        for n in range(8):
                            last = nc.tensor.transpose(PS[2 * (u % 2) + j][:, n * P:(n + 1) * P],
                                                       xin[:, u, (8 * j + n) * P:(8 * j + n + 1) * P], ident[:, :])
                        last.then_inc(x_tp, 1)
            pe.wait_ge(h_lo, 4 + 2 * QB)
            def project_tile(t, par, turn, m=P, between=None):
                pe.wait_ge(pj_free[par], turn + 1)
                for j in range(PIECES):
                    pe.wait_ge(w_lo_s, 4 * t + j + 1 + PIECES)
                    for k in range(PK):
                        kt = j * PK + k
                        for n in range(2):
                            o = PJ[par][0:m, n * NT:(n + 1) * NT]
                            hi, lo = hT_hi[:, kt, n * NT:(n + 1) * NT], hT_lo[:, kt, n * NT:(n + 1) * NT]
                            whi, wlo = w_hi[:, j, k, 0:m], w_lo[:, j, k, 0:m]
                            end = kt == KT - 1
                            nc.tensor.matmul(o, wlo, hi, start=(kt == 0), stop=False)
                            nc.tensor.matmul(o, whi, lo, start=False, stop=False)
                            last = nc.tensor.matmul(o, whi, hi, start=False, stop=end)
                        if k == PK - 1:
                            last.then_inc(w_used, 1)
                        if between:
                            between(kt)

            project_tile(0, 0, 0, m=KW)
            pe.wait_ge(small_in, 16 * 8)
            nc.tensor.transpose(X[1][:, 0:PARS], par_rows[:, :], ident[0:PARS, 0:PARS]).then_inc(small_tp, 1)
            project_tile(1, 1, 0)
            pe.wait_ge(small_cp, 1)
            pe.wait_ge(pj_free[0], 2)
            pe.wait_ge(ones_made, 1)
            for n in range(2):
                last = nc.tensor.matmul(X[0][0:ID, n * NT:(n + 1) * NT], ones_k[:, :],
                                        kw_sb[0:ID, n * NT:(n + 1) * NT], start=True, stop=True)
            last.then_inc(k_mean, 1)
            project_tile(2, 0, 1)
            pe.wait_ge(k_sq, 1)
            for n in range(2):
                last = nc.tensor.matmul(X[1][0:ID, n * NT:(n + 1) * NT], ones_k[:, :],
                                        k_t[:, n * NT:(n + 1) * NT], start=True, stop=True)
            last.then_inc(k_var, 1)
            for q in range(QB):
                last = nc.tensor.transpose(X[0][:, q * IH:(q + 1) * IH], kw_sb[ID:KW, q * P:(q + 1) * P],
                                           ident[ID:KW, ID:KW])
            last.then_inc(w_tp, 1)
            project_tile(3, 1, 1)
            pe.wait_ge(c_sq_s, 2)
            pe.wait_ge(k_sd, 1)
            for n in range(2):
                for t in range(CT):
                    last = nc.tensor.matmul(X[1][:, n * NT:(n + 1) * NT], ones_c[:, :],
                                            c_sq[:, t, n * NT:(n + 1) * NT], start=(t == 0), stop=(t == CT - 1))
            last.then_inc(c_var, 1)


            def score(t, par, turn, ms, first=False):
                for m in ms:
                    q = FIRST_SCORED + m % (UNITS // 2)
                    w = (q + 1) * P
                    k = t * UNITS + (m - UNITS * T_QI)
                    if m == 0:
                        pe.wait_ge(pj_free[par], turn + 2)
                    if m == 0 and first:
                        pe.wait_ge(ki_done, 2)
                        pe.wait_ge(c_sd, 1)
                        pe.wait_ge(w_nat_s, 1)
                    pe.wait_ge(ix_relu, k + 1)
                    st = (stack_a, stack_b)[m // (UNITS // 2)][par]
                    for n in range(0, w, NT):
                        e = min(n + NT, w)
                        nc.tensor.matmul(X[m % 2][:, n:e], st[:, q * P:(q + 1) * P], ki_lo[:, n:e],
                                         start=True, stop=False)
                        last = nc.tensor.matmul(X[m % 2][:, n:e], st[:, q * P:(q + 1) * P], ki_hi[:, n:e],
                                                start=False, stop=True)
                    last.then_inc(ix_mm, 1)

            def step_b(t, par, turn, first=False):
                before = turn - 1 + par
                project_tile(t, par, turn, between=lambda kt: score(
                    t - 1, 1 - par, before, range(kt - 3, kt - 2) if 3 <= kt < UNITS + 3 else [], first))

            step_b(T_QI + 1, 0, 2, first=True)
            with pe.Fori(0, 3) as i:
                step_b(i * 2 + (T_QI + 2), 1, i + 2)
                step_b(i * 2 + (T_QI + 3), 0, i + 3)
            step_b(T_LRU, 1, T_LRU // 2)

            def lru(g, first=False):
                if not first:
                    project_tile(g * 2 + T_LRU, 1, g + T_LRU // 2)
                project_tile(g * 2 + (T_LRU + 1), 0, g + (T_LRU + 1) // 2)
                pe.wait_ge(pj_free[1], g + T_LRU // 2 + 2)
                pe.wait_ge(gw_in, g * 32 + 32)
                pe.wait_ge(i_sig, g + 1)
                for k in range(2):
                    for n in range(2):
                        last = nc.tensor.matmul(X[k][:, n * NT:(n + 1) * NT], w_gates[:, k, :],
                                                xc[:, n * NT:(n + 1) * NT], start=True, stop=True)
                last.then_inc(gates_mm, 1)

            lru(0, first=True)
            with pe.Fori(1, G) as g:
                lru(g)

            project_tile(T_ATT, 1, T_ATT // 2)
            project_tile(T_ATT + 1, 0, (T_ATT + 1) // 2)
            pe.wait_ge(wuk_in, 16)
            pe.wait_ge(i_sig, G + 1)
            for k in range(2):
                for n in range(8):
                    h, t = (8 * k + n) // CT, n % CT
                    last = nc.tensor.transpose(X[k][:, n * P:(n + 1) * P], wuk[:, h, t * P:(t + 1) * P], ident[:, :])
                last.then_inc(wuk_tp, 1)
            with pe.Fori(1, NH) as h:
                project_tile(h * 2 + T_ATT, 1, h + T_ATT // 2)
                project_tile(h * 2 + (T_ATT + 1), 0, h + (T_ATT + 1) // 2)

            def kv_mm(h, p, part, turn):
                if part == 0:
                    pe.wait_ge(kv_ld[p], turn * 32 + 32)
                for k in range(2):
                    if part == 0:
                        pe.wait_ge(o_used, 4 * h - 1 + k)
                    else:
                        pe.wait_ge(kv_cp, 4 * h + k + 1)
                    o = X[1][:, k * NT:(k + 1) * NT]
                    if part == 0:
                        for t in range(CT):
                            last = nc.tensor.matmul(o, wk[p][:, t, :], c_t[:, t, k * NT:(k + 1) * NT],
                                                    start=(t == 0), stop=(t == CT - 1))
                    else:
                        for s in range(4):
                            for t in range(CT):
                                last = nc.tensor.matmul(o[:, s * HD:(s + 1) * HD],
                                                        c_t[:, t, (4 * k + s) * P:(4 * k + s + 1) * P], wv[p][:, t, :],
                                                        start=(t == 0), stop=(t == CT - 1))
                    last.then_inc(kv_mm_s, 1)

            def logits(h, q, p, turn):
                w = (q + 1) * P
                if q == 0:
                    pe.wait_ge(qb_ld[p], turn * 32 + 32)
                    pe.wait_ge(kv_cp, 4 * h + 2)
                pe.wait_ge(p_cp, 8 * h + q + 5 - LAST[q])
                for n in range(0, w, NT):
                    e = min(n + NT, w)
                    last = nc.tensor.matmul(LG[q][:, n:e], qT[p][:, q * P:(q + 1) * P], kT[p][:, n:e],
                                            start=True, stop=True)
                last.then_inc(lg_mm, 1)

            def turn_p(h, q):
                pe.wait_ge(p_norm, 8 * h + q + 1)
                for t in range(q + 1):
                    last = nc.tensor.transpose(LG[q][:, t * P:(t + 1) * P], prob[q][:, t * P:(t + 1) * P],
                                               ident[:, :])
                last.then_inc(p_tp, 1)

            def read_out(h, pr, p, last_head):
                pe.wait_ge(p_cp, 8 * h + 2 * pr + 6)
                if pr == 0:
                    pe.wait_ge(kv_cp, 4 * h + 4)
                if pr < 2 and not last_head:
                    pe.wait_ge(kv_cp, 4 * h + pr + 7)
                else:
                    pe.wait_ge(o_used, 4 * h + pr + 3)
                k = pr % 2
                for t in range(2 * pr + 2):
                    c0 = P if t == 2 * pr + 1 else 0
                    last = nc.tensor.matmul(X[1][:, k * NT + c0:k * NT + 2 * P], vN[p][:, t, :],
                                            pT[k][:, t, c0:2 * P], start=(t == 0), stop=(t == 2 * pr + 1))
                last.then_inc(ro_mm, 1)

            def pe_head(h, p, turn_next, last=False):
                for q in range(QB):
                    if q > 0:
                        turn_p(h, q)
                    if q in (3, 4, 6):
                        read_out(h, {3: 0, 4: 1, 6: 2}[q], p, last)
                    if 0 < q < QB - AHEAD:
                        logits(h, q + AHEAD, p, None)
                    elif q == 6 and not last:
                        logits(h + 1, 0, 1 - p, turn_next)
                        logits(h + 1, 1, 1 - p, turn_next)
                    elif q == 7 and not last:
                        logits(h + 1, 2, 1 - p, turn_next)
                        turn_p(h + 1, 0)
                        logits(h + 1, 3, 1 - p, turn_next)
                    if q < 2 and not last:
                        kv_mm(h + 1, 1 - p, q, turn_next)
                read_out(h, 3, p, last)

            pe.wait_ge(c_ld, 16)
            pe.wait_ge(wuk_cp, 2)
            pe.wait_ge(kv_ld[0], 32)
            for k in range(2):
                for t in range(CT):
                    last = nc.tensor.matmul(X[1][:, k * NT:(k + 1) * NT], wk[0][:, t, :],
                                            c_t[:, t, k * NT:(k + 1) * NT], start=(t == 0), stop=(t == CT - 1))
                last.then_inc(kv_mm_s, 1)
            kv_mm(0, 0, 1, 0)
            pe.wait_ge(pj_free[0], TILES // 2 + 2)
            pe.wait_ge(pj_free[1], TILES // 2 + 1)
            logits(0, 0, 0, 0)
            logits(0, 1, 0, 0)
            logits(0, 2, 0, 0)
            turn_p(0, 0)
            logits(0, 3, 0, 0)
            with pe.Fori(0, 3) as i:
                pe_head(i * 2, 0, i)
                pe_head(i * 2 + 1, 1, i + 1)
            pe_head(6, 0, 3)
            pe_head(7, 1, None, last=True)

            def banks(u, q):
                return PS[2 * u + q // 2][:, (q % 2) * NT:(q % 2) * NT + OC]

            def out_chunk(cg, th, u):
                for j in range(OP):
                    pe.wait_ge(wo_lo_s, 8 * cg + j + 5)
                    for q in range(HALF_T):
                        if j == 0:
                            pe.wait_ge(o_add, 4 * cg + q + 1)
                        tok = slice((th * HALF_T + q) * P, (th * HALF_T + q + 1) * P)
                        for k in range(OPK):
                            kt = j * OPK + k
                            o = banks(u, q)
                            nc.tensor.matmul(o, hT_lo[:, kt, tok], wo_hi[:, j % 2, k, :], start=(kt == 0), stop=False)
                            nc.tensor.matmul(o, hT_hi[:, kt, tok], wo_lo[:, j % 2, k, :], start=False, stop=False)
                            last = nc.tensor.matmul(o, hT_hi[:, kt, tok], wo_hi[:, j % 2, k, :],
                                                    start=False, stop=(kt == KT - 1))
                        if j == OP - 1 and q < HALF_T - 1:
                            last.then_inc(o_mm, 1)
                    last.then_inc(wo_used, 1)

            pe.wait_ge(y_att, 4 * NH + 1)
            pe.wait_ge(yl_lo, 1 + 2 * G)
            for th in range(2):
                with pe.Fori(0, 2) as i:
                    out_chunk(i * 2 + OCH * th, th, 0)
                    out_chunk(i * 2 + (OCH * th + 1), th, 1)

        @block.vector
        def _(dve):
            nc.vector.sem_inc(h_lo, 4)
            nc.vector.sem_inc(ix_acc, 8)
            nc.vector.sem_inc(y_lru, 1)
            nc.vector.sem_inc(o_used, 4)
            nc.vector.sem_inc(yl_lo, 1)
            nc.vector.sem_inc(y_att, 1)
            nc.vector.sem_inc(o_add, 8)
            step = Tally(dve_step)
            tt, stt = nc.vector.tensor_tensor, nc.vector.scalar_tensor_tensor

            def chain(ins):
                dve.wait_ge(dve_step, step.did(ins))

            def hold():
                nc.vector.memset(pause[:, :], 0.0)

            nc.vector.memset(eps[:, :], EPS).then_inc(eps_made, 1)
            nc.vector.memset(par_rows[:, :], 0.0).then_inc(rows_clear, 1)
            dve.wait_ge(g_in, 16)

            def norm_x(i):
                dve.wait_ge(x_sd, i + 1)
                root, inverse = (stat[:, k * XB + i % XB:k * XB + i % XB + 1] for k in (1, 2))
                chain(nc.vector.reciprocal(inverse, root))
                stt(xin[:, i % XB, :], xin[:, i % XB, :], inverse, g_bc[:, :], ALU.mult, ALU.mult
                    ).then_inc(x_norm, 1)

            def low_x(i):
                for j in range(2):
                    dve.wait_ge(h_hi, 2 * i + j + 1)
                    part = (slice(None), slice(8 * j, 8 * j + 8), slice(i * P, (i + 1) * P))
                    tt(hT_lo[part], PS[2 * (i % 2) + j][:, :].rearrange("p (t s) -> p t s", s=P),
                       hT_hi[part].bitcast(F32), ALU.subtract).then_inc(h_lo, 1)

            norm_x(0)
            for i in range(QB):
                if i + 1 < QB:
                    norm_x(i + 1)
                low_x(i)

            dve.wait_ge(x_tp, 2 * QB)
            dve.wait_ge(bias_st, 16)
            chain(nc.vector.memset(ones_k[:, :], 1.0 / ID))
            nc.vector.memset(ones_c[:, :], 1.0 / C).then_inc(ones_made, 1)
            chain(nc.vector.memset(scores[:, :], 0.0))
            dve.wait_ge(consts, 1)
            for q in range(FIRST_SCORED, QB):
                s = step.did(nc.vector.tensor_copy(scores[:, off(q) + q * P:off(q) + (q + 1) * P], causal[:, :]))
            dve.wait_ge(dve_step, s)
            dve.wait_ge(small_cp, 1)
            lam = lru_p[:, 3, :]
            chain(nc.vector.tensor_scalar(sp_t[:, 4, :], lam, -1.0, None, ALU.mult))
            chain(nc.vector.tensor_scalar(sp_t[:, 2, :], sp_t[:, 4, :], 0.0, None, ALU.max))
            tt(sp_t[:, 0, :], sp_t[:, 4, :], lam, ALU.min).then_inc(sp_in, 1)
            dve.wait_ge(k_mean, 1)
            tt(kw_sb[0:ID, :], kw_sb[0:ID, :], X[0][0:ID, :], ALU.subtract).then_inc(k_dev, 1)
            dve.wait_ge(k_sd, 1)
            chain(nc.vector.reciprocal(k_t[:, :], k_t[:, :]))
            tt(kw_sb[0:ID, :], kw_sb[0:ID, :], k_t[:, :], ALU.mult).then_inc(k_nrm, 1)
            dve.wait_ge(w_tp, 1)
            nc.vector.tensor_scalar(w_nat[:, :, :], X[0][:, 0:QB * IH].rearrange("p (q h) -> p q h", h=IH),
                                    IH ** -0.5 * ID ** -0.5, None, ALU.mult).then_inc(w_nat_s, 1)
            dve.wait_ge(k_ln, 3)
            tt(ki_lo[0:ID, :], k_t[:, :], ki_hi[0:ID, :].bitcast(F32), ALU.subtract).then_inc(ki_done, 1)
            tt(ki_lo[ID:P, :], k_t[:, :], ki_hi[0:ID, :].bitcast(F32), ALU.subtract).then_inc(ki_done, 1)
            dve.wait_ge(sp_exp, 1)
            z, s_, q_, p_ = (sp_t[:, k, :] for k in (1, 3, 4, 0))
            chain(nc.vector.tensor_scalar(s_, z, 2.0, None, ALU.add))
            chain(nc.vector.reciprocal(s_, s_))
            chain(tt(s_, s_, z, ALU.mult))
            chain(tt(q_, s_, s_, ALU.mult))
            chain(nc.vector.tensor_scalar(p_, q_, 1.0 / 13, None, ALU.mult))
            for n in (11, 9, 7, 5, 3):
                chain(stt(p_, p_, 1.0 / n, q_, ALU.add, ALU.mult))
            chain(stt(p_, p_, 1.0, s_, ALU.add, ALU.mult))
            chain(stt(p_, p_, 2.0, sp_t[:, 2, :], ALU.mult, ALU.add))
            chain(nc.vector.tensor_scalar(decay[:, 0, :], p_, 8.0, None, ALU.mult))
            nc.vector.tensor_scalar(decay[:, 1, :], p_, -8.0, None, ALU.mult).then_inc(dec_s, 1)

            def stacks(t, par):
                dve.wait_ge(st_hi, t * 2 - 2 * (T_QI - 1))
                tt(stack_a[par][ID:P, :], PJ[par][0:ID, :], stack_a[par][0:ID, :].bitcast(F32), ALU.subtract)
                tt(stack_b[par][0:ID, :], PJ[par][ID:P, :], stack_b[par][ID:P, :].bitcast(F32), ALU.subtract
                   ).then_inc(pj_free[par], 1)

            def norm_latent(j):
                tok = slice(j * S // 4, (j + 1) * S // 4)
                if j == 0:
                    dve.wait_ge(c_sd, 1)
                chain(nc.vector.reciprocal(c_rs[:, tok], c_rs[:, tok]))
                for t in range(CT):
                    stt(c_sb[:, t, tok], c_sb[:, t, tok], c_g[:, t:t + 1], c_rs[:, tok], ALU.mult, ALU.mult
                        ).then_inc(c_done, 1)

            def add_scores(t, first=False):
                for m in range(UNITS):
                    if first and m % 2 == 1 and m < 8:
                        norm_latent(m // 2)
                    q = FIRST_SCORED + m % (UNITS // 2)
                    w = (q + 1) * P
                    k = t * UNITS + (m - UNITS * T_QI)
                    dve.wait_ge(ix_relu, k + 3)
                    dve.wait_ge(ix_acc, k + 3)
                    acc = scores[:, off(q):off(q) + w]
                    head = t * 2 + (m // (UNITS // 2) - 2 * T_QI)
                    stt(acc, relu[m % 2][:, 0:w], w_nat[:, q, ds(head, 1)], acc, ALU.mult, ALU.add
                        ).then_inc(ix_acc, 1)

            def dve_b(t, par, first=False):
                stacks(t - 1, 1 - par)
                add_scores(t - 1, first)

            dve_b(T_QI + 1, 0, first=True)
            with dve.Fori(0, 3) as i:
                dve_b(i * 2 + (T_QI + 2), 1)
                dve_b(i * 2 + (T_QI + 3), 0)
            stacks(T_QI + 7, 0)
            add_scores(T_QI + 7)
            dve.wait_ge(ix_acc, 8 + 8 * UNITS)

            def top_rounds(n):
                for _ in range(n):
                    for q in range(FIRST_SCORED, QB):
                        found = step.did(nc.vector.max(top8[:, q, :], scores[:, off(q):off(q) + (q + 1) * P]))
                    dve.wait_ge(dve_step, found)
                    hold()
                    for q in range(FIRST_SCORED, QB):
                        left = scores[:, off(q):off(q) + (q + 1) * P]
                        marked = step.did(nc.vector.match_replace(left, top8[:, q, :], left, TAKEN))
                    dve.wait_ge(dve_step, marked)
                    hold()

            per = ROUNDS // (G + NH)
            with dve.Fori(0, G) as g:
                step.enter(g, 2 + 12 * per + 4)
                dve.wait_ge(xc0, g + 1)
                xa = PJ[1]
                for n in (1, 2, 3):
                    tap = stt(xc[:, n:], xa[:, 0:S - n], conv_w[:, CONV - 1 - n, ds(g, 1)], xc[:, n:],
                              ALU.mult, ALU.add)
                    if n < 3:
                        chain(tap)
                    else:
                        tap.then_inc(pj_free[1], 1)
                top_rounds(per)
                dve.wait_ge(a_sq, g + 1)
                stt(th[:, :], rg[:, :], 1.0, th[:, :], ALU.add, ALU.mult).then_inc(one_m, 1)
                dve.wait_ge(i_sig, g + 2)
                chain(tt(ig[:, :], ig[:, :], xc[:, :], ALU.mult))
                dve.wait_ge(g_sig, g + 1)
                tt(sg[:, :], PJ[0][:, :], sg[:, :], ALU.mult).then_inc(pj_free[0], 1)
                dve.wait_ge(root, g + 1)
                chain(nc.vector.memset(th[:, 0:1], 1.0))
                chain(tt(ig[:, :], ig[:, :], th[:, :], ALU.mult))
                chain(nc.vector.tensor_tensor_scan(rg[:, :], av[:, :], ig[:, :], 0.0, ALU.mult, ALU.add))
                tt(sg[:, :], sg[:, :], rg[:, :], ALU.mult).then_inc(y_lru, 1)
                step.leave(G)
            dve.wait_ge(y_lru, G + 1)

            def finish_gate(h):
                dve.wait_ge(d_sig, h + 1)
                dve.wait_ge(gate_st, h * 16 + 16)
                tt(rg[:, :], PJ[0][:, :], ig[:, :], ALU.mult).then_inc(pj_free[0], 1)

            with dve.Fori(0, NH - 1) as h:
                step.enter(h, 12 * per)
                top_rounds(per)
                finish_gate(h)
                step.leave(NH - 1)
            top_rounds(per)
            for q in range(FIRST_SCORED, QB):
                nc.vector.tensor_scalar(mask[:, OFF[q]:OFF[q] + (q + 1) * P], scores[:, off(q):off(q) + (q + 1) * P],
                                        (NEG + TAKEN) / 2, BIG, ALU.is_gt, ALU.mult)
            nc.vector.memset(mask[:, P:2 * P], 0.0)
            nc.vector.tensor_scalar(mask[:, 0:P], causal[:, :], NEG / 2, BIG, ALU.is_lt, ALU.mult)
            nc.vector.tensor_scalar(mask[:, 2 * P:3 * P], causal[:, :], NEG / 2, BIG, ALU.is_lt, ALU.mult
                                    ).then_inc(mask_s, 1)
            dve.wait_ge(mask_s, 1)
            finish_gate(NH - 1)

            def softmin(h, q, p, turn):
                w = (q + 1) * P
                n = min(w, 2 * P)
                if q == 0:
                    dve.wait_ge(qb_ld[p], turn * 32 + 32)
                dve.wait_ge(lg_mm, 8 * h + q + 1)
                lg = LG[q]
                chain(tt(lg[:, w - n:w], lg[:, w - n:w], tb[p][:, 2 * P - n:2 * P], ALU.add))
                dve.wait_ge(p_tp, 8 * h + q + 1)
                hold()
                nc.vector.tensor_tensor_reduce(prob[q], lg[:, 0:w], mask[:, OFF[q]:OFF[q] + w],
                                               1.0, 3.0e38, ALU.add, ALU.min, sums[:, q, 0:1]
                                               ).then_inc(lg_used, 1)

            def normalise(h, q):
                dve.wait_ge(p_exp, 8 * h + q + 1)
                chain(nc.vector.reciprocal(sums[:, q, 2:3], sums[:, q, 1:2]))
                nc.vector.tensor_scalar(prob[q], prob[q], sums[:, q, 2:3], None, ALU.mult).then_inc(p_norm, 1)

            def gated(h, r):
                dve.wait_ge(ro_mm, 4 * h + r + 5)
                dve.wait_ge(gate_ld[r % 2], h * 32 + 16 * (r // 2) + 16)
                dve.wait_ge(y_att, 4 * h + r + 1)
                tok = slice(2 * r * P, 2 * (r + 1) * P)
                tt(yf[:, :], X[1][:, (r % 2) * NT:(r % 2) * NT + 2 * P], gate[:, r % 2, :], ALU.mult).then_inc(o_used, 1)
                dve.wait_ge(o_used, 4 * h + r + 5)
                y3 = yf[:, :].rearrange("p (o s) -> p o s", o=1)
                chain(nc.vector.tensor_copy(hT_hi[:, ds(h + G, 1), tok], y3))
                tt(hT_lo[:, ds(h + G, 1), tok], y3, hT_hi[:, ds(h + G, 1), tok].bitcast(F32), ALU.subtract
                   ).then_inc(y_att, 1)

            def low_y(h, k):
                dve.wait_ge(yl_hi, 2 * h + k + 1)
                piece = (slice(None), ds(h, 1), slice(k * NT, (k + 1) * NT))
                tt(hT_lo[piece], yl_raw[:, :].rearrange("p (o s) -> p o s", o=1),
                   hT_hi[piece].bitcast(F32), ALU.subtract).then_inc(yl_lo, 1)

            def dve_head(h, p, turn, last=False):
                for q in range(QB):
                    if q in (4, 5, 7):
                        gated(h, {4: 0, 5: 1, 7: 2}[q])
                    if q < QB - AHEAD:
                        normalise(h, q + 2)
                        softmin(h, q + AHEAD, p, None)
                    elif q == 6 and not last:
                        softmin(h + 1, 0, 1 - p, turn)
                        softmin(h + 1, 1, 1 - p, turn)
                    elif q == 7 and not last:
                        softmin(h + 1, 2, 1 - p, turn)
                    if q == 5:
                        normalise(h, 7)
                    elif q > 5 and not last:
                        normalise(h + 1, q - 6)
                    if q in (3, 5):
                        low_y(h, (q - 3) // 2)
                gated(h, 3)

            softmin(0, 0, 0, 0)
            softmin(0, 1, 0, 0)
            softmin(0, 2, 0, 0)
            normalise(0, 0)
            normalise(0, 1)
            links = 8 + 8 + 4
            with dve.Fori(0, 3) as i:
                step.enter(i, 2 * links)
                dve_head(i * 2, 0, i)
                dve_head(i * 2 + 1, 1, i + 1)
                step.leave(3)
            dve_head(6, 0, 3)
            dve_head(7, 1, None, last=True)
            dve.wait_ge(y_att, 4 * NH + 1)

            def add_residual(cg, c, u, half=None):
                for q in range(HALF_T):
                    if q < HALF_T - 1:
                        dve.wait_ge(o_mm, cg * (HALF_T - 1) + q + 1)
                    else:
                        dve.wait_ge(wo_used, cg * OP + OP + 2)
                    r = res[q][:, ds(c * OC, OC)]
                    tt(r, PS[2 * u + q // 2][:, (q % 2) * NT:(q % 2) * NT + OC], r, ALU.add).then_inc(o_add, 1)
                    if half == 1 and q > 0:
                        final_norm(cg, q - 1, 1)
                if half == 0:
                    final_norm(cg, 0, HALF_T)
                if half == 1:
                    final_norm(cg, HALF_T - 1, 1)

            def final_norm(cg, q, n):
                dve.wait_ge(o_sq, 4 * cg + q + n + 1)
                nc.vector.reduce_sum(fstat[:, 0, q:q + n], ssq[:, q:q + n, :], AX.X).then_inc(f_tot, 1)
                dve.wait_ge(f_sd, 1 if n > 1 else q + 2)
                chain(nc.vector.reciprocal(fstat[:, 2, q:q + n], fstat[:, 1, q:q + n]))
                for k in range(q, q + n):
                    stt(res[k], res[k], fstat[:, 2, k:k + 1], gf_bc[:, :], ALU.mult, ALU.mult).then_inc(f_out, 1)

            dve.wait_ge(gf_in, 16)
            for half in range(2):
                dve.wait_ge(res_in, 64 * (half + 1))
                with dve.Fori(0, OCH // 2 - 1) as i:
                    for u in range(2):
                        add_residual(i * 2 + (OCH * half + u), i * 2 + u, u)
                add_residual(OCH * half + OCH - 2, OCH - 2, 0)
                add_residual(OCH * half + OCH - 1, OCH - 1, 1, half)


def distance_buckets():
    import numpy as np
    dist = np.maximum(2 * P - 1 - np.arange(BR), 0)
    exact = BUCKETS // 2
    far = exact + (np.log(np.maximum(dist, 1) / exact) / math.log(MAX_DIST / exact)
                   * (BUCKETS - exact)).astype(np.int64)
    bucket = np.where(dist < exact, dist, np.minimum(far, BUCKETS - 1))
    hot = (np.arange(BUCKETS)[:, None] == bucket[None, :]).astype(np.float32)
    hot[BUCKETS - 1] -= 1.0
    return np.ascontiguousarray(-hot)


_INS = ["x", "norm_g", "w_in", "conv_w", "conv_b", "lru_wa", "lru_ba", "lru_wx", "lru_bx", "lru_lambda",
        "ckv_norm_g", "idx_k_norm_g", "idx_k_norm_b", "w_uk", "w_uv", "w_out", "rel_bias", "final_norm_g"]


def kernel(**inputs):
    import numpy as np
    import concourse.bacc as bacc
    from concourse.bass_utils import run_bass_kernel_spmd

    nc = bacc.Bacc("TRN2", target_bir_lowering=False, num_devices=1)
    arrays, aps = {}, {}
    values = {name: np.ascontiguousarray(inputs[name]) for name in _INS}
    values["onehot"] = distance_buckets()
    for name, v in values.items():
        arrays[f"in_{name}"] = v
        aps[name] = nc.dram_tensor(f"in_{name}", v.shape, mybir.dt.from_np(v.dtype), kind="ExternalInput").ap()
    out = nc.dram_tensor("out_0", (1, S, D), F32, kind="ExternalOutput").ap()
    layer(nc, aps, out)
    r = run_bass_kernel_spmd(nc, [arrays], core_ids=[0])
    return r.results[0]["out_0"]
```

```python
import math
from contextlib import ExitStack

import concourse.bass as bass
from concourse import mybir

F32 = mybir.dt.float32
F32R = mybir.dt.float32r
BF16 = mybir.dt.bfloat16
ALU = mybir.AluOpType
ACT = mybir.ActivationFunctionType
AX = mybir.AxisListType
ds = bass.ds

P = 128
D = 2048
S = 1024
KT = D // P
QB = S // P
LRU = 1024
G = LRU // P
CONV = 4
NH = 8
HD = 128
C = 256
CT = C // P
IH = 16
ID = 64
TOPK = 256
BUCKETS = 32
MAX_DIST = 128
EPS = 1e-6
NT = 512

COL_XA, COL_GA, COL_Q, COL_CKV, COL_GB, COL_QI, COL_KI = 0, 1024, 2048, 3072, 3328, 4352, 5376
KW = ID + IH
PIECES = 4
PK = KT // PIECES

T_KW, T_C, T_QI, T_LRU, T_ATT = 0, 1, 3, 11, 27
TILES = 43

PARS = (CONV + 4) * G + CT + 2

XB = 4
AHEAD = 3

FIRST_SCORED = TOPK // P
UNITS = 2 * (QB - FIRST_SCORED)
FULL = sum((q + 1) * P for q in range(QB))
OFF = [P * q * (q + 1) // 2 for q in range(QB)]
SCORED = FULL - OFF[FIRST_SCORED]
NEG = -3.0e38
TAKEN = -3.38e38
BIG = 1.0e30
ROUNDS = TOPK // 8
BR = 3 * P

OC = 512
OCH = D // OC
OPK = 2
OP = KT // OPK
HALF_T = 4
CHUNKS = 2 * OCH


def off(q):
    return OFF[q] - OFF[FIRST_SCORED]


class Tally:

    def __init__(self, sem):
        self.sem, self.base, self.n = sem, 0, 0

    def did(self, ins):
        ins.then_inc(self.sem, 1)
        self.n += 1
        return self.base + self.n

    def now(self):
        return self.base + self.n

    def enter(self, i, per):
        self.start, self.per = self.base + self.n, per
        self.base, self.n = self.start + i * per, 0

    def leave(self, count):
        assert self.n == self.per, (self.n, self.per)
        self.base, self.n = self.start + count * self.per, 0


def layer(nc, a, out):
    x, w_in, w_out = a["x"][0], a["w_in"][0], a["w_out"][0]

    yl_d = nc.dram_tensor("y_lru_dram", [G, P, S], F32).ap()
    q_d = nc.dram_tensor("q_dram", [NH, P, S], F32).ap()
    gate_d = nc.dram_tensor("gate_dram", [NH, P, S], F32).ap()
    c_d = nc.dram_tensor("c_dram", [CT, P, S], F32).ap()
    wk_d = nc.dram_tensor("wuk_dram", [NH, P, CT, HD], F32).ap()
    bias_h = nc.dram_tensor("bias_rows", [NH, P * BR], F32)
    bias_d = bias_h.ap()

    ctx = ExitStack()
    with ctx:
        def sem(name):
            return ctx.enter_context(nc.semaphore(name))

        def alloc(stack):
            return lambda name, shape, dt=F32: stack.enter_context(nc.sbuf_tensor(name, shape, dt))

        sb = alloc(ctx)
        hT_hi = sb("hT_hi", [P, KT, S], F32R)
        hT_lo = sb("hT_lo", [P, KT, S], F32R)
        ident = sb("ident", [P, P])
        causal = sb("causal", [P, P])
        par_t = sb("par_t", [P, PARS])
        conv_w = par_t[:, 0:CONV * G].rearrange("p (j g) -> p j g", g=G)
        lru_p = par_t[:, CONV * G:(CONV + 4) * G].rearrange("p (k g) -> p k g", g=G)
        c_g = par_t[:, PARS - 4:PARS - 2]
        k_gb = par_t[0:ID, PARS - 2:PARS]
        decay = sb("decay", [P, 2, G])
        sp_t = sb("sp_t", [P, 5, G])
        eps = sb("eps", [P, 1])
        pause = sb("pause", [P, 1])
        stat = sb("stat", [P, 3 * XB])
        w_nat = sb("w_nat", [P, QB, IH])
        sums = sb("sums", [P, QB, 3])

        ph = ExitStack()
        sbp = alloc(ph)
        w_raw = sbp("w_raw", [P, PIECES, PK, P])
        w_hi = sbp("w_hi", [P, PIECES, PK, P], F32R)
        w_lo = sbp("w_lo", [P, PIECES, PK, P], F32R)
        p0 = ExitStack()
        s0 = alloc(p0)
        xin = s0("xin", [P, XB, D])
        g_bc = s0("g_bc", [P, D])
        junk = s0("junk", [P, D], BF16)
        par_rows = s0("par_rows", [PARS, P])
        onehot = s0("onehot", [BUCKETS, BR])
        rel = s0("rel", [BUCKETS, NH])
        bias_sb = s0("bias_sb", [NH, BR])
        p0.close()
        scores = sbp("scores", [P, SCORED])
        pb = ExitStack()
        sB = alloc(pb)
        ki_hi = sB("ki_hi", [P, S], F32R)
        ki_lo = sB("ki_lo", [P, S], F32R)
        pa = ExitStack()
        sA = alloc(pa)
        kw_sb = sA("kw_sb", [KW, S])
        k_t = sA("k_t", [ID, S])
        c_sb = sA("c_sb", [P, CT, S])
        c_sq = sA("c_sq", [P, CT, S])
        c_rs = sA("c_rs", [P, S])
        ones_k = sA("ones_k", [ID, ID])
        ones_c = sA("ones_c", [P, P])
        pa.close()
        stack_a1 = sB("stack_a1", [P, S], F32R)
        stack_b1 = sB("stack_b1", [P, S], F32R)
        stack_a0 = sB("stack_a0", [P, S], F32R)
        stack_b0 = sB("stack_b0", [P, S], F32R)
        relu = [sB(f"relu{i}", [P, S]) for i in range(2)]
        stack_a, stack_b = [stack_a0, stack_a1], [stack_b0, stack_b1]
        pb.close()
        pc = ExitStack()
        sC = alloc(pc)
        rg = sC("rg", [P, S])
        pu = ExitStack()
        xc_lo = alloc(pu)("xc_lo", [P, S], F32R)
        pu.close()
        av = sC("av", [P, S])
        ig = sC("ig", [P, S])
        pu = ExitStack()
        sU = alloc(pu)
        wuk = sU("wuk", [P, NH, C])
        wuk_t0 = sU("wuk_t0", [P, NH * CT // 2, HD])
        pu.close()
        pu = ExitStack()
        wuk_t1 = alloc(pu)("wuk_t1", [P, NH * CT // 2, HD])
        pu.close()
        wuk_t = [wuk_t0, wuk_t1]
        xc = sC("xc", [P, S])
        pu = ExitStack()
        xc_hi = alloc(pu)("xc_hi", [P, S], F32R)
        pu.close()
        th = sC("th", [P, S])
        sg = sC("sg", [P, S])
        w_gates = sC("w_gates", [P, 2, P])
        mask_at = 4 * (3 * PIECES * PK * P + SCORED + 6 * S + 2 * P)
        mask = sC("mask", [P, FULL], BF16)
        top8 = sC("top8", [P, QB, 8])
        wg_hi = sC("wg_hi", [P, 2, P], F32R)
        wg_lo = sC("wg_lo", [P, 2, P], F32R)
        pc.close()
        ph.close()

        ph = ExitStack()
        s3 = alloc(ph)
        c_t = s3("c_t", [P, CT, S])
        kT = [s3(f"kT{i}", [P, S]) for i in range(2)]
        vN = [s3(f"vN{i}", [P, QB, HD]) for i in range(2)]
        prob_sb = s3("prob_sb", [P, (8 + 7 + 6) * P])
        pT0 = s3("pT0", [P, 6, 2 * P])
        pT1 = s3("pT1", [P, 8, 2 * P])
        qT1 = s3("qT1", [P, S])
        qT0 = s3("qT0", [P, S])
        qT = [qT0, qT1]
        gate = s3("gate", [P, 2, 2 * P])
        wk = s3("wk", [P, CT, HD])
        wk_lo = s3("wk_lo", [P, CT, HD], F32R)
        wv = [s3(f"wv{i}", [P, CT, HD]) for i in range(2)]
        tb = [s3(f"tb{i}", [P, 2 * P]) for i in range(2)]
        yf = s3("yf", [P, 2 * P])
        before = 4 * (CT * S + 6 * S + 21 * P + 14 * 2 * P + 4 * P + 4 * CT * HD + 4 * P + 2 * P)
        assert before == mask_at
        s3("mask_kept", [P, FULL], BF16)
        yl_raw = s3("yl_raw", [P, NT])
        wk_hi = s3("wk_hi", [P, CT, HD], F32R)
        pT = [pT0, pT1]
        ph.close()

        ph = ExitStack()
        s4 = alloc(ph)
        wo_raw = s4("wo_raw", [P, 4, OPK, OC])
        gf_bc = s4("gf_bc", [P, D])
        wo_lo = s4("wo_lo", [P, 2, OPK, OC], F32R)
        res01 = s4("res01", [P, 2, D])
        s4("wo_pad", [P, P])
        wo_hi = s4("wo_hi", [P, 2, OPK, OC], F32R)
        res23 = s4("res23", [P, 2, D])
        res = [res01[:, 0, :], res01[:, 1, :], res23[:, 0, :], res23[:, 1, :]]
        junk4 = s4("junk4", [P, OC], BF16)
        ssq = s4("ssq", [P, HALF_T, OCH])
        fstat = s4("fstat", [P, 3, HALF_T])
        ph.close()

        latent = slice(G - CT, G)
        c_hi, c_lo = hT_hi[:, latent, :], hT_lo[:, latent, :]

        PS = [ctx.enter_context(nc.psum_tensor(f"ps{i}", [P, S], F32)) for i in range(4)]
        PJ, X = PS[0:2], PS[2:4]

        PROB_AT = [15 * P, 16 * P, 18 * P, 8 * P, 0, 15 * P, 8 * P, 0]
        prob = [prob_sb[:, PROB_AT[q]:PROB_AT[q] + (q + 1) * P] for q in range(QB)]
        LG = [PS[0][:, 0:NT], PS[0][:, NT:S], PS[1][:, 0:NT], PS[1][:, NT:S], PS[2], PS[0], PS[1], PS[2]]
        LAST = [3, 4, 4, 5, 5, 4, 3, 3]

        id_made = sem("id_made")
        consts = sem("consts")
        eps_made = sem("eps_made")
        ones_made = sem("ones_made")
        rows_clear = sem("rows_clear")
        small_in = sem("small_in")
        small_tp = sem("small_tp")
        small_cp = sem("small_cp")
        bias_in = sem("bias_in")
        bias_mm = sem("bias_mm")
        bias_cp = sem("bias_cp")
        bias_st = sem("bias_st")
        wuk_in = sem("wuk_in")
        wuk_tp = sem("wuk_tp")
        wuk_cp = sem("wuk_cp")
        wuk_st = sem("wuk_st")
        g_in = sem("g_in")
        x_in = [sem(f"x_in{i}") for i in range(XB)]
        x_rest = [sem(f"x_rest{i}") for i in range(QB - XB)]
        x_sd = sem("x_sd")
        x_norm = sem("x_norm")
        x_tp = sem("x_tp")
        h_hi = sem("h_hi")
        h_lo = sem("h_lo")
        w_in_s = [sem(f"w_in{j}") for j in range(PIECES)]
        w_hi_s = sem("w_hi_s")
        w_lo_s = sem("w_lo_s")
        w_used = sem("w_used")
        pj_free = [sem("pj_free0"), sem("pj_free1")]
        k_mean = sem("k_mean")
        k_dev = sem("k_dev")
        k_sq = sem("k_sq")
        k_var = sem("k_var")
        k_sd = sem("k_sd")
        k_nrm = sem("k_nrm")
        k_ln = sem("k_ln")
        ki_done = sem("ki_done")
        w_tp = sem("w_tp")
        w_nat_s = sem("w_nat_s")
        c_sq_s = sem("c_sq_s")
        c_var = sem("c_var")
        c_sd = sem("c_sd")
        c_done = sem("c_done")
        c_st = sem("c_st")
        st_hi = sem("st_hi")
        ix_mm = sem("ix_mm")
        ix_relu = sem("ix_relu")
        ix_acc = sem("ix_acc")
        sp_exp = sem("sp_exp")
        sp_in = sem("sp_in")
        dec_s = sem("dec_s")
        gw_in = sem("gw_in")
        xc0 = sem("xc0")
        xc_hi_s = sem("xc_hi_s")
        wg_hi_s = sem("wg_hi_s")
        gates_lo_s = sem("gates_lo_s")
        gates_mm = sem("gates_mm")
        r_sig = sem("r_sig")
        i_sig = sem("i_sig")
        g_sig = sem("g_sig")
        a_sq = sem("a_sq")
        one_m = sem("one_m")
        root = sem("root")
        y_lru = sem("y_lru_s")
        y_st = sem("y_st")
        d_sig = sem("d_sig")
        q_st = sem("q_st")
        gate_st = sem("gate_st")
        mask_s = sem("mask_s")
        c_ld = sem("c_ld")
        c_hi_s = sem("c_hi_s")
        c_lo_s = sem("c_lo_s")
        wk_hi_s = sem("wk_hi_s")
        wk_lo_s = sem("wk_lo_s")
        kv_ld = [sem("kv_ld0"), sem("kv_ld1")]
        qb_ld = [sem("qb_ld0"), sem("qb_ld1")]
        gate_ld = [sem("gate_ld0"), sem("gate_ld1")]
        yl_ld = sem("yl_ld")
        yl_hi = sem("yl_hi")
        yl_lo = sem("yl_lo")
        kv_mm_s = sem("kv_mm")
        ro_mm = sem("ro_mm")
        kv_cp = sem("kv_cp")
        o_used = sem("o_used")
        lg_mm = sem("lg_mm")
        lg_used = sem("lg_used")
        p_exp = sem("p_exp")
        p_norm = sem("p_norm")
        p_tp = sem("p_tp")
        p_cp = sem("p_cp")
        y_att = sem("y_att")
        wo_in = [sem(f"wo_in{i}") for i in range(4)]
        wo_hi_s = sem("wo_hi_s")
        wo_lo_s = sem("wo_lo_s")
        wo_used = sem("wo_used")
        gf_in = sem("gf_in")
        res_in = sem("res_in")
        o_mm = sem("o_mm")
        o_add = sem("o_add")
        o_sq = sem("o_sq")
        f_tot = sem("f_tot")
        f_sd = sem("f_sd")
        f_out = sem("f_out")
        out_st = [sem(f"out_st{q}") for q in range(HALF_T)]
        act_step = sem("act_step")
        dve_step = sem("dve_step")
        pool_step = sem("pool_step")

        def x_bank(i, j):
            return (PS[2 * (i % 2) + j] if i < XB else X[j])[:, :]

        def out_piece(n):
            j = n // 2
            if n % 2 == 0:
                return wo_hi[:, j % 2, :, :], wo_lo[:, j % 2, :, :]
            return hT_hi[:, OPK * j:OPK * (j + 1), 0:OC], hT_lo[:, OPK * j:OPK * (j + 1), 0:OC]

        def w_rows(c0, n):
            v = w_in.rearrange("(j k p) e -> j p k e", j=PIECES, p=P)
            return [v[j, :, :, ds(c0, n)] for j in range(PIECES)]

        block = ctx.enter_context(nc.Block())

        @block.sync
        def _(sp):
            def weights(t, c0, n=P):
                for j, src in enumerate(w_rows(c0, n)):
                    sp.wait_ge(w_lo_s, 4 * t + j + 1)
                    sp.dma_start(w_raw[:, j, :, 0:n], src).then_inc(w_in_s[j], 16)

            def x_load(i):
                sp.dma_start(xin[:, i, :], x[i * P:(i + 1) * P, :]).then_inc(x_in[i], 16)

            x_load(0)
            sp.dma_start(g_bc[:, :], a["norm_g"].broadcast_to([P, D])).then_inc(g_in, 16)
            x_load(1)
            sp.dma_start(rel[:, :], a["rel_bias"]).then_inc(bias_in, 16)
            sp.dma_start(onehot[:, :], a["onehot"]).then_inc(bias_in, 16)
            for i in range(2, XB):
                x_load(i)
            sp.wait_ge(rows_clear, 1)
            rows = 0
            for name, n, m in [("conv_w", CONV * G, P), ("conv_b", G, P), ("lru_ba", G, P), ("lru_bx", G, P),
                               ("lru_lambda", G, P), ("ckv_norm_g", CT, P), ("idx_k_norm_g", 1, ID),
                               ("idx_k_norm_b", 1, ID)]:
                v = a[name][0]
                src = v.rearrange("j (g p) -> (j g) p", p=P) if len(v.shape) == 2 else v.rearrange("(g p) -> g p", p=m)
                sp.dma_start(par_rows[rows:rows + n, 0:m], src).then_inc(small_in, 16)
                rows += n
            weights(T_KW, COL_KI, KW)
            for i in range(QB - XB):
                sp.wait_ge(x_tp, 2 * i + 2)
                sp.dma_start(xin[:, i, :], x[(i + XB) * P:(i + XB + 1) * P, :]).then_inc(x_rest[i], 16)
            sp.wait_ge(bias_cp, 1)
            sp.dma_start(bias_d.rearrange("h (p m) -> h p m", p=P),
                         bias_sb[:, :].rearrange("h (o m) -> h o m", o=1).broadcast_to([NH, P, BR])).then_inc(bias_st, 16)
            weights(T_C, COL_CKV)
            weights(T_C + 1, COL_CKV + P)
            weights(T_QI, COL_QI)
            weights(T_QI + 1, COL_QI + P)
            weights(T_QI + 2, COL_QI + 2 * P)
            sp.wait_ge(c_done, 4 * CT)
            for t in range(CT):
                sp.dma_start(c_d[t], c_sb[:, t, :]).then_inc(c_st, 16)
            with sp.Fori(0, 5) as i:
                weights(T_QI + 3 + i, COL_QI + 3 * P + i * P)
            def lru_loads(g):
                weights(T_LRU + 2 * g, COL_XA + g * P)
                weights(T_LRU + 1 + 2 * g, COL_GA + g * P)

            def gate_loads(g):
                sp.wait_ge(gates_mm, g + 1)
                sp.dma_start(w_gates[:, 0, :], a["lru_wa"][0, ds(g, 1)].rearrange("o i j -> (o i) j")
                             ).then_inc(gw_in, 16)
                sp.dma_start(w_gates[:, 1, :], a["lru_wx"][0, ds(g, 1)].rearrange("o i j -> (o i) j")
                             ).then_inc(gw_in, 16)

            lru_loads(0)
            sp.wait_ge(ix_acc, 8 + 8 * UNITS)
            gate_loads(0)
            with sp.Fori(1, G) as g:
                lru_loads(g)
                sp.wait_ge(y_lru, g + 1)
                sp.dma_start(yl_d[ds(g - 1, 1)].rearrange("o p s -> (o p) s"), sg[:, :]).then_inc(y_st, 16)
                gate_loads(g)
            def att_loads(h):
                weights(T_ATT + 2 * h, COL_Q + h * P)
                weights(T_ATT + 1 + 2 * h, COL_GB + h * P)

            def att_stores(h):
                sp.wait_ge(pj_free[1], h + T_ATT // 2 + 2)
                sp.dma_start(q_d[ds(h, 1)].rearrange("o p s -> (o p) s"), av[:, :]).then_inc(q_st, 16)
                sp.wait_ge(pj_free[0], h + (T_ATT + 1) // 2 + 2)
                sp.dma_start(gate_d[ds(h, 1)].rearrange("o p s -> (o p) s"), rg[:, :]).then_inc(gate_st, 16)

            att_loads(0)
            sp.wait_ge(y_lru, G + 1)
            sp.dma_start(yl_d[G - 1], sg[:, :]).then_inc(y_st, 16)
            sp.dma_start(wuk[:, :, :], a["w_uk"][0].rearrange("h d c -> d h c")).then_inc(wuk_in, 16)
            att_loads(1)
            att_stores(0)
            for k in range(2):
                sp.wait_ge(wuk_cp, k + 1)
                sp.dma_start(wk_d[k * NH // 2:(k + 1) * NH // 2].rearrange("h c t d -> c h t d"),
                             wuk_t[k][:, :, :].rearrange("c (h t) d -> c h t d", t=CT)).then_inc(wuk_st, 16)
            with sp.Fori(2, NH) as h:
                att_loads(h)
                att_stores(h - 1)

            def kv_loads(h, p, early=False):
                sp.wait_ge(wk_lo_s, h + 1)
                sp.dma_start(wk[:, :, :], wk_d[ds(h, 1)].rearrange("o p t d -> (o p) t d")).then_inc(kv_ld[p], 16)
                if not early:
                    sp.wait_ge(kv_mm_s, 4 * h - 4)
                sp.dma_start(wv[p][:, :, :], a["w_uv"][0, ds(h, 1)].rearrange("o (t p) d -> (o p) t d", p=P)
                             ).then_inc(kv_ld[p], 16)

            def qb_loads(h, p):
                sp.dma_start(qT[p][:, :], q_d[ds(h, 1)].rearrange("o p s -> (o p) s")).then_inc(qb_ld[p], 16)
                src = bias_d[ds(h, 1), P - 1:P - 1 + P * (BR - 1)].rearrange("o (p m) -> (o p) m", p=P)[:, 0:2 * P]
                sp.dma_start(tb[p][:, :], src).then_inc(qb_ld[p], 16)

            def tail_loads(h):
                for k in range(2):
                    sp.wait_ge(yl_lo, 2 * h + k + 1)
                    sp.dma_start(yl_raw[:, :], yl_d[ds(h, 1), :, k * NT:(k + 1) * NT].rearrange(
                        "o p s -> (o p) s")).then_inc(yl_ld, 16)

            def head_loads(h, p):
                kv_loads(h, p)
                sp.wait_ge(lg_used, 8 * h - 8)
                qb_loads(h, p)
                tail_loads(h - 1)

            sp.wait_ge(c_st, 16 * CT)
            sp.wait_ge(w_lo_s, 4 * TILES + 4)
            sp.dma_start(c_t[:, :, :], c_d.rearrange("t p s -> p t s")).then_inc(c_ld, 16)
            sp.wait_ge(wuk_st, 32)
            kv_loads(0, 0, early=True)
            sp.wait_ge(bias_st, 16)
            sp.wait_ge(q_st, 32)
            qb_loads(0, 0)
            att_stores(NH - 1)
            kv_loads(1, 1, early=True)
            sp.wait_ge(mask_s, 1)
            sp.wait_ge(y_st, 16 * (G + 1))
            sp.wait_ge(q_st, 16 * (NH + 1))
            qb_loads(1, 1)
            tail_loads(0)
            with sp.Fori(1, NH // 2) as i:
                head_loads(i * 2, 0)
                head_loads(i * 2 + 1, 1)
            v_out = w_out.rearrange("(j k p) e -> j p k e", j=OP, p=P)

            def out_weights(cg, chunk, js=range(OP)):
                for j in js:
                    sp.wait_ge(wo_lo_s, 8 * cg + j + 1)
                    sp.dma_start(wo_raw[:, j % 4, :, :], v_out[j, :, :, ds(chunk * OC, OC)]
                                 ).then_inc(wo_in[j % 4], 16)

            sp.wait_ge(kv_mm_s, 4 * NH)
            out_weights(0, 0, range(2))
            sp.wait_ge(lg_used, 8 * (NH - 1))
            out_weights(0, 0, [2])
            tail_loads(NH - 1)
            sp.wait_ge(lg_used, 8 * NH)
            out_weights(0, 0, [3])
            sp.wait_ge(y_att, 4 * NH + 1)

            def token_rows(th, q):
                return slice((th * HALF_T + q) * P, (th * HALF_T + q + 1) * P)

            def residual(th, q):
                sp.dma_start(res[q], x[token_rows(th, q), :]).then_inc(res_in, 16)

            def stores(th):
                for q in range(HALF_T):
                    for k in range(2):
                        sp.wait_ge(f_out, 2 * (HALF_T * th + q) + k + 1)
                        half = slice(k * D // 2, (k + 1) * D // 2)
                        sp.dma_start(out[0, token_rows(th, q), half], res[q][:, half]).then_inc(out_st[q], 16)

            for q in range(HALF_T):
                residual(0, q)
            sp.dma_start(gf_bc[:, :], a["final_norm_g"].rearrange("(o d) -> o d", o=1).broadcast_to([P, D])
                         ).then_inc(gf_in, 16)
            out_weights(0, 0, range(4, OP))
            with sp.Fori(1, OCH) as c:
                out_weights(c, c)
            out_weights(OCH, 0)
            stores(0)
            for q in range(HALF_T):
                sp.wait_ge(out_st[q], 32)
                residual(1, q)
                if q == 1:
                    out_weights(OCH + 1, 1, range(2))
            out_weights(OCH + 1, 1, range(2, OP))
            for n in range(2 * OP):
                sp.wait_ge(wo_lo_s, OP * (CHUNKS - 2) + n + 1)
                sp.dma_start(wo_raw[:, n % 4, :, :], v_out[n // 2, :, :, (OCH - 2 + n % 2) * OC:(OCH - 1 + n % 2) * OC]
                             ).then_inc(wo_in[n % 4], 16)
            stores(1)
            for q in range(HALF_T):
                sp.wait_ge(out_st[q], 64)

        @block.gpsimd
        def _(pool):
            nc.gpsimd.sem_inc(w_lo_s, PIECES)
            nc.gpsimd.sem_inc(wo_lo_s, 4)
            nc.gpsimd.sem_inc(wk_lo_s, 1)
            nc.gpsimd.memset(ident[:, :], 0.0).then_inc(pool_step, 1)
            nc.gpsimd.memset(causal[:, :], 0.0).then_inc(pool_step, 1)
            pool.wait_ge(pool_step, 2)
            nc.gpsimd.affine_select(out=ident[:, :], in_=ident[:, :], compare_op=ALU.not_equal, fill=1.0,
                                    base=0, pattern=[[-1, P]], channel_multiplier=1).then_inc(id_made, 1)
            nc.gpsimd.affine_select(out=causal[:, :], in_=causal[:, :], compare_op=ALU.is_ge, fill=NEG,
                                    base=0, pattern=[[-1, P]], channel_multiplier=1).then_inc(consts, 1)

            def low(t, n=P):
                for j in range(PIECES):
                    pool.wait_ge(w_hi_s, 4 * t + j + 1)
                    nc.gpsimd.tensor_tensor(w_lo[:, j, :, 0:n], w_raw[:, j, :, 0:n],
                                            w_hi[:, j, :, 0:n].bitcast(F32), ALU.subtract).then_inc(w_lo_s, 1)

            low(T_KW, KW)
            with pool.Fori(1, TILES) as t:
                low(t)
            pool.wait_ge(c_hi_s, 1)
            nc.gpsimd.tensor_tensor(c_lo, c_t[:, :, :], c_hi.bitcast(F32), ALU.subtract).then_inc(c_lo_s, 1)

            def low_wk(h, p):
                pool.wait_ge(wk_hi_s, h + 1)
                nc.gpsimd.tensor_tensor(wk_lo[:, :, :], wk[:, :, :], wk_hi[:, :, :].bitcast(F32), ALU.subtract
                                        ).then_inc(wk_lo_s, 1)

            low_wk(0, 0)
            low_wk(1, 1)
            pool.wait_ge(gate_st, 16 * (NH + 1))
            pool.wait_ge(wuk_st, 32)
            def gate_loads(h):
                for r in range(4):
                    pool.wait_ge(o_used, 4 * h + r + 3)
                    pool.dma_start(gate[:, r % 2, :], gate_d[ds(h, 1), :, 2 * r * P:2 * (r + 1) * P].rearrange(
                        "o p s -> (o p) s")).then_inc(gate_ld[r % 2], 16)

            with pool.Fori(0, NH // 2 - 1) as i:
                for p in range(2):
                    gate_loads(i * 2 + p)
                    low_wk(i * 2 + (2 + p), p)
            gate_loads(NH - 2)
            gate_loads(NH - 1)
            pool.wait_ge(p_tp, 8 * NH + 3)
            with pool.Fori(0, CHUNKS - 2) as c:
                for j in range(OP):
                    pool.wait_ge(wo_hi_s, 8 * c + j + 1)
                    nc.gpsimd.tensor_tensor(wo_lo[:, j % 2, :, :], wo_raw[:, j % 4, :, :],
                                            wo_hi[:, j % 2, :, :].bitcast(F32), ALU.subtract).then_inc(wo_lo_s, 1)
            for n in range(2 * OP):
                pool.wait_ge(wo_hi_s, OP * (CHUNKS - 2) + n + 1)
                hi, lo = out_piece(n)
                nc.gpsimd.tensor_tensor(lo, wo_raw[:, n % 4, :, :], hi.bitcast(F32), ALU.subtract).then_inc(wo_lo_s, 1)

        @block.scalar
        def _(act):
            nc.scalar.sem_inc(ix_relu, 2)
            nc.scalar.sem_inc(pj_free[0], 1)
            nc.scalar.sem_inc(pj_free[1], 1)
            nc.scalar.sem_inc(p_cp, 4)
            nc.scalar.sem_inc(o_sq, 1)
            nc.scalar.sem_inc(i_sig, 1)
            nc.scalar.sem_inc(y_st, 16)
            nc.scalar.sem_inc(q_st, 16)
            nc.scalar.sem_inc(gate_st, 16)
            step = Tally(act_step)
            done = lambda t: 4 * t + 8

            def square(i):
                act.wait_ge(x_in[i] if i < XB else x_rest[i - XB], 16)
                step.did(nc.scalar.activation(junk[:, :], xin[:, i % XB, :], ACT.Square,
                                              accum_out=stat[:, i % XB:i % XB + 1]))

            def root_x(i):
                act.wait_ge(act_step, i + 2)
                nc.scalar.activation(stat[:, XB + i % XB:XB + i % XB + 1], stat[:, i % XB:i % XB + 1], ACT.Sqrt,
                                     scale=1.0 / D, bias=eps[:, :]).then_inc(x_sd, 1)

            def high_x(i):
                for j in range(2):
                    act.wait_ge(x_tp, 2 * i + j + 1)
                    nc.scalar.activation(
                        hT_hi[:, 8 * j:8 * j + 8, i * P:(i + 1) * P],
                        x_bank(i, j).rearrange("p (t s) -> p t s", s=P), ACT.Copy).then_inc(h_hi, 1)

            def high(t, js=range(PIECES), n=P):
                for j in js:
                    act.wait_ge(w_in_s[j], 16 * t + 16)
                    act.wait_ge(w_used, 4 * t + j + 1)
                    nc.scalar.activation(w_hi[:, j, :, 0:n], w_raw[:, j, :, 0:n], ACT.Copy).then_inc(w_hi_s, 1)

            act.wait_ge(eps_made, 1)
            s = step.did(nc.scalar.activation(junk[:, 0:1], eps[:, :], ACT.Sqrt))
            act.wait_ge(act_step, s)
            square(0)
            root_x(0)
            square(1)
            act.wait_ge(bias_mm, 1)
            nc.scalar.activation(bias_sb[:, :], X[0][0:NH, 0:BR], ACT.Copy).then_inc(bias_cp, 1)
            for i in range(QB):
                if i + 1 < QB:
                    root_x(i + 1)
                if i + 2 < QB:
                    square(i + 2)
                high_x(i)
                if i == XB - 2:
                    high(0, n=KW)

            high(1)
            act.wait_ge(small_tp, 1)
            nc.scalar.activation(par_t[:, :], X[1][:, 0:PARS], ACT.Copy).then_inc(small_cp, 1)
            act.wait_ge(bias_st, 16)
            act.wait_ge(w_used, done(0))
            nc.scalar.activation(kw_sb[:, :], PJ[0][0:KW, :], ACT.Copy).then_inc(pj_free[0], 1)
            high(2)
            act.wait_ge(w_used, done(1))
            nc.scalar.activation(c_sb[:, 0, :], PJ[1][:, :], ACT.Copy).then_inc(pj_free[1], 1)
            act.wait_ge(pj_free[1], 2)
            nc.scalar.activation(c_sq[:, 0, :], c_sb[:, 0, :], ACT.Square).then_inc(c_sq_s, 1)
            act.wait_ge(k_dev, 1)
            nc.scalar.activation(k_t[:, :], kw_sb[0:ID, :], ACT.Square).then_inc(k_sq, 1)
            high(3)
            act.wait_ge(w_used, done(2))
            nc.scalar.activation(c_sb[:, 1, :], PJ[0][:, :], ACT.Copy).then_inc(pj_free[0], 1)
            act.wait_ge(pj_free[0], 3)
            nc.scalar.activation(c_sq[:, 1, :], c_sb[:, 1, :], ACT.Square).then_inc(c_sq_s, 1)
            act.wait_ge(k_var, 1)
            nc.scalar.activation(k_t[:, :], X[1][0:ID, :], ACT.Sqrt, bias=eps[0:ID, :]).then_inc(k_sd, 1)
            act.wait_ge(k_nrm, 1)
            nc.scalar.activation(k_t[:, :], kw_sb[0:ID, :], ACT.Identity, scale=k_gb[:, 0:1],
                                 bias=k_gb[:, 1:2]).then_inc(k_ln, 1)
            act.wait_ge(k_ln, 1)
            nc.scalar.activation(ki_hi[0:ID, :], k_t[:, :], ACT.Copy).then_inc(k_ln, 1)
            nc.scalar.activation(ki_hi[ID:P, :], k_t[:, :], ACT.Copy).then_inc(k_ln, 1)
            high(4)
            act.wait_ge(sp_in, 1)
            nc.scalar.activation(sp_t[:, 1, :], sp_t[:, 0, :], ACT.Exp).then_inc(sp_exp, 1)
            act.wait_ge(c_var, 1)
            nc.scalar.activation(c_rs[:, :], X[1][:, :], ACT.Sqrt, bias=eps[:, :]).then_inc(c_sd, 1)
            act.wait_ge(ki_done, 2)
            act.wait_ge(w_tp, 1)

            def stacks(t, par):
                act.wait_ge(w_used, done(t))
                act.wait_ge(ix_mm, t * UNITS - UNITS * (T_QI - 1))
                nc.scalar.activation(stack_a[par][0:ID, :], PJ[par][0:ID, :], ACT.Copy).then_inc(st_hi, 1)
                nc.scalar.activation(stack_b[par][ID:P, :], PJ[par][ID:P, :], ACT.Copy).then_inc(st_hi, 1)

            def relus(t, ms):
                for m in ms:
                    q = FIRST_SCORED + m % (UNITS // 2)
                    w = (q + 1) * P
                    k = t * UNITS + (m - UNITS * T_QI)
                    act.wait_ge(ix_mm, k + 1 + 2 * UNITS)
                    act.wait_ge(ix_acc, k + 7)
                    nc.scalar.activation(relu[m % 2][:, 0:w], X[m % 2][:, 0:w], ACT.Relu).then_inc(ix_relu, 1)

            def act_b(t, par):
                stacks(t - 1, 1 - par)
                for j in range(PIECES):
                    high(t + 1, [j])
                    relus(t - 1, range(min(4 * j, UNITS), min(4 * j + 4, UNITS)))

            act_b(T_QI + 1, 0)
            act.wait_ge(c_st, 16 * CT)
            with act.Fori(0, 3) as i:
                act_b(i * 2 + (T_QI + 2), 1)
                act_b(i * 2 + (T_QI + 3), 0)
            act_b(T_LRU, 1)

            act.wait_ge(ix_acc, 8 + 8 * UNITS)
            act.wait_ge(dec_s, 1)

            def lru(g, first=False):
                par = lambda k: lru_p[:, k, ds(g, 1)]
                if not first:
                    high(g * 2 + (T_LRU + 1))
                act.wait_ge(w_used, g * 8 + done(T_LRU))
                act.wait_ge(y_lru, g + 1)
                nc.scalar.activation(xc[:, :], PJ[1][:, :], ACT.Identity, scale=conv_w[:, CONV - 1, ds(g, 1)],
                                     bias=par(0)).then_inc(xc0, 1)
                act.wait_ge(gw_in, g * 32 + 32)
                nc.scalar.activation(wg_hi[:, :, :], w_gates[:, :, :], ACT.Copy).then_inc(wg_hi_s, 1)
                act.wait_ge(pj_free[1], g + T_LRU // 2 + 2)
                nc.scalar.activation(xc_hi[:, :], xc[:, :], ACT.Copy).then_inc(xc_hi_s, 1)
                high(g * 2 + (T_LRU + 2))
                act.wait_ge(gates_mm, g + 2)
                nc.scalar.activation(rg[:, :], X[0][:, :], ACT.Sigmoid, bias=par(1)).then_inc(r_sig, 1)
                nc.scalar.activation(ig[:, :], X[1][:, :], ACT.Sigmoid, bias=par(2)).then_inc(i_sig, 1)
                act.wait_ge(y_st, 16 * g + 16)
                nc.scalar.activation(sg[:, :], PJ[0][:, :], ACT.Sigmoid).then_inc(g_sig, 1)
                act.wait_ge(r_sig, g + 1)
                nc.scalar.activation(th[:, :], rg[:, :], ACT.Tanh, scale=decay[:, 0, ds(g, 1)])
                s = step.did(nc.scalar.activation(av[:, :], rg[:, :], ACT.Exp, scale=decay[:, 1, ds(g, 1)]))
                act.wait_ge(act_step, s)
                nc.scalar.activation(rg[:, :], av[:, :], ACT.Square).then_inc(a_sq, 1)
                act.wait_ge(one_m, g + 1)
                nc.scalar.activation(th[:, :], th[:, :], ACT.Sqrt).then_inc(root, 1)

            lru(0, first=True)
            with act.Fori(1, G) as g:
                step.enter(g - 1, 1)
                lru(g)
                step.leave(G - 1)

            act.wait_ge(y_lru, G + 1)

            def high_wk(p, turn):
                act.wait_ge(kv_ld[p], turn * 32 + 32)
                nc.scalar.activation(wk_hi[:, :, :], wk[:, :, :], ACT.Copy).then_inc(wk_hi_s, 1)

            def att(h, last):
                high(h * 2 + (T_ATT + 1))
                act.wait_ge(w_used, h * 8 + done(T_ATT))
                act.wait_ge(q_st, h * 16 + 16)
                nc.scalar.activation(av[:, :], PJ[1][:, :], ACT.Copy, scale=-HD ** -0.5).then_inc(pj_free[1], 1)
                if not last:
                    high(h * 2 + (T_ATT + 2))
                else:
                    act.wait_ge(c_ld, 16)
                    act.wait_ge(w_used, 4 * (TILES - 1) + G // PK + 4)
                    nc.scalar.activation(c_hi, c_t[:, :, :], ACT.Copy).then_inc(c_hi_s, 1)
                    high_wk(0, 0)
                act.wait_ge(w_used, h * 8 + done(T_ATT + 1))
                act.wait_ge(pj_free[0], h + (T_ATT + 1) // 2 + 1)
                nc.scalar.activation(ig[:, :], PJ[0][:, :], ACT.Sigmoid).then_inc(d_sig, 1)

            att(0, False)
            for k in range(2):
                if k == 0:
                    act.wait_ge(y_st, 16 * (G + 1))
                act.wait_ge(wuk_tp, k + 1)
                nc.scalar.activation(wuk_t[k][:, :, :], X[k][:, :].rearrange("p (t d) -> p t d", d=HD), ACT.Copy
                                     ).then_inc(wuk_cp, 1)
            with act.Fori(1, NH - 1) as h:
                att(h, False)
            att(NH - 1, True)

            def kv(h, p, part, ks=range(2)):
                for k in ks:
                    act.wait_ge(kv_mm_s, 4 * h + 2 * part + k + 1)
                    src = X[1][:, k * NT:(k + 1) * NT]
                    if part == 0:
                        dst = kT[p][:, k * NT:(k + 1) * NT]
                    else:
                        dst, src = vN[p][:, 4 * k:4 * k + 4, :], src.rearrange("p (t d) -> p t d", d=HD)
                    nc.scalar.activation(dst, src, ACT.Copy).then_inc(kv_cp, 1)

            def softexp(h, q):
                act.wait_ge(lg_used, 8 * h + q + 1)
                nc.scalar.activation(prob[q], prob[q], ACT.Exp, scale=-1.0,
                                     bias=sums[:, q, 0:1], accum_out=sums[:, q, 1:2]).then_inc(p_exp, 1)

            def p_copy(h, q):
                act.wait_ge(p_tp, 8 * h + q + 4)
                if q % 2 == 0:
                    act.wait_ge(ro_mm, 4 * h + q // 2 + 3)
                nc.scalar.activation(pT[(q // 2) % 2][:, 0:q + 1, (q % 2) * P:(q % 2) * P + P],
                                     LG[q][:, 0:(q + 1) * P].rearrange("p (t s) -> p t s", s=P),
                                     ACT.Copy).then_inc(p_cp, 1)

            def act_head(h, p, turn=None, last=False):
                for q in range(QB):
                    p_copy(h, q)
                    if q + 2 >= QB and not last:
                        softexp(h + 1, q + 2 - QB)
                    elif q + 2 < QB and q != 2:
                        softexp(h, q + 2)
                    if q == 5 and turn is not None:
                        high_wk(p, turn)
                    if q == 0 and not last:
                        kv(h + 1, 1 - p, 0)
                    if q == 1:
                        if not last:
                            kv(h + 1, 1 - p, 1, [0])
                        softexp(h, 4)
                        if not last:
                            kv(h + 1, 1 - p, 1, [1])
                    if q in (2, 5):
                        k = q // 5
                        act.wait_ge(yl_ld, 32 * h + 16 * k + 16)
                        nc.scalar.activation(hT_hi[:, ds(h, 1), k * NT:(k + 1) * NT],
                                             yl_raw[:, :].rearrange("p (o s) -> p o s", o=1), ACT.Copy
                                             ).then_inc(yl_hi, 1)

            kv(0, 0, 0)
            high_wk(1, 0)
            kv(0, 0, 1)
            softexp(0, 0)
            softexp(0, 1)
            act.wait_ge(q_st, 16 * (NH + 1))
            act.wait_ge(gate_st, 16 * (NH + 1))
            with act.Fori(0, 3) as i:
                act_head(i * 2, 0, i + 1)
                act_head(i * 2 + 1, 1, i + 1)
            act_head(6, 0)
            act_head(7, 1, last=True)

            def out_high(cg, js):
                for j in js:
                    act.wait_ge(wo_in[j % 4], 32 * cg + 16 * (j // 4) + 16)
                    act.wait_ge(wo_used, 8 * cg + j + 1)
                    nc.scalar.activation(wo_hi[:, j % 2, :, :], wo_raw[:, j % 4, :, :], ACT.Copy
                                         ).then_inc(wo_hi_s, 1)

            def squares(cg, c, half=None):
                for q in range(HALF_T):
                    act.wait_ge(o_add, 4 * cg + q + 9)
                    act.wait_ge(o_sq, 4 * cg + q + 1)
                    nc.scalar.activation(junk4[:, :], res[q][:, ds(c * OC, OC)], ACT.Square,
                                         accum_out=ssq[:, q, ds(c, 1)]).then_inc(o_sq, 1)
                    if half == 1:
                        root_mean(q, 1)
                if half == 0:
                    root_mean(0, HALF_T)

            def root_mean(q, n):
                act.wait_ge(f_tot, 1 if n > 1 else q + 2)
                nc.scalar.activation(fstat[:, 1, q:q + n], fstat[:, 0, q:q + n], ACT.Sqrt, scale=1.0 / D,
                                     bias=eps[:, :]).then_inc(f_sd, 1)

            out_high(0, range(2))
            def last_high(ns):
                for n in ns:
                    act.wait_ge(wo_in[n % 4], 32 * (CHUNKS - 2) + 16 * (n // 4) + 16)
                    if n % 2 == 0:
                        act.wait_ge(wo_used, OP * (CHUNKS - 2) + n // 2 + 1)
                    nc.scalar.activation(out_piece(n)[0], wo_raw[:, n % 4, :, :], ACT.Copy).then_inc(wo_hi_s, 1)

            with act.Fori(0, OCH - 1) as c:
                out_high(c, range(2, OP))
                out_high(c + 1, range(2))
                squares(c, c)
            out_high(OCH - 1, range(2, OP))
            out_high(OCH, range(2))
            squares(OCH - 1, OCH - 1, 0)
            with act.Fori(0, OCH - 3) as c:
                out_high(c + OCH, range(2, OP))
                out_high(c + (OCH + 1), range(2))
                squares(c + OCH, c)
            out_high(CHUNKS - 3, range(2, OP))
            last_high(range(4))
            squares(CHUNKS - 3, OCH - 3)
            last_high(range(4, 2 * OP))
            squares(CHUNKS - 2, OCH - 2)
            squares(CHUNKS - 1, OCH - 1, 1)

        @block.tensor
        def _(pe):
            nc.tensor.sem_inc(w_used, PIECES)
            nc.tensor.sem_inc(wo_used, 2)
            nc.tensor.sem_inc(ix_mm, 2 * UNITS)
            nc.tensor.sem_inc(gates_mm, 1)
            nc.tensor.sem_inc(p_tp, 3)
            nc.tensor.sem_inc(ro_mm, 4)
            pe.wait_ge(bias_in, 32)
            nc.tensor.matmul(X[0][0:NH, 0:BR], rel[:, :], onehot[:, :], start=True, stop=True).then_inc(bias_mm, 1)
            pe.wait_ge(id_made, 1)
            pe.wait_ge(bias_cp, 1)
            def triple(o, j, k, n, m):
                kt = j * PK + k
                hi, lo = hT_hi[:, kt, n * NT:(n + 1) * NT], hT_lo[:, kt, n * NT:(n + 1) * NT]
                whi, wlo = w_hi[:, j, k, 0:m], w_lo[:, j, k, 0:m]
                nc.tensor.matmul(o, wlo, hi, start=(kt == 0), stop=False)
                nc.tensor.matmul(o, whi, lo, start=False, stop=False)
                return nc.tensor.matmul(o, whi, hi, start=False, stop=(kt == KT - 1))

            def turn_x(i):
                pe.wait_ge(x_norm, i + 1)
                for j in range(2):
                    pe.wait_ge(h_lo, 2 * i + j + (1 if i < XB else 3))
                    for n in range(8):
                        last = nc.tensor.transpose(x_bank(i, j)[:, n * P:(n + 1) * P],
                                                   xin[:, i % XB, (8 * j + n) * P:(8 * j + n + 1) * P], ident[:, :])
                    last.then_inc(x_tp, 1)

            for i in range(QB):
                turn_x(i)
                if i >= XB:
                    pe.wait_ge(h_lo, 4 + 2 * XB)
                    pe.wait_ge(w_lo_s, i - XB + 1 + PIECES)
                    for k in range(PK):
                        triple(PJ[0][0:KW, 0:NT], i - XB, k, 0, KW)
            pe.wait_ge(h_lo, 4 + 2 * QB)

            def project_tile(t, par, turn, m=P, between=None, ns=range(2)):
                pe.wait_ge(pj_free[par], turn + 1)
                for j in range(PIECES):
                    pe.wait_ge(w_lo_s, 4 * t + j + 1 + PIECES)
                    for k in range(PK):
                        kt = j * PK + k
                        for n in ns:
                            last = triple(PJ[par][0:m, n * NT:(n + 1) * NT], j, k, n, m)
                        if k == PK - 1:
                            last.then_inc(w_used, 1)
                        if between:
                            between(kt)

            project_tile(0, 0, 0, m=KW, ns=[1])
            pe.wait_ge(small_in, 16 * 8)
            nc.tensor.transpose(X[1][:, 0:PARS], par_rows[:, :], ident[0:PARS, 0:PARS]).then_inc(small_tp, 1)
            project_tile(1, 1, 0)
            pe.wait_ge(small_cp, 1)
            pe.wait_ge(pj_free[0], 2)
            pe.wait_ge(ones_made, 1)
            for n in range(2):
                last = nc.tensor.matmul(X[0][0:ID, n * NT:(n + 1) * NT], ones_k[:, :],
                                        kw_sb[0:ID, n * NT:(n + 1) * NT], start=True, stop=True)
            last.then_inc(k_mean, 1)
            project_tile(2, 0, 1)
            pe.wait_ge(k_sq, 1)
            for n in range(2):
                last = nc.tensor.matmul(X[1][0:ID, n * NT:(n + 1) * NT], ones_k[:, :],
                                        k_t[:, n * NT:(n + 1) * NT], start=True, stop=True)
            last.then_inc(k_var, 1)
            for q in range(QB):
                last = nc.tensor.transpose(X[0][:, q * IH:(q + 1) * IH], kw_sb[ID:KW, q * P:(q + 1) * P],
                                           ident[ID:KW, ID:KW])
            last.then_inc(w_tp, 1)
            project_tile(3, 1, 1)
            pe.wait_ge(c_sq_s, 2)
            pe.wait_ge(k_sd, 1)
            for n in range(2):
                for t in range(CT):
                    last = nc.tensor.matmul(X[1][:, n * NT:(n + 1) * NT], ones_c[:, :],
                                            c_sq[:, t, n * NT:(n + 1) * NT], start=(t == 0), stop=(t == CT - 1))
            last.then_inc(c_var, 1)


            def score(t, par, turn, ms, first=False):
                for m in ms:
                    q = FIRST_SCORED + m % (UNITS // 2)
                    w = (q + 1) * P
                    k = t * UNITS + (m - UNITS * T_QI)
                    if m == 0:
                        pe.wait_ge(pj_free[par], turn + 2)
                    if m == 0 and first:
                        pe.wait_ge(ki_done, 2)
                        pe.wait_ge(c_sd, 1)
                        pe.wait_ge(w_nat_s, 1)
                    pe.wait_ge(ix_relu, k + 1)
                    st = (stack_a, stack_b)[m // (UNITS // 2)][par]
                    for n in range(0, w, NT):
                        e = min(n + NT, w)
                        nc.tensor.matmul(X[m % 2][:, n:e], st[:, q * P:(q + 1) * P], ki_lo[:, n:e],
                                         start=True, stop=False)
                        last = nc.tensor.matmul(X[m % 2][:, n:e], st[:, q * P:(q + 1) * P], ki_hi[:, n:e],
                                                start=False, stop=True)
                    last.then_inc(ix_mm, 1)

            def step_b(t, par, turn, first=False):
                before = turn - 1 + par
                project_tile(t, par, turn, between=lambda kt: score(
                    t - 1, 1 - par, before, range(kt - 3, kt - 2) if 3 <= kt < UNITS + 3 else [], first))

            step_b(T_QI + 1, 0, 2, first=True)
            with pe.Fori(0, 3) as i:
                step_b(i * 2 + (T_QI + 2), 1, i + 2)
                step_b(i * 2 + (T_QI + 3), 0, i + 3)
            step_b(T_LRU, 1, T_LRU // 2)

            def lru(g, first=False):
                if not first:
                    project_tile(g * 2 + T_LRU, 1, g + T_LRU // 2)
                project_tile(g * 2 + (T_LRU + 1), 0, g + (T_LRU + 1) // 2)
                pe.wait_ge(gates_lo_s, g + 1)
                pe.wait_ge(i_sig, g + 1)
                for k in range(2):
                    for n in range(2):
                        o, tok = X[k][:, n * NT:(n + 1) * NT], slice(n * NT, (n + 1) * NT)
                        nc.tensor.matmul(o, wg_lo[:, k, :], xc_hi[:, tok], start=True, stop=False)
                        nc.tensor.matmul(o, wg_hi[:, k, :], xc_lo[:, tok], start=False, stop=False)
                        last = nc.tensor.matmul(o, wg_hi[:, k, :], xc_hi[:, tok], start=False, stop=True)
                last.then_inc(gates_mm, 1)

            lru(0, first=True)
            with pe.Fori(1, G) as g:
                lru(g)

            project_tile(T_ATT, 1, T_ATT // 2)
            project_tile(T_ATT + 1, 0, (T_ATT + 1) // 2)
            pe.wait_ge(wuk_in, 16)
            pe.wait_ge(i_sig, G + 1)
            for k in range(2):
                for n in range(8):
                    h, t = (8 * k + n) // CT, n % CT
                    last = nc.tensor.transpose(X[k][:, n * P:(n + 1) * P], wuk[:, h, t * P:(t + 1) * P], ident[:, :])
                last.then_inc(wuk_tp, 1)
            with pe.Fori(1, NH) as h:
                project_tile(h * 2 + T_ATT, 1, h + T_ATT // 2)
                project_tile(h * 2 + (T_ATT + 1), 0, h + (T_ATT + 1) // 2)

            def keys(o, k):
                for t in range(CT):
                    hi, lo = (hT[:, G - CT + t, k * NT:(k + 1) * NT] for hT in (hT_hi, hT_lo))
                    nc.tensor.matmul(o, wk_lo[:, t, :], hi, start=(t == 0), stop=False)
                    nc.tensor.matmul(o, wk_hi[:, t, :], lo, start=False, stop=False)
                    last = nc.tensor.matmul(o, wk_hi[:, t, :], hi, start=False, stop=(t == CT - 1))
                return last

            def kv_mm(h, p, part, turn):
                if part == 0:
                    pe.wait_ge(wk_lo_s, h + 2)
                else:
                    pe.wait_ge(kv_ld[p], turn * 32 + 32)
                for k in range(2):
                    if part == 0:
                        pe.wait_ge(o_used, 4 * h - 1 + k)
                    else:
                        pe.wait_ge(kv_cp, 4 * h + k + 1)
                    o = X[1][:, k * NT:(k + 1) * NT]
                    if part == 0:
                        last = keys(o, k)
                    else:
                        for s in range(4):
                            for t in range(CT):
                                last = nc.tensor.matmul(o[:, s * HD:(s + 1) * HD],
                                                        c_t[:, t, (4 * k + s) * P:(4 * k + s + 1) * P], wv[p][:, t, :],
                                                        start=(t == 0), stop=(t == CT - 1))
                    last.then_inc(kv_mm_s, 1)

            def logits(h, q, p, turn):
                w = (q + 1) * P
                if q == 0:
                    pe.wait_ge(qb_ld[p], turn * 32 + 32)
                    pe.wait_ge(kv_cp, 4 * h + 2)
                pe.wait_ge(p_cp, 8 * h + q + 5 - LAST[q])
                for n in range(0, w, NT):
                    e = min(n + NT, w)
                    last = nc.tensor.matmul(LG[q][:, n:e], qT[p][:, q * P:(q + 1) * P], kT[p][:, n:e],
                                            start=True, stop=True)
                last.then_inc(lg_mm, 1)

            def turn_p(h, q):
                pe.wait_ge(p_norm, 8 * h + q + 1)
                for t in range(q + 1):
                    last = nc.tensor.transpose(LG[q][:, t * P:(t + 1) * P], prob[q][:, t * P:(t + 1) * P],
                                               ident[:, :])
                last.then_inc(p_tp, 1)

            def read_out(h, pr, p, last_head):
                pe.wait_ge(p_cp, 8 * h + 2 * pr + 6)
                if pr == 0:
                    pe.wait_ge(kv_cp, 4 * h + 4)
                if pr < 2 and not last_head:
                    pe.wait_ge(kv_cp, 4 * h + pr + 7)
                else:
                    pe.wait_ge(o_used, 4 * h + pr + 3)
                k = pr % 2
                for t in range(2 * pr + 2):
                    c0 = P if t == 2 * pr + 1 else 0
                    last = nc.tensor.matmul(X[1][:, k * NT + c0:k * NT + 2 * P], vN[p][:, t, :],
                                            pT[k][:, t, c0:2 * P], start=(t == 0), stop=(t == 2 * pr + 1))
                last.then_inc(ro_mm, 1)

            def pe_head(h, p, turn_next, last=False):
                for q in range(QB):
                    if q > 0:
                        turn_p(h, q)
                    if q in (3, 4, 6):
                        read_out(h, {3: 0, 4: 1, 6: 2}[q], p, last)
                    if 0 < q < QB - AHEAD:
                        logits(h, q + AHEAD, p, None)
                    elif q == 6 and not last:
                        logits(h + 1, 0, 1 - p, turn_next)
                        logits(h + 1, 1, 1 - p, turn_next)
                    elif q == 7 and not last:
                        logits(h + 1, 2, 1 - p, turn_next)
                        logits(h + 1, 3, 1 - p, turn_next)
                        turn_p(h + 1, 0)
                    if q < 2 and not last:
                        kv_mm(h + 1, 1 - p, q, turn_next)
                read_out(h, 3, p, last)

            pe.wait_ge(c_ld, 16)
            pe.wait_ge(wuk_cp, 2)
            pe.wait_ge(c_lo_s, 1)
            pe.wait_ge(wk_lo_s, 2)
            for k in range(2):
                keys(X[1][:, k * NT:(k + 1) * NT], k).then_inc(kv_mm_s, 1)
            kv_mm(0, 0, 1, 0)
            pe.wait_ge(pj_free[0], TILES // 2 + 2)
            pe.wait_ge(pj_free[1], TILES // 2 + 1)
            logits(0, 0, 0, 0)
            logits(0, 1, 0, 0)
            logits(0, 2, 0, 0)
            logits(0, 3, 0, 0)
            turn_p(0, 0)
            with pe.Fori(0, 3) as i:
                pe_head(i * 2, 0, i)
                pe_head(i * 2 + 1, 1, i + 1)
            pe_head(6, 0, 3)
            pe_head(7, 1, None, last=True)

            def banks(u, q):
                return PS[2 * u + q // 2][:, (q % 2) * NT:(q % 2) * NT + OC]

            def out_chunk(cg, th, u, step=1):
                for j in range(OP):
                    pe.wait_ge(wo_lo_s, 8 * cg + step * j + 5)
                    for q in range(HALF_T):
                        if j == 0:
                            pe.wait_ge(o_add, 4 * cg + q + 1)
                        tok = slice((th * HALF_T + q) * P, (th * HALF_T + q + 1) * P)
                        for k in range(OPK):
                            kt = j * OPK + k
                            o = banks(u, q)
                            nc.tensor.matmul(o, hT_lo[:, kt, tok], wo_hi[:, j % 2, k, :], start=(kt == 0), stop=False)
                            nc.tensor.matmul(o, hT_hi[:, kt, tok], wo_lo[:, j % 2, k, :], start=False, stop=False)
                            last = nc.tensor.matmul(o, hT_hi[:, kt, tok], wo_hi[:, j % 2, k, :],
                                                    start=False, stop=(kt == KT - 1))
                        if j == OP - 1 and q < HALF_T - 1:
                            last.then_inc(o_mm, 1)
                    last.then_inc(wo_used, 1)

            pe.wait_ge(y_att, 4 * NH + 1)
            pe.wait_ge(yl_lo, 1 + 2 * G)
            with pe.Fori(0, 2) as i:
                out_chunk(i * 2, 0, 0)
                out_chunk(i * 2 + 1, 0, 1)
            out_chunk(CHUNKS - 4, 1, 0)
            out_chunk(CHUNKS - 3, 1, 1)
            out_chunk(CHUNKS - 2, 1, 0, step=2)
            for q in range(HALF_T):
                pe.wait_ge(o_add, 4 * (CHUNKS - 1) + q + 1)
                for kt in range(KT):
                    if q == 0 and kt % OPK == 0:
                        pe.wait_ge(wo_lo_s, OP * (CHUNKS - 2) + 2 * (kt // OPK) + 6)
                    tok = slice((HALF_T + q) * P, (HALF_T + q + 1) * P)
                    whi, wlo = hT_hi[:, kt, 0:OC], hT_lo[:, kt, 0:OC]
                    o = banks(1, q)
                    nc.tensor.matmul(o, hT_lo[:, kt, tok], whi, start=(kt == 0), stop=False)
                    nc.tensor.matmul(o, hT_hi[:, kt, tok], wlo, start=False, stop=False)
                    last = nc.tensor.matmul(o, hT_hi[:, kt, tok], whi, start=False, stop=(kt == KT - 1))
                last.then_inc(o_mm, 1)

        @block.vector
        def _(dve):
            nc.vector.sem_inc(h_lo, 4)
            nc.vector.sem_inc(ix_acc, 8)
            nc.vector.sem_inc(y_lru, 1)
            nc.vector.sem_inc(o_used, 4)
            nc.vector.sem_inc(yl_lo, 1)
            nc.vector.sem_inc(y_att, 1)
            nc.vector.sem_inc(o_add, 8)
            step = Tally(dve_step)
            tt, stt = nc.vector.tensor_tensor, nc.vector.scalar_tensor_tensor

            def chain(ins):
                dve.wait_ge(dve_step, step.did(ins))

            def hold():
                nc.vector.memset(pause[:, :], 0.0)

            nc.vector.memset(eps[:, :], EPS).then_inc(eps_made, 1)
            nc.vector.memset(par_rows[:, :], 0.0).then_inc(rows_clear, 1)
            dve.wait_ge(g_in, 16)

            def norm_x(i):
                dve.wait_ge(x_sd, i + 1)
                root, inverse = (stat[:, k * XB + i % XB:k * XB + i % XB + 1] for k in (1, 2))
                chain(nc.vector.reciprocal(inverse, root))
                stt(xin[:, i % XB, :], xin[:, i % XB, :], inverse, g_bc[:, :], ALU.mult, ALU.mult
                    ).then_inc(x_norm, 1)

            def low_x(i):
                for j in range(2):
                    dve.wait_ge(h_hi, 2 * i + j + 1)
                    part = (slice(None), slice(8 * j, 8 * j + 8), slice(i * P, (i + 1) * P))
                    tt(hT_lo[part], x_bank(i, j).rearrange("p (t s) -> p t s", s=P),
                       hT_hi[part].bitcast(F32), ALU.subtract).then_inc(h_lo, 1)

            norm_x(0)
            for i in range(QB):
                if i + 1 < QB:
                    norm_x(i + 1)
                low_x(i)

            dve.wait_ge(x_tp, 2 * QB)
            dve.wait_ge(bias_st, 16)
            chain(nc.vector.memset(ones_k[:, :], 1.0 / ID))
            nc.vector.memset(ones_c[:, :], 1.0 / C).then_inc(ones_made, 1)
            chain(nc.vector.memset(scores[:, :], 0.0))
            dve.wait_ge(consts, 1)
            for q in range(FIRST_SCORED, QB):
                s = step.did(nc.vector.tensor_copy(scores[:, off(q) + q * P:off(q) + (q + 1) * P], causal[:, :]))
            dve.wait_ge(dve_step, s)
            dve.wait_ge(small_cp, 1)
            lam = lru_p[:, 3, :]
            chain(nc.vector.tensor_scalar(sp_t[:, 4, :], lam, -1.0, None, ALU.mult))
            chain(nc.vector.tensor_scalar(sp_t[:, 2, :], sp_t[:, 4, :], 0.0, None, ALU.max))
            tt(sp_t[:, 0, :], sp_t[:, 4, :], lam, ALU.min).then_inc(sp_in, 1)
            dve.wait_ge(k_mean, 1)
            tt(kw_sb[0:ID, :], kw_sb[0:ID, :], X[0][0:ID, :], ALU.subtract).then_inc(k_dev, 1)
            dve.wait_ge(k_sd, 1)
            chain(nc.vector.reciprocal(k_t[:, :], k_t[:, :]))
            tt(kw_sb[0:ID, :], kw_sb[0:ID, :], k_t[:, :], ALU.mult).then_inc(k_nrm, 1)
            dve.wait_ge(w_tp, 1)
            nc.vector.tensor_scalar(w_nat[:, :, :], X[0][:, 0:QB * IH].rearrange("p (q h) -> p q h", h=IH),
                                    IH ** -0.5 * ID ** -0.5, None, ALU.mult).then_inc(w_nat_s, 1)
            dve.wait_ge(k_ln, 3)
            tt(ki_lo[0:ID, :], k_t[:, :], ki_hi[0:ID, :].bitcast(F32), ALU.subtract).then_inc(ki_done, 1)
            tt(ki_lo[ID:P, :], k_t[:, :], ki_hi[0:ID, :].bitcast(F32), ALU.subtract).then_inc(ki_done, 1)
            dve.wait_ge(sp_exp, 1)
            z, s_, q_, p_ = (sp_t[:, k, :] for k in (1, 3, 4, 0))
            chain(nc.vector.tensor_scalar(s_, z, 2.0, None, ALU.add))
            chain(nc.vector.reciprocal(s_, s_))
            chain(tt(s_, s_, z, ALU.mult))
            chain(tt(q_, s_, s_, ALU.mult))
            chain(nc.vector.tensor_scalar(p_, q_, 1.0 / 13, None, ALU.mult))
            for n in (11, 9, 7, 5, 3):
                chain(stt(p_, p_, 1.0 / n, q_, ALU.add, ALU.mult))
            chain(stt(p_, p_, 1.0, s_, ALU.add, ALU.mult))
            chain(stt(p_, p_, 2.0, sp_t[:, 2, :], ALU.mult, ALU.add))
            chain(nc.vector.tensor_scalar(decay[:, 0, :], p_, 8.0, None, ALU.mult))
            nc.vector.tensor_scalar(decay[:, 1, :], p_, -8.0, None, ALU.mult).then_inc(dec_s, 1)

            def stacks(t, par):
                dve.wait_ge(st_hi, t * 2 - 2 * (T_QI - 1))
                tt(stack_a[par][ID:P, :], PJ[par][0:ID, :], stack_a[par][0:ID, :].bitcast(F32), ALU.subtract)
                tt(stack_b[par][0:ID, :], PJ[par][ID:P, :], stack_b[par][ID:P, :].bitcast(F32), ALU.subtract
                   ).then_inc(pj_free[par], 1)

            def norm_latent(j):
                tok = slice(j * S // 4, (j + 1) * S // 4)
                if j == 0:
                    dve.wait_ge(c_sd, 1)
                chain(nc.vector.reciprocal(c_rs[:, tok], c_rs[:, tok]))
                for t in range(CT):
                    stt(c_sb[:, t, tok], c_sb[:, t, tok], c_g[:, t:t + 1], c_rs[:, tok], ALU.mult, ALU.mult
                        ).then_inc(c_done, 1)

            def add_scores(t, first=False):
                for m in range(UNITS):
                    if first and m % 2 == 1 and m < 8:
                        norm_latent(m // 2)
                    q = FIRST_SCORED + m % (UNITS // 2)
                    w = (q + 1) * P
                    k = t * UNITS + (m - UNITS * T_QI)
                    dve.wait_ge(ix_relu, k + 3)
                    dve.wait_ge(ix_acc, k + 3)
                    acc = scores[:, off(q):off(q) + w]
                    head = t * 2 + (m // (UNITS // 2) - 2 * T_QI)
                    stt(acc, relu[m % 2][:, 0:w], w_nat[:, q, ds(head, 1)], acc, ALU.mult, ALU.add
                        ).then_inc(ix_acc, 1)

            def dve_b(t, par, first=False):
                stacks(t - 1, 1 - par)
                add_scores(t - 1, first)

            dve_b(T_QI + 1, 0, first=True)
            with dve.Fori(0, 3) as i:
                dve_b(i * 2 + (T_QI + 2), 1)
                dve_b(i * 2 + (T_QI + 3), 0)
            stacks(T_QI + 7, 0)
            add_scores(T_QI + 7)
            dve.wait_ge(ix_acc, 8 + 8 * UNITS)

            def top_rounds(n):
                for _ in range(n):
                    for q in range(FIRST_SCORED, QB):
                        found = step.did(nc.vector.max(top8[:, q, :], scores[:, off(q):off(q) + (q + 1) * P]))
                    dve.wait_ge(dve_step, found)
                    hold()
                    for q in range(FIRST_SCORED, QB):
                        left = scores[:, off(q):off(q) + (q + 1) * P]
                        marked = step.did(nc.vector.match_replace(left, top8[:, q, :], left, TAKEN))
                    dve.wait_ge(dve_step, marked)
                    hold()

            per = ROUNDS // (G + NH)
            with dve.Fori(0, G) as g:
                step.enter(g, 2 + 12 * per + 4)
                dve.wait_ge(xc0, g + 1)
                xa = PJ[1]
                for n in (1, 2, 3):
                    tap = stt(xc[:, n:], xa[:, 0:S - n], conv_w[:, CONV - 1 - n, ds(g, 1)], xc[:, n:],
                              ALU.mult, ALU.add)
                    if n < 3:
                        chain(tap)
                    else:
                        tap.then_inc(pj_free[1], 1)
                dve.wait_ge(wg_hi_s, g + 1)
                tt(wg_lo[:, :, :], w_gates[:, :, :], wg_hi[:, :, :].bitcast(F32), ALU.subtract)
                dve.wait_ge(xc_hi_s, g + 1)
                tt(xc_lo[:, :], xc[:, :], xc_hi[:, :].bitcast(F32), ALU.subtract).then_inc(gates_lo_s, 1)
                top_rounds(per)
                dve.wait_ge(a_sq, g + 1)
                stt(th[:, :], rg[:, :], 1.0, th[:, :], ALU.add, ALU.mult).then_inc(one_m, 1)
                dve.wait_ge(i_sig, g + 2)
                chain(tt(ig[:, :], ig[:, :], xc[:, :], ALU.mult))
                dve.wait_ge(g_sig, g + 1)
                tt(sg[:, :], PJ[0][:, :], sg[:, :], ALU.mult).then_inc(pj_free[0], 1)
                dve.wait_ge(root, g + 1)
                chain(nc.vector.memset(th[:, 0:1], 1.0))
                chain(tt(ig[:, :], ig[:, :], th[:, :], ALU.mult))
                chain(nc.vector.tensor_tensor_scan(rg[:, :], av[:, :], ig[:, :], 0.0, ALU.mult, ALU.add))
                tt(sg[:, :], sg[:, :], rg[:, :], ALU.mult).then_inc(y_lru, 1)
                step.leave(G)
            dve.wait_ge(y_lru, G + 1)

            def finish_gate(h):
                dve.wait_ge(d_sig, h + 1)
                dve.wait_ge(gate_st, h * 16 + 16)
                tt(rg[:, :], PJ[0][:, :], ig[:, :], ALU.mult).then_inc(pj_free[0], 1)

            with dve.Fori(0, NH - 1) as h:
                step.enter(h, 12 * per)
                top_rounds(per)
                finish_gate(h)
                step.leave(NH - 1)
            top_rounds(per)
            for q in range(FIRST_SCORED, QB):
                nc.vector.tensor_scalar(mask[:, OFF[q]:OFF[q] + (q + 1) * P], scores[:, off(q):off(q) + (q + 1) * P],
                                        (NEG + TAKEN) / 2, BIG, ALU.is_gt, ALU.mult)
            nc.vector.memset(mask[:, P:2 * P], 0.0)
            nc.vector.tensor_scalar(mask[:, 0:P], causal[:, :], NEG / 2, BIG, ALU.is_lt, ALU.mult)
            nc.vector.tensor_scalar(mask[:, 2 * P:3 * P], causal[:, :], NEG / 2, BIG, ALU.is_lt, ALU.mult
                                    ).then_inc(mask_s, 1)
            dve.wait_ge(mask_s, 1)
            finish_gate(NH - 1)

            def softmin(h, q, p, turn):
                w = (q + 1) * P
                n = min(w, 2 * P)
                if q == 0:
                    dve.wait_ge(qb_ld[p], turn * 32 + 32)
                dve.wait_ge(lg_mm, 8 * h + q + 1)
                lg = LG[q]
                chain(tt(lg[:, w - n:w], lg[:, w - n:w], tb[p][:, 2 * P - n:2 * P], ALU.add))
                dve.wait_ge(p_tp, 8 * h + q + 1)
                hold()
                nc.vector.tensor_tensor_reduce(prob[q], lg[:, 0:w], mask[:, OFF[q]:OFF[q] + w],
                                               1.0, 3.0e38, ALU.add, ALU.min, sums[:, q, 0:1]
                                               ).then_inc(lg_used, 1)

            def normalise(h, q):
                dve.wait_ge(p_exp, 8 * h + q + 1)
                chain(nc.vector.reciprocal(sums[:, q, 2:3], sums[:, q, 1:2]))
                nc.vector.tensor_scalar(prob[q], prob[q], sums[:, q, 2:3], None, ALU.mult).then_inc(p_norm, 1)

            def gated(h, r):
                dve.wait_ge(ro_mm, 4 * h + r + 5)
                dve.wait_ge(gate_ld[r % 2], h * 32 + 16 * (r // 2) + 16)
                dve.wait_ge(y_att, 4 * h + r + 1)
                tt(yf[:, :], X[1][:, (r % 2) * NT:(r % 2) * NT + 2 * P], gate[:, r % 2, :], ALU.mult).then_inc(o_used, 1)

            def cut_y(h, r):
                tok = slice(2 * r * P, 2 * (r + 1) * P)
                dve.wait_ge(o_used, 4 * h + r + 5)
                y3 = yf[:, :].rearrange("p (o s) -> p o s", o=1)
                chain(nc.vector.tensor_copy(hT_hi[:, ds(h + G, 1), tok], y3))
                tt(hT_lo[:, ds(h + G, 1), tok], y3, hT_hi[:, ds(h + G, 1), tok].bitcast(F32), ALU.subtract
                   ).then_inc(y_att, 1)

            def low_y(h, k):
                dve.wait_ge(yl_hi, 2 * h + k + 1)
                piece = (slice(None), ds(h, 1), slice(k * NT, (k + 1) * NT))
                tt(hT_lo[piece], yl_raw[:, :].rearrange("p (o s) -> p o s", o=1),
                   hT_hi[piece].bitcast(F32), ALU.subtract).then_inc(yl_lo, 1)

            def dve_head(h, p, turn, last=False):
                for q in range(QB):
                    if q < QB - AHEAD:
                        normalise(h, q + 2)
                    if q in (4, 5, 7):
                        gated(h, {4: 0, 5: 1, 7: 2}[q])
                    if q < QB - AHEAD:
                        softmin(h, q + AHEAD, p, None)
                    elif q == 6 and not last:
                        softmin(h + 1, 0, 1 - p, turn)
                        softmin(h + 1, 1, 1 - p, turn)
                    elif q == 7 and not last:
                        softmin(h + 1, 2, 1 - p, turn)
                    if q == 5:
                        normalise(h, 7)
                    elif q > 5 and not last:
                        normalise(h + 1, q - 6)
                    if q in (4, 5, 7):
                        cut_y(h, {4: 0, 5: 1, 7: 2}[q])
                    if q in (2, 5):
                        low_y(h, q // 5)
                gated(h, 3)
                cut_y(h, 3)

            softmin(0, 0, 0, 0)
            softmin(0, 1, 0, 0)
            softmin(0, 2, 0, 0)
            normalise(0, 0)
            normalise(0, 1)
            links = 8 + 8 + 4
            with dve.Fori(0, 3) as i:
                step.enter(i, 2 * links)
                dve_head(i * 2, 0, i)
                dve_head(i * 2 + 1, 1, i + 1)
                step.leave(3)
            dve_head(6, 0, 3)
            dve_head(7, 1, None, last=True)
            dve.wait_ge(y_att, 4 * NH + 1)

            def add_residual(cg, c, u, half=None):
                for q in range(HALF_T):
                    if q < HALF_T - 1 or half == 1:
                        dve.wait_ge(o_mm, cg * (HALF_T - 1) + q + 1)
                    else:
                        dve.wait_ge(wo_used, cg * OP + OP + 2)
                    r = res[q][:, ds(c * OC, OC)]
                    tt(r, PS[2 * u + q // 2][:, (q % 2) * NT:(q % 2) * NT + OC], r, ALU.add).then_inc(o_add, 1)
                    if half == 1:
                        final_norm(cg, q, 1)
                if half == 0:
                    final_norm(cg, 0, HALF_T)

            def final_norm(cg, q, n):
                dve.wait_ge(o_sq, 4 * cg + q + n + 1)
                nc.vector.reduce_sum(fstat[:, 0, q:q + n], ssq[:, q:q + n, :], AX.X).then_inc(f_tot, 1)
                dve.wait_ge(f_sd, 1 if n > 1 else q + 2)
                chain(nc.vector.reciprocal(fstat[:, 2, q:q + n], fstat[:, 1, q:q + n]))
                for k in range(q, q + n):
                    for part in (slice(0, D // 2), slice(D // 2, D)):
                        stt(res[k][:, part], res[k][:, part], fstat[:, 2, k:k + 1], gf_bc[:, part],
                            ALU.mult, ALU.mult).then_inc(f_out, 1)

            dve.wait_ge(gf_in, 16)
            for half in range(2):
                dve.wait_ge(res_in, 64 * (half + 1))
                with dve.Fori(0, OCH // 2 - 1) as i:
                    for u in range(2):
                        add_residual(i * 2 + (OCH * half + u), i * 2 + u, u)
                add_residual(OCH * half + OCH - 2, OCH - 2, 0)
                add_residual(OCH * half + OCH - 1, OCH - 1, 1, half)


def distance_buckets():
    import numpy as np
    dist = np.maximum(2 * P - 1 - np.arange(BR), 0)
    exact = BUCKETS // 2
    far = exact + (np.log(np.maximum(dist, 1) / exact) / math.log(MAX_DIST / exact)
                   * (BUCKETS - exact)).astype(np.int64)
    bucket = np.where(dist < exact, dist, np.minimum(far, BUCKETS - 1))
    hot = (np.arange(BUCKETS)[:, None] == bucket[None, :]).astype(np.float32)
    hot[BUCKETS - 1] -= 1.0
    return np.ascontiguousarray(-hot)


_INS = ["x", "norm_g", "w_in", "conv_w", "conv_b", "lru_wa", "lru_ba", "lru_wx", "lru_bx", "lru_lambda",
        "ckv_norm_g", "idx_k_norm_g", "idx_k_norm_b", "w_uk", "w_uv", "w_out", "rel_bias", "final_norm_g"]


def kernel(**inputs):
    import numpy as np
    import concourse.bacc as bacc
    from concourse.bass_utils import run_bass_kernel_spmd

    nc = bacc.Bacc("TRN2", target_bir_lowering=False, num_devices=1)
    arrays, aps = {}, {}
    values = {name: np.ascontiguousarray(inputs[name]) for name in _INS}
    values["onehot"] = distance_buckets()
    for name, v in values.items():
        arrays[f"in_{name}"] = v
        aps[name] = nc.dram_tensor(f"in_{name}", v.shape, mybir.dt.from_np(v.dtype), kind="ExternalInput").ap()
    out = nc.dram_tensor("out_0", (1, S, D), F32, kind="ExternalOutput").ap()
    layer(nc, aps, out)
    r = run_bass_kernel_spmd(nc, [arrays], core_ids=[0])
    return r.results[0]["out_0"]
```
